# Optimizing a Trainium2 kernel written in Bass

```python
import jax, jax.numpy as jnp
from jax import lax
import numpy as np
import math

D_MODEL = 1024
BATCH = 1
SEQ = 512
DEPTH = 1

GRID_W = 64
CTX_LEN = 256
D_MIX = D_MODEL
RET_HEADS = 4
RET_WIDTH = D_MIX // 2
RET_DK = RET_WIDTH // RET_HEADS
RET_DV = RET_WIDTH // RET_HEADS
GLA_HEADS = 4
GLA_WIDTH = D_MIX - RET_WIDTH
GLA_DV = GLA_WIDTH // GLA_HEADS
GLA_DK = GLA_DV // 2
GLA_RANK = 16
GLA_GATE_NORM = 16.0
CHUNK = 64
ROPE_BASE = 10000.0
N_KEYS = 128
N_EXPERTS = N_KEYS * N_KEYS
PEER_HEADS = 8
PEER_TOPK = 16
PEER_DQ = 256
PEER_BLOCK = 128
N_MOD = 6
EPS = 1e-6
IN_SIZES = (RET_WIDTH, RET_WIDTH, RET_WIDTH, RET_WIDTH,
            GLA_HEADS * GLA_DK, GLA_HEADS * GLA_DK, GLA_WIDTH, GLA_WIDTH,
            GLA_RANK, GLA_RANK)
IN_COLS = sum(IN_SIZES)


F32 = jnp.float32

def rmsnorm(x, w):
    xf = x.astype(F32)
    y = xf * lax.rsqrt(jnp.mean(xf * xf, axis=-1, keepdims=True) + EPS)
    return (y * w.astype(F32)).astype(x.dtype)

def head_rmsnorm(o):
    o = o * lax.rsqrt(jnp.mean(o * o, axis=-1, keepdims=True) + EPS)
    B, H, L, d = o.shape
    return o.transpose(0, 2, 1, 3).reshape(B, L, H * d)

def modulate(h, shift, scale):
    return h * (1 + scale) + shift

def to_heads(t, n_heads):
    B, L, W = t.shape
    return t.reshape(B, L, n_heads, W // n_heads).transpose(0, 2, 1, 3)

def flip_seq(t):
    return jnp.flip(t, axis=2)

def axial_rope(rows, cols):
    r, c = jnp.meshgrid(jnp.arange(rows, dtype=F32), jnp.arange(cols, dtype=F32), indexing="ij")
    n_freq = RET_DK // 4
    inv = ROPE_BASE ** (-jnp.arange(n_freq, dtype=F32) / n_freq)
    ang = jnp.concatenate([r.reshape(-1, 1) * inv, c.reshape(-1, 1) * inv], axis=-1)
    return jnp.cos(ang), jnp.sin(ang)

def apply_rope(t, cos, sin):
    t1, t2 = jnp.split(t, 2, axis=-1)
    return jnp.concatenate([t1 * cos - t2 * sin, t2 * cos + t1 * sin], axis=-1)

def to_chunks(t):
    B, H, L, d = t.shape
    return t.reshape(B, H, L // CHUNK, CHUNK, d).transpose(2, 0, 1, 3, 4)

def from_chunks(t):
    n, B, H, C, d = t.shape
    return t.transpose(1, 2, 0, 3, 4).reshape(B, H, n * C, d)

def retention_scan(q, k, v, log_gamma, s0):
    idx = jnp.arange(CHUNK, dtype=F32)
    rel = idx[:, None] - idx[None, :]
    lg = log_gamma[:, None, None]
    decay_mask = jnp.where(rel >= 0, jnp.exp(lg * jnp.maximum(rel, 0.0)), 0.0)
    q_dec = jnp.exp(log_gamma[:, None] * (idx + 1.0))[None, :, :, None]
    k_dec = jnp.exp(log_gamma[:, None] * (CHUNK - 1.0 - idx))[None, :, :, None]
    chunk_dec = jnp.exp(log_gamma * CHUNK)[None, :, None, None]

    def step(s, inp):
        qc, kc, vc = inp
        scores = jnp.einsum("bhid,bhjd->bhij", qc, kc) * decay_mask
        out = (jnp.einsum("bhij,bhjv->bhiv", scores, vc)
               + jnp.einsum("bhid,bhdv->bhiv", qc * q_dec, s))
        s = chunk_dec * s + jnp.einsum("bhjd,bhjv->bhdv", kc * k_dec, vc)
        return s, out

    s, out = lax.scan(step, s0, (to_chunks(q), to_chunks(k), to_chunks(v)))
    return from_chunks(out), s

def gla_scan(q, k, v, log_a, s0):
    causal = (jnp.arange(CHUNK)[:, None] >= jnp.arange(CHUNK)[None, :])

    def step(s, inp):
        qc, kc, vc, ac = inp
        G = jnp.cumsum(ac, axis=2)
        G_last = G[:, :, -1:, :]
        q_t = qc * jnp.exp(G)
        k_t = kc * jnp.exp(-G)
        scores = jnp.where(causal, jnp.einsum("bhid,bhjd->bhij", q_t, k_t), 0.0)
        out = (jnp.einsum("bhij,bhjv->bhiv", scores, vc)
               + jnp.einsum("bhid,bhdv->bhiv", q_t, s))
        s = (jnp.exp(G_last[:, :, 0, :])[..., None] * s
             + jnp.einsum("bhjd,bhjv->bhdv", kc * jnp.exp(G_last - G), vc))
        return s, out

    s, out = lax.scan(step, s0, (to_chunks(q), to_chunks(k), to_chunks(v), to_chunks(log_a)))
    return from_chunks(out), s

def retention_final_state(k, v, log_gamma):
    L = k.shape[2]
    w = jnp.exp(log_gamma[:, None] * (L - 1.0 - jnp.arange(L, dtype=F32)))
    return jnp.einsum("bhld,bhle->bhde", k * w[None, :, :, None], v)

def gla_final_state(k, v, log_a):
    G = jnp.cumsum(log_a, axis=2)
    return jnp.einsum("bhld,bhle->bhde", k * jnp.exp(G[:, :, -1:, :] - G), v)

def project(h, w_in, gk_up_f, gk_bias_f, gk_up_b, gk_bias_b, rope):
    p = (h @ w_in).astype(F32)
    splits = [int(s) for s in np.cumsum(IN_SIZES)[:-1]]
    rq, rk, rv, rg, gq, gk, gv, gg, lr_f, lr_b = jnp.split(p, splits, axis=-1)
    rq = to_heads(rq, RET_HEADS)
    rk = to_heads(rk, RET_HEADS) * (RET_DK ** -0.5)
    rv = to_heads(rv, RET_HEADS)
    if rope is not None:
        rq = apply_rope(rq, *rope)
        rk = apply_rope(rk, *rope)
    gq = to_heads(gq, GLA_HEADS) * (GLA_DK ** -0.5)
    gk = to_heads(gk, GLA_HEADS)
    gv = to_heads(gv, GLA_HEADS)
    la_f = to_heads(jax.nn.log_sigmoid(lr_f @ gk_up_f.astype(F32) + gk_bias_f.astype(F32)) / GLA_GATE_NORM, GLA_HEADS)
    la_b = to_heads(jax.nn.log_sigmoid(lr_b @ gk_up_b.astype(F32) + gk_bias_b.astype(F32)) / GLA_GATE_NORM, GLA_HEADS)
    return (rq, rk, rv, rg, gq, gk, gv, gg, la_f, la_b)

def bidir_mix(feats, lg_f, lg_b, states):
    rq, rk, rv, rg, gq, gk, gv, gg, la_f, la_b = feats
    s_rf, s_rb, s_gf, s_gb = states
    o_rf, s_rf = retention_scan(rq, rk, rv, lg_f, s_rf)
    o_rb, s_rb = retention_scan(flip_seq(rq), flip_seq(rk), flip_seq(rv), lg_b, s_rb)
    o_gf, s_gf = gla_scan(gq, gk, gv, la_f, s_gf)
    o_gb, s_gb = gla_scan(flip_seq(gq), flip_seq(gk), flip_seq(gv), flip_seq(la_b), s_gb)
    ret = head_rmsnorm(o_rf + flip_seq(o_rb)) * jax.nn.silu(rg)
    gla = head_rmsnorm(o_gf + flip_seq(o_gb)) * jax.nn.silu(gg)
    return jnp.concatenate([ret, gla], axis=-1), (s_rf, s_rb, s_gf, s_gb)

def context_final_states(feats, lg_f, lg_b):
    _, rk, rv, _, _, gk, gv, _, la_f, la_b = feats
    return (retention_final_state(rk, rv, lg_f),
            retention_final_state(flip_seq(rk), flip_seq(rv), lg_b),
            gla_final_state(gk, gv, la_f),
            gla_final_state(flip_seq(gk), flip_seq(gv), flip_seq(la_b)))

def zero_states(b):
    return (jnp.zeros((b, RET_HEADS, RET_DK, RET_DV), F32),
            jnp.zeros((b, RET_HEADS, RET_DK, RET_DV), F32),
            jnp.zeros((b, GLA_HEADS, GLA_DK, GLA_DV), F32),
            jnp.zeros((b, GLA_HEADS, GLA_DK, GLA_DV), F32))

def peer_ffn(h, w_q, k1, k2, down, up):
    B, L, D = h.shape
    half = PEER_DQ // 2
    blocks = h.reshape(-1, PEER_BLOCK, D)

    def block(xb):
        q = (xb @ w_q).astype(F32).reshape(PEER_BLOCK, PEER_HEADS, 2, half)
        s1 = jnp.einsum("thd,hnd->thn", q[:, :, 0], k1.astype(F32))
        s2 = jnp.einsum("thd,hnd->thn", q[:, :, 1], k2.astype(F32))
        v1, i1 = lax.top_k(s1, PEER_TOPK)
        v2, i2 = lax.top_k(s2, PEER_TOPK)
        cand_s = (v1[..., :, None] + v2[..., None, :]).reshape(PEER_BLOCK, PEER_HEADS, PEER_TOPK * PEER_TOPK)
        cand_i = (i1[..., :, None] * N_KEYS + i2[..., None, :]).reshape(PEER_BLOCK, PEER_HEADS, PEER_TOPK * PEER_TOPK)
        top_s, pos = lax.top_k(cand_s, PEER_TOPK)
        idx = jnp.take_along_axis(cand_i, pos, axis=-1)
        g = jax.nn.softmax(top_s, axis=-1)
        u = down[idx]
        act = jax.nn.gelu(jnp.einsum("thkd,td->thk", u, xb).astype(F32), approximate=False)
        return jnp.einsum("thk,thkd->td", (g * act).astype(xb.dtype), up[idx])

    return lax.map(block, blocks).reshape(B, L, D)

def trunk_layer(x, xc, c, c_ctx, w_mod, b_mod, norm1_w, norm2_w, w_in,
                ret_decay_f, ret_decay_b, gk_up_f, gk_bias_f, gk_up_b, gk_bias_b,
                w_out, peer_w_q, peer_k1, peer_k2, peer_down, peer_up, rope, update_ctx):
    mod = (jax.nn.silu(c) @ w_mod + b_mod)[:, None, :]
    mod_c = (jax.nn.silu(c_ctx) @ w_mod + b_mod)[None, None, :]
    sh1, sc1, g1, sh2, sc2, g2 = jnp.split(mod, N_MOD, axis=-1)
    csh1, csc1, cg1, csh2, csc2, cg2 = jnp.split(mod_c, N_MOD, axis=-1)
    lg_f = jax.nn.log_sigmoid(ret_decay_f.astype(F32))
    lg_b = jax.nn.log_sigmoid(ret_decay_b.astype(F32))

    feats_c = project(modulate(rmsnorm(xc, norm1_w), csh1, csc1),
                      w_in, gk_up_f, gk_bias_f, gk_up_b, gk_bias_b, None)
    if update_ctx:
        yc, ctx_states = bidir_mix(feats_c, lg_f, lg_b, zero_states(xc.shape[0]))
    else:
        ctx_states = context_final_states(feats_c, lg_f, lg_b)

    feats = project(modulate(rmsnorm(x, norm1_w), sh1, sc1),
                    w_in, gk_up_f, gk_bias_f, gk_up_b, gk_bias_b, rope)
    y, _ = bidir_mix(feats, lg_f, lg_b, ctx_states)
    x = x + g1 * (y.astype(x.dtype) @ w_out)
    x = x + g2 * peer_ffn(modulate(rmsnorm(x, norm2_w), sh2, sc2),
                          peer_w_q, peer_k1, peer_k2, peer_down, peer_up)
    if update_ctx:
        xc = xc + cg1 * (yc.astype(xc.dtype) @ w_out)
        xc = xc + cg2 * peer_ffn(modulate(rmsnorm(xc, norm2_w), csh2, csc2),
                                 peer_w_q, peer_k1, peer_k2, peer_down, peer_up)
    return x, xc

def first_inputs(seed: int = 0) -> dict:
    key = jax.random.key(seed)
    ks = jax.random.split(key, 24)

    def nrm(k, shape, s):
        return jax.random.normal(k, shape, F32) * s

    base_logit = jnp.asarray(np.log(2.0 ** (5 + np.arange(RET_HEADS)) - 1.0), F32)[None, :]
    return {
        "x": nrm(ks[0], (BATCH, SEQ, D_MODEL), 1.0),
        "c": nrm(ks[1], (BATCH, D_MODEL), 1.0),
        "ctx": nrm(ks[2], (BATCH, CTX_LEN, D_MODEL), 1.0),
        "c_ctx": nrm(ks[3], (D_MODEL,), 1.0),
        "w_mod": nrm(ks[4], (DEPTH, D_MODEL, N_MOD * D_MODEL), 0.5 * D_MODEL ** -0.5),
        "b_mod": nrm(ks[5], (DEPTH, N_MOD * D_MODEL), 0.02),
        "norm1_w": 1.0 + nrm(ks[6], (DEPTH, D_MODEL), 0.02),
        "norm2_w": 1.0 + nrm(ks[7], (DEPTH, D_MODEL), 0.02),
        "w_in": nrm(ks[8], (DEPTH, D_MODEL, IN_COLS), D_MODEL ** -0.5),
        "ret_decay_f": base_logit + nrm(ks[9], (DEPTH, RET_HEADS), 0.05),
        "ret_decay_b": base_logit + nrm(ks[10], (DEPTH, RET_HEADS), 0.05),
        "gla_gk_up_f": nrm(ks[11], (DEPTH, GLA_RANK, GLA_HEADS * GLA_DK), GLA_RANK ** -0.5),
        "gla_gk_bias_f": nrm(ks[12], (DEPTH, GLA_HEADS * GLA_DK), 0.1),
        "gla_gk_up_b": nrm(ks[13], (DEPTH, GLA_RANK, GLA_HEADS * GLA_DK), GLA_RANK ** -0.5),
        "gla_gk_bias_b": nrm(ks[14], (DEPTH, GLA_HEADS * GLA_DK), 0.1),
        "w_out": nrm(ks[15], (DEPTH, D_MIX, D_MODEL), D_MIX ** -0.5),
        "peer_w_q": nrm(ks[16], (DEPTH, D_MODEL, PEER_HEADS * PEER_DQ), D_MODEL ** -0.5),
        "peer_k1": nrm(ks[17], (DEPTH, PEER_HEADS, N_KEYS, PEER_DQ // 2), (PEER_DQ // 2) ** -0.5),
        "peer_k2": nrm(ks[18], (DEPTH, PEER_HEADS, N_KEYS, PEER_DQ // 2), (PEER_DQ // 2) ** -0.5),
        "peer_down": nrm(ks[19], (DEPTH, N_EXPERTS, D_MODEL), D_MODEL ** -0.5),
        "peer_up": nrm(ks[20], (DEPTH, N_EXPERTS, D_MODEL), 0.5),
        "norm_f_w": 1.0 + nrm(ks[21], (D_MODEL,), 0.02),
    }

def first_block(x, c, ctx, c_ctx, w_mod, b_mod, norm1_w, norm2_w, w_in,
              ret_decay_f, ret_decay_b, gla_gk_up_f, gla_gk_bias_f, gla_gk_up_b, gla_gk_bias_b,
              w_out, peer_w_q, peer_k1, peer_k2, peer_down, peer_up, norm_f_w):
    L = x.shape[1]
    ROWS = L // GRID_W
    rope = axial_rope(ROWS, GRID_W)
    xc = ctx
    for li in range(DEPTH):
        x, xc = trunk_layer(x, xc, c, c_ctx, w_mod[li], b_mod[li], norm1_w[li], norm2_w[li], w_in[li],
                            ret_decay_f[li], ret_decay_b[li], gla_gk_up_f[li], gla_gk_bias_f[li],
                            gla_gk_up_b[li], gla_gk_bias_b[li], w_out[li], peer_w_q[li],
                            peer_k1[li], peer_k2[li], peer_down[li], peer_up[li], rope,
                            li < DEPTH - 1)
    return rmsnorm(x, norm_f_w)


PLE_DIM = 256
D_MIX_2 = D_MODEL
CONV_WIDTH = D_MIX_2 // 2
CONV_HEADS = 8
POOL_WIDTH = D_MIX_2 - CONV_WIDTH
POOL_WINDOWS = (2, 4, 8, 16)
POOL_GROUP = POOL_WIDTH // len(POOL_WINDOWS)
IN_PROJ_WIDTH = 3 * CONV_WIDTH + POOL_WIDTH
CONV_K = 3
PEER_QDIM = 256
PEER_HALF = PEER_QDIM // 2
N_EXPERTS_2 = N_KEYS * N_KEYS
TOKEN_BLOCK = 128


def rms_norm(x, g):
    xf = x.astype(jnp.float32)
    y = xf * lax.rsqrt(jnp.mean(xf * xf, axis=-1, keepdims=True) + EPS)
    return (y * g.astype(jnp.float32)).astype(x.dtype)

def short_conv_mixer(b_gate, c_gate, v, conv_w):
    z = c_gate * v
    zp = jnp.pad(z, ((0, 0), (1, 1), (0, 0)))
    y = conv_w[0] * zp[:, :-2] + conv_w[1] * zp[:, 1:-1] + conv_w[2] * zp[:, 2:]
    return b_gate * y

def pool_mixer(u, pool_w, pool_scale):
    bsz, seq, _ = u.shape
    ug = u.astype(jnp.float32).reshape(bsz, seq, len(POOL_WINDOWS), POOL_GROUP)
    t = jnp.arange(seq)
    outs = []
    for g, w in enumerate(POOL_WINDOWS):
        xg = ug[:, :, g]
        cs = jnp.concatenate([jnp.zeros((bsz, 1, POOL_GROUP), jnp.float32),
                              jnp.cumsum(xg, axis=1)], axis=1)
        lo = jnp.clip(t - w // 2, 0, seq)
        hi = jnp.clip(t + w // 2, 0, seq)
        win_sum = jnp.take(cs, hi, axis=1) - jnp.take(cs, lo, axis=1)
        cnt = (hi - lo).astype(jnp.float32)[None, :, None]
        outs.append(win_sum / cnt - xg)
    pooled = jnp.stack(outs, axis=2).astype(u.dtype)
    y = jnp.einsum('bsgc,gcd->bsgd', pooled, pool_w)
    return y.reshape(bsz, seq, POOL_WIDTH) * pool_scale

def peer_block(xb, w_q, sub_keys, expert_u, expert_v):
    T = xb.shape[0]
    q = (xb @ w_q).reshape(T, PEER_HEADS, 2, PEER_HALF)
    s = jnp.einsum('thpd,hpkd->thpk', q, sub_keys)
    sv, si = lax.top_k(s, PEER_TOPK)
    cand = (sv[:, :, 0, :, None] + sv[:, :, 1, None, :]).reshape(T, PEER_HEADS, PEER_TOPK * PEER_TOPK)
    cidx = (si[:, :, 0, :, None] * N_KEYS + si[:, :, 1, None, :]).reshape(T, PEER_HEADS, PEER_TOPK * PEER_TOPK)
    top_s, pos = lax.top_k(cand, PEER_TOPK)
    eidx = jnp.take_along_axis(cidx, pos, axis=-1)
    gate = jax.nn.softmax(top_s.astype(jnp.float32), axis=-1).astype(xb.dtype)
    u = jnp.take(expert_u, eidx, axis=0)
    act = jax.nn.gelu(jnp.einsum('thkd,td->thk', u, xb))
    v = jnp.take(expert_v, eidx, axis=0)
    return jnp.einsum('thk,thkd->td', gate * act, v)

def peer_ffn_2(xn, w_q, sub_keys, expert_u, expert_v):
    bsz, seq, d = xn.shape
    blocks = xn.reshape(-1, TOKEN_BLOCK, d)
    out = lax.map(lambda xb: peer_block(xb, w_q, sub_keys, expert_u, expert_v), blocks)
    return out.reshape(bsz, seq, d)

def second_inputs(seed: int = 0) -> dict:
    key = jax.random.key(seed)
    ks = jax.random.split(key, 20)
    f32 = jnp.float32
    def nrm(k, shape, scale):
        return jax.random.normal(k, shape, f32) * scale
    def gain(k, shape):
        return 1.0 + 0.05 * jax.random.normal(k, shape, f32)
    return {
        "x": nrm(ks[0], (BATCH, SEQ, D_MODEL), 1.0),
        "p": nrm(ks[1], (DEPTH, BATCH, SEQ, PLE_DIM), 1.0),
        "g_mix": gain(ks[2], (DEPTH, D_MODEL)),
        "w_in": nrm(ks[3], (DEPTH, D_MODEL, IN_PROJ_WIDTH), D_MODEL ** -0.5),
        "conv_w": nrm(ks[4], (DEPTH, CONV_K, CONV_WIDTH), CONV_K ** -0.5),
        "pool_w": nrm(ks[5], (DEPTH, len(POOL_WINDOWS), POOL_GROUP, POOL_GROUP), POOL_GROUP ** -0.5),
        "pool_scale": gain(ks[6], (DEPTH, POOL_WIDTH)),
        "w_o": nrm(ks[7], (DEPTH, D_MIX_2, D_MODEL), D_MIX_2 ** -0.5),
        "g_ffn": gain(ks[8], (DEPTH, D_MODEL)),
        "w_q": nrm(ks[9], (DEPTH, D_MODEL, PEER_HEADS * PEER_QDIM), D_MODEL ** -0.5),
        "sub_keys": nrm(ks[10], (DEPTH, PEER_HEADS, 2, N_KEYS, PEER_HALF), PEER_HALF ** -0.5),
        "expert_u": nrm(ks[11], (DEPTH, N_EXPERTS_2, D_MODEL), D_MODEL ** -0.5),
        "expert_v": nrm(ks[12], (DEPTH, N_EXPERTS_2, D_MODEL), PEER_HEADS ** -0.5),
        "g_ple": gain(ks[13], (DEPTH, D_MODEL)),
        "w_ple_gate": nrm(ks[14], (DEPTH, D_MODEL, D_MODEL), D_MODEL ** -0.5),
        "w_ple_proj": nrm(ks[15], (DEPTH, PLE_DIM, D_MODEL), PLE_DIM ** -0.5),
        "g_final": gain(ks[16], (D_MODEL,)),
    }

def second_block(x, p, g_mix, w_in, conv_w, pool_w, pool_scale, w_o, g_ffn, w_q, sub_keys,
              expert_u, expert_v, g_ple, w_ple_gate, w_ple_proj, g_final):
    h = x
    for i in range(DEPTH):
        xn = rms_norm(h, g_mix[i])
        proj = xn @ w_in[i]
        b_gate = proj[..., :CONV_WIDTH]
        c_gate = proj[..., CONV_WIDTH:2 * CONV_WIDTH]
        v_conv = proj[..., 2 * CONV_WIDTH:3 * CONV_WIDTH]
        u_pool = proj[..., 3 * CONV_WIDTH:]
        y_conv = short_conv_mixer(b_gate, c_gate, v_conv, conv_w[i])
        y_pool = pool_mixer(u_pool, pool_w[i], pool_scale[i])
        h = h + jnp.concatenate([y_conv, y_pool], axis=-1) @ w_o[i]
        h = h + peer_ffn_2(rms_norm(h, g_ffn[i]), w_q[i], sub_keys[i], expert_u[i], expert_v[i])
        gate = jax.nn.sigmoid(rms_norm(h, g_ple[i]) @ w_ple_gate[i])
        h = h + gate * (p[i] @ w_ple_proj[i])
    return rms_norm(h, g_final)


def setup_inputs(seed=0):
    out = dict(first_inputs(seed))
    for name, value in second_inputs(seed + 1).items():
        if name != "x":
            out[name + "_2"] = value
    return out


def reference(
    x, c, ctx, c_ctx, w_mod, b_mod, norm1_w, norm2_w, w_in, ret_decay_f, ret_decay_b,
    gla_gk_up_f, gla_gk_bias_f, gla_gk_up_b, gla_gk_bias_b, w_out, peer_w_q, peer_k1, peer_k2,
    peer_down, peer_up, norm_f_w, p_2, g_mix_2, w_in_2, conv_w_2, pool_w_2, pool_scale_2, w_o_2,
    g_ffn_2, w_q_2, sub_keys_2, expert_u_2, expert_v_2, g_ple_2, w_ple_gate_2, w_ple_proj_2,
    g_final_2,
):
    x = first_block(
        x, c, ctx, c_ctx, w_mod, b_mod, norm1_w, norm2_w, w_in, ret_decay_f, ret_decay_b,
        gla_gk_up_f, gla_gk_bias_f, gla_gk_up_b, gla_gk_bias_b, w_out, peer_w_q, peer_k1,
        peer_k2, peer_down, peer_up, norm_f_w,
    )
    return second_block(
        x, p_2, g_mix_2, w_in_2, conv_w_2, pool_w_2, pool_scale_2, w_o_2, g_ffn_2, w_q_2,
        sub_keys_2, expert_u_2, expert_v_2, g_ple_2, w_ple_gate_2, w_ple_proj_2, g_final_2,
    )


_drawn_inputs = setup_inputs


def setup_inputs(seed=0):
    import zlib

    import numpy as np

    out = dict(_drawn_inputs(seed))
    spreads = {}
    factors = {'norm1_w': 2.829,
     'gla_gk_bias_f': 3.721,
     'gla_gk_bias_b': 3.542,
     'g_ple_2': 7.811,
     'norm2_w': 2.708}
    for name, (base, spread) in spreads.items():
        noise = np.random.default_rng([zlib.crc32(name.encode()), seed]).standard_normal(out[name].shape)
        drawn = base * np.exp(spread * noise) if base else spread * noise
        out[name] = __import__('jax').numpy.asarray(drawn.astype(out[name].dtype))
    for name, factor in factors.items():
        out[name] = (out[name] * factor).astype(out[name].dtype)
    return out
```

```python
import numpy as np
from contextlib import ExitStack

import concourse.bass as bass
from concourse import mybir

P = 128
F32 = mybir.dt.float32
U32 = mybir.dt.uint32
ALU = mybir.AluOpType
ACT = mybir.ActivationFunctionType
AX_X = mybir.AxisListType.X

D = 1024
KT = D // P
L = 512
TT = L // P
LC = 256
TC = LC // P
HEADS = 4
DV = 128
RET_DK = 128
GLA_DK = 64
PAIRS = 2
RANK = 16
GATE_NORM = 16.0
EPS = 1e-6
GRID_W = 64
CW = 512
RING = 3
FWD, BWD = 0, 1
PH = 8
TOPK = 16
NKEYS = 128
PQ = PH * 2 * P
SLOTS = 8
IDX_SLOTS = 4
V_CREDIT = 64
WINDOWS = (2, 4, 8, 16)
PAD = 8
LOWEST = -3.0e38

WIDE = 384 + L + 256
C_IDENT, C_COS, C_SIN = 0, 128, 640
C_AHEAD, C_BEHIND = 1152, 1152 + WIDE
C_TRI = C_BEHIND + 384 + L
TRI_PREFIX, TRI_SUFFIX, TRI_AFTER, TRI_BEFORE, TRI_ONES = range(5)
C_ROT = C_TRI + 5 * 128
C_TWICE = C_ROT + 128
C_IOTA = C_TWICE + 128
N_CONST = C_IOTA + 16

VEC = [("c", 8), ("c_ctx", 8), ("b_mod", 48), ("norm1_w", 8), ("norm2_w", 8), ("g_mix_2", 8),
       ("g_ffn_2", 8), ("g_ple_2", 8), ("conv_w_2", 12), ("pool_scale_2", 4)]
VEC_AT = {}
for _name, _rows in VEC:
    VEC_AT[_name] = sum(r for n, r in VEC[:len(VEC_AT)])
N_VEC = sum(r for _, r in VEC)

W_RQ, W_RK, W_RV, W_RG, W_GQK, W_GV, W_GG, W_LR = 0, 512, 1024, 1536, 2048, 2560, 3072, 3584

CHUNKS = ([("w_mod", CW * i) for i in range(4)]
          + [("w_in", W_RK), ("w_in", W_RV), ("w_in", W_RQ), ("w_in", W_GQK), ("w_in", W_GV),
             ("w_in", W_RG), ("w_in", W_GG)]
          + [("w_mod", CW * 4), ("w_mod", CW * 5), ("w_out", 0), ("w_out", CW)]
          + [("w_mod", CW * i) for i in range(6, 12)] + [("keys", 0)]
          + [("w_in_2", CW * i) for i in range(4)] + [("w_o_2", 0), ("w_o_2", CW), ("keys_2", 0)]
          + [("w_ple_gate_2", 0), ("w_ple_gate_2", CW), ("w_ple_proj_2", 0)])


CHUNK_LAST_JOB = {("w_in", W_RK): ("rkc", 1), ("w_in", W_RV): ("rvc", TC - 1), ("w_in", W_RQ): ("rq", HEADS - 1),
                  ("w_in", W_GQK): ("gkc",), ("w_in", W_GV): ("gvc", TC - 1), ("w_in", W_RG): ("rg", TT - 1),
                  ("w_in", W_GG): ("gg", TT - 1), ("keys", 0): ("kT", 0, 3), ("keys_2", 0): ("kT", 1, 3),
                  ("w_in_2", CW * 3): ("pu", 3), ("w_ple_gate_2", 0): ("pp", TT - 1, 0)}
CHUNK_LAST_JOB.update({("w_mod", CW * i): ("mod", i) for i in range(4)})
CHUNK_LAST_JOB.update({("w_mod", CW * (6 + i)): ("mod2", i) for i in range(4)})
for _n in range(2):
    CHUNK_LAST_JOB.update({("w_mod", CW * (4 + _n)): ("g1", _n), ("w_mod", CW * (10 + _n)): ("g2", _n),
                           ("w_out", CW * _n): ("wo", TT - 1, _n), ("w_o_2", CW * _n): ("wo2", TT - 1, _n)})
CHUNK_LAST_JOB.update({("w_in_2", CW * i): ("cb", 3) for i in range(3)})


def chunk_number(name, col=0):
    return CHUNKS.index((name, col))


def shape_constants():
    p = np.arange(P)[:, None].astype(np.float64)
    c = np.zeros((P, N_CONST), np.float32)
    c[:, C_IDENT:C_IDENT + P] = np.eye(P)
    n_freq = RET_DK // 4
    inv = np.float32(10000.0) ** (-np.arange(n_freq, dtype=np.float32) / np.float32(n_freq))
    t = np.arange(L)
    ang = np.concatenate([(t // GRID_W).astype(np.float32)[:, None] * inv,
                          (t % GRID_W).astype(np.float32)[:, None] * inv], axis=1).astype(np.float64)
    cos, sin = np.cos(ang).T, np.sin(ang).T
    c[:, C_COS:C_COS + L] = np.concatenate([cos, cos])
    c[:, C_SIN:C_SIN + L] = np.concatenate([-sin, sin])
    m = np.arange(WIDE)[None, :]
    c[:, C_AHEAD:C_AHEAD + WIDE] = np.maximum(m - 384 - p, 0)
    c[:, C_BEHIND:C_BEHIND + 384 + L] = np.maximum(p + 384 - m, 0)[:, :384 + L]
    q = np.arange(P)[None, :]
    for i, tri in enumerate([p <= q, p >= q, p > q, p < q, p >= 0]):
        c[:, C_TRI + i * P:C_TRI + (i + 1) * P] = tri
    c[:, C_ROT:C_ROT + P] = (p == (q + 64) % P)
    c[:, C_TWICE:C_TWICE + P] = 1 + np.eye(P)
    c[:, C_IOTA:C_IOTA + 16] = np.arange(16)
    counts = np.zeros((4, L), np.float64)
    for g, w in enumerate(WINDOWS):
        counts[g] = np.clip(t + w // 2, 0, L) - np.clip(t - w // 2, 0, L)
    return c, (1.0 / counts).astype(np.float32)


class PsumJobs:

    def __init__(self):
        self.names, self.who, self.rank, self.total = [], [], [], {"A": 0, "D": 0}

    def add(self, name, who):
        self.names.append(name)
        self.who.append(who)
        self.total[who] += 1
        self.rank.append(self.total[who])

    def number(self, *name):
        return self.names.index(name)

    def upto(self, n):
        return {w: sum(x == w for x in self.who[:n]) for w in "AD"}


def plan_jobs():
    jobs = PsumJobs()
    alternate = lambda i: "AD"[i % 2]
    jobs.add(("cols",), "D")
    for c in range(4):
        jobs.add(("mod", c), "D")
    for k in range(KT):
        jobs.add(("norm", 0, k), alternate(k))
    for k in range(KT):
        jobs.add(("normc", k), alternate(k))
    for h in range(HEADS):
        jobs.add(("rk", h), "A")
    for h in range(HEADS):
        jobs.add(("rkrot", h), "D")
    for g in range(2):
        jobs.add(("rkc", g), "A")
    for t in range(TT):
        jobs.add(("rv", t), "A")
    for t in range(TC):
        jobs.add(("rvc", t), "A")
    for h in range(HEADS):
        jobs.add(("rq", h), "A")
    for h in range(HEADS):
        jobs.add(("rqrot", h), "D")
    for h in range(HEADS):
        for j in range(TT + TC):
            jobs.add(("rs", h, j), "D")
        jobs.add(("ro", h), "A")
    for p in range(PAIRS):
        jobs.add(("gq", p), "A")
    for p in range(PAIRS):
        jobs.add(("gk", p), "A")
    jobs.add(("gkc",), "A")
    for t in range(TT):
        jobs.add(("gv", t), alternate(t))
    for t in range(TC):
        jobs.add(("gvc", t), alternate(t))
    jobs.add(("lr",), "A")
    jobs.add(("lrc",), "A")
    for t in range(TT + TC):
        jobs.add(("la", t), "D")
    for p in range(PAIRS):
        for d in (FWD, BWD):
            jobs.add(("cum", p, d), "D")
            jobs.add(("cumc", p, d), "A")
            jobs.add(("kcT", p, d), "A")
            jobs.add(("s0", p, d), "D")
            jobs.add(("kdT", p, d), "A")
            for s in range(TT - 1):
                jobs.add(("up", p, d, s), "D")
    for h in range(HEADS):
        for d in (FWD, BWD):
            jobs.add(("gs", h, d), "A")
    for c in range(TT):
        for odd in range(2):
            jobs.add(("go", c, odd), "A")
    for t in range(TT):
        jobs.add(("rg", t), "A")
    for t in range(TT):
        jobs.add(("gg", t), "A")
    for n in range(2):
        jobs.add(("g1", n), "D")
    for k in range(KT):
        jobs.add(("yT", k), alternate(k))
    for n in range(2):
        for t in range(TT):
            jobs.add(("wo", t, n), "D")
    for c in range(4):
        jobs.add(("mod2", c), "D")
    for n in range(2):
        jobs.add(("g2", n), "D")
    for k in range(KT):
        jobs.add(("norm", 1, k), alternate(k))
    for g in range(4):
        jobs.add(("kT", 0, g), "A")
    for k in range(KT):
        jobs.add(("norm", 2, k), alternate(k))
    for j in range(4):
        jobs.add(("cc", j), "A")
        jobs.add(("cv", j), "D")
        jobs.add(("cb", j), "D")
    for g in range(4):
        jobs.add(("pu", g), "A")
    for g in range(4):
        jobs.add(("py", g), "A")
    for n in range(2):
        for t in range(TT):
            jobs.add(("wo2", t, n), "D")
    for k in range(KT):
        jobs.add(("norm", 3, k), alternate(k))
    for g in range(4):
        jobs.add(("kT", 1, g), "A")
    for k in range(KT):
        jobs.add(("norm", 4, k), alternate(k))
    for k in range(2):
        jobs.add(("pT", k), "A")
    for n in range(2):
        for t in range(TT):
            jobs.add(("gate", t, n), "A")
            jobs.add(("pp", t, n), "D")
    return jobs


def build(nc, a, consts, inv_counts, out):
    jobs = plan_jobs()
    with ExitStack() as ctx:
        def sb(name, shape, dt=F32):
            return ctx.enter_context(nc.sbuf_tensor(name, shape, dt))

        def sem(name):
            return ctx.enter_context(nc.semaphore(name))

        X = sb("X", [P, TT, D])
        hT = sb("hT", [P, KT, L])
        ring = sb("ring", [P, RING * KT * CW])
        const = sb("const", [P, N_CONST])
        row_a = sb("row_a", [P, D])
        row_b = sb("row_b", [P, D])
        cols = sb("cols", [P, N_VEC])
        silu = sb("silu", [P, 2, KT])
        mod = sb("mod", [P, 32, 2])
        gain = sb("gain", [P, 3, KT])
        stat = sb("stat", [P, 4, 6])
        hstat = sb("hstat", [P, 4, 2 * TT * HEADS])
        lg = sb("lg", [P, 4, 8])
        chunk_dec = sb("chunk_dec", [P, 4, TT])
        SCR = 25600
        scr = sb("scr", [P, SCR])
        banks = ctx.enter_context(nc.psum_tensor("banks", [P, 8 * 512], F32))
        psum = [banks[:, 512 * i:512 * (i + 1)] for i in range(8)]
        xn = banks[:, 0:D]
        peer_sum = banks[:, D:2 * D]

        def at(base, off, *dims):
            n = int(np.prod(dims))
            v = base[:, off:off + n]
            if len(dims) == 1:
                return v
            if len(dims) == 2:
                return v.rearrange("p (a b) -> p a b", b=dims[1])
            return v.rearrange("p (a b c) -> p a b c", b=dims[1], c=dims[2])

        ident = const[:, C_IDENT:C_IDENT + P]
        cos_t, sin_t = const[:, C_COS:C_COS + L], const[:, C_SIN:C_SIN + L]
        rot = const[:, C_ROT:C_ROT + P]

        def tri(i):
            return const[:, C_TRI + i * P:C_TRI + (i + 1) * P]

        def chunk(n):
            return at(ring, (n % RING) * KT * CW, KT, CW)

        xr = at(scr, 0, TT, D)
        xc = at(scr, 8192, TC, D)
        vrows = at(scr, 21504, P)[0:N_VEC, :]
        rqT, rkT = at(scr, 0, HEADS, L), at(scr, 2048, HEADS, L)
        o_ret, o_gla = at(scr, 4096, TT, HEADS * DV), at(scr, 6144, TT, HEADS * DV)
        r_p = at(scr, 8192, TT + TC, L)
        rkTc, rv, rvc = at(scr, 11264, HEADS, LC), at(scr, 12288, TT, 512), at(scr, 14336, TC, 512)
        mask_m = [at(scr, 15360 + 3072 * i, 2, 384 + L) for i in range(2)]
        mask_c = [at(scr, 15360 + 3072 * i + 1792, 2, 640) for i in range(2)]
        rot_tmp = at(scr, 8192, 2, L)
        w_lr = at(scr, 22528, KT, 64)
        gk_up = at(scr, 22016, 512)[0:64, :]
        hTc = at(scr, 23040, KT, LC)
        q_in, k_in = at(scr, 0, 4, L), at(scr, 2048, 4, L)
        gqT, gkT, gkTc = at(scr, 8192, PAIRS, L), at(scr, 9216, PAIRS, L), at(scr, 10240, PAIRS, LC)
        gv, gvc = at(scr, 10752, TT, 512), at(scr, 12800, TC, 512)
        la = at(scr, 13824, TT + TC, 512)
        q_st = at(scr, 16896, 4, L)
        kdT = at(scr, 18944, 4, TT, P)
        state = at(scr, 20992, 4, TT, DV)
        g_p = [at(scr, 23040 + 512 * i, TT, P) for i in range(4)] + [at(scr, 13824 + 512 * i, TT, P) for i in range(4)]
        G = at(const, C_COS, L)
        G_mid, G_last, G_neg = at(const, C_AHEAD, L), at(const, C_AHEAD + 512, L), at(const, C_AHEAD + 1024, L)
        kc_exp, kcT = at(const, C_SIN, LC), at(const, C_SIN + LC, TC, P)
        lrT = at(scr, 18944, 768)[0:64, :]
        la_tmp = at(scr, 20992, 2, 512)
        gate_tmp = at(scr, 8192, 2, 512)
        yT = at(scr, 0, KT, L)
        sq_tmp = at(scr, 9216, 2, 512)
        silu_b = at(scr, 24576, KT, P)
        u_rows = at(scr, 0, SLOTS, D)
        v_rows = at(ring, 0, SLOTS, D)
        w_q = at(scr, 8192, KT, PQ)
        diag = at(ring, 2 * KT * CW, TOPK, P)
        peer_qT = at(ring, 2 * KT * CW + 2048, 2, 2, P)
        x_cur = at(ring, 2 * KT * CW + 2560, KT, P)
        onehot = at(ring, 2 * KT * CW + 3584, 2, TOPK, TOPK)
        kT = at(const, C_AHEAD, 2 * PH, P)
        score = at(const, C_COS, 2, 2, NKEYS)
        score_rest = at(const, C_COS + 512, 2, NKEYS)
        cand = at(const, C_COS + 768, TOPK, TOPK)
        cand_rest = at(scr, 24576, TOPK * TOPK)
        o = 24832
        top1 = at(scr, o, 2, TOPK)
        key_f = at(scr, o + 32, 2, TOPK)
        top2 = at(scr, o + 64, TOPK)
        neg_max = at(scr, o + 80, 1)
        exp_s = at(scr, o + 96, TOPK)
        exp_sum = at(scr, o + 112, 1)
        exp_inv = at(scr, o + 113, 1)
        gate = at(scr, o + 128, 2, TOPK)
        picked = at(scr, o + 160, 2, TOPK)
        idx_f = at(scr, o + 192, TOPK)
        dots = at(scr, o + 208, 2, TOPK)
        gelu = at(scr, o + 240, 2, TOPK)
        weight = at(scr, o + 272, 2, TOPK)
        key_i = sb("key_i", [P, 2, TOPK], U32)
        pos_i = sb("pos_i", [P, TOPK], U32)
        pos_ab = sb("pos_ab", [P, 2, TOPK], U32)
        idx = sb("idx", [P, IDX_SLOTS, TOPK], U32)
        yT2 = at(scr, 4096, KT, L)
        z_pad = [at(scr, 514 * i, 514) for i in range(2)]
        u_pad = [at(scr, 1028 + 528 * i, 528) for i in range(2)]
        win = [at(scr, 2084 + 528 * i, 528) for i in range(2)]
        c_gate = at(const, C_COS, 2, L)
        inv_cnt = at(const, C_AHEAD, 4, L)
        pool_w = at(scr, 24576, 4, P)
        p_rows = at(scr, 8192, TT, 256)
        pT = at(scr, 9216, 2, L)
        ple_gate = at(scr, 10240, 2, CW)

        def col(name, k, n=1):
            return cols[:, VEC_AT[name] + k:VEC_AT[name] + k + n]

        bank_ready = sem("bank_ready")
        emptied = {"A": sem("act_emptied"), "D": sem("dve_emptied")}
        const_in, vec_in, x_in, ctx_in, lg_in = sem("const_in"), sem("vec_in"), sem("x_in"), sem("ctx_in"), sem("lg_in")
        lr_in, row_a_in, row_b_in = sem("lr_in"), sem("row_a_in"), sem("row_b_in")
        gap_zeroed = sem("gap_zeroed")
        chunk_in = [sem(f"chunk_in{i}") for i in range(RING)]
        w_q_in, inv_in, pool_w_in, p_in, out_done = (sem("w_q_in"), sem("inv_in"), sem("pool_w_in"), sem("p_in"),
                                                     sem("out_done"))
        silu_done, silu_b_done, gains_done = sem("silu_done"), sem("silu_b_done"), sem("gains_done")
        sumsq, meansq, root, rstd, rows_scaled = sem("sumsq"), sem("meansq"), sem("root"), sem("rstd"), sem("rows_scaled")
        x_new = sem("x_new")
        rotating, roped = sem("rotating"), sem("roped")
        lg_act, lg_step = sem("lg_act"), sem("lg_step")
        exps, mask_step = sem("exps"), sem("mask_step")
        ones_set = sem("ones_set")
        la_act, la_min = sem("la_act"), sem("la_min")
        g_sub, g_exp, g_mul, kc_mul = sem("g_sub"), sem("g_exp"), sem("g_mul"), sem("kc_mul")
        state_half, p_masked = sem("state_half"), sem("p_masked")
        head_step, head_root, y_step, y_done = sem("head_step"), sem("head_root"), sem("y_step"), sem("y_done")
        wo_mul = sem("wo_mul")
        pads_zeroed, conv_step, pool_step, pooled = sem("pads_zeroed"), sem("conv_step"), sem("pool_step"), sem("pooled")
        ple_mul, out_ready = sem("ple_mul"), sem("out_ready")
        u_loaded = [sem(f"u_loaded{i}") for i in range(SLOTS)]
        v_loaded = [sem(f"v_loaded{i}") for i in range(SLOTS)]
        u_used = sem("u_used")
        v_used = sem("v_used")
        x_cur_set, xn_ready = sem("x_cur_set"), sem("xn_ready")
        q_done, q_copied, s_done, s_copied = sem("q_done"), sem("q_copied"), sem("s_done"), sem("s_copied")
        topped = sem("topped")
        exp_done, gelu_done, weighted = sem("exp_done"), sem("gelu_done"), sem("weighted")
        routed = sem("routed")
        diag_set = sem("diag_set")
        x_added = sem("x_added")
        route_step = sem("route_step")
        sum_scaled = sem("sum_scaled")
        passed = sem("passed")

        def full(eng, *name):
            n = jobs.number(*name)
            eng.wait_ge(bank_ready, n + 1)
            return psum[n % 8]

        def empty(eng, *name):
            n = jobs.number(*name)
            eng.wait_ge(emptied[jobs.who[n]], jobs.rank[n])

        def all_empty(eng, *last):
            for w, n in jobs.upto(jobs.number(*last) + 1).items():
                eng.wait_ge(emptied[w], n)

        def chunk_read(eng, n):
            eng.wait_ge(bank_ready, jobs.number(*CHUNK_LAST_JOB[CHUNKS[n]]) + 1)

        def hold(eng, s, value):
            eng.wait_ge(s, value)
            eng.sem_inc(passed, 1)

        NORM_TILES = [TT + TC, TT, TT, TT, TT, TT, TT]
        ROWS_UPTO = [sum(NORM_TILES[:i + 1]) for i in range(len(NORM_TILES))]
        NORM_R = {0: 0, 1: 1, 2: 3, 3: 4, 4: 5}

        block = ctx.enter_context(nc.Block())

        @block.sync
        def _(sp):
            wide = {"w_mod": a["w_mod"][0], "w_in": a["w_in"][0], "w_out": a["w_out"][0],
                    "w_in_2": a["w_in_2"][0], "w_o_2": a["w_o_2"][0], "w_ple_gate_2": a["w_ple_gate_2"][0]}

            def load_chunk(n):
                name, c0 = CHUNKS[n]
                if n >= RING:
                    chunk_read(sp, n - RING)
                s = chunk_in[n % RING]
                if name in wide:
                    sp.dma_start(chunk(n), wide[name].rearrange("(k p) n -> p k n", p=P)[:, :, c0:c0 + CW]).then_inc(s, 16)
                elif name == "keys":
                    raw = at(ring, (n % RING) * KT * CW, PH, 2, P)
                    sp.dma_start(raw[:, :, 0, :], a["peer_k1"][0].rearrange("h n d -> n h d")).then_inc(s, 16)
                    sp.dma_start(raw[:, :, 1, :], a["peer_k2"][0].rearrange("h n d -> n h d")).then_inc(s, 16)
                elif name == "keys_2":
                    raw = at(ring, (n % RING) * KT * CW, 2 * PH, P)
                    sp.dma_start(raw, a["sub_keys_2"][0].rearrange("h s n d -> n (h s) d")).then_inc(s, 16)
                else:
                    raw = at(ring, (n % RING) * KT * CW, 2, D)
                    sp.dma_start(raw, a["w_ple_proj_2"][0].rearrange("(k p) n -> p k n", p=P)).then_inc(s, 16)

            for name, rows in VEC:
                src = a[name]
                dims = " ".join("abcd"[:len(src.shape)])
                flat = src.rearrange(f"{dims} -> ({dims})") if len(src.shape) > 1 else src
                sp.dma_start(vrows[VEC_AT[name]:VEC_AT[name] + rows, :],
                             flat.rearrange("(r p) -> r p", p=P)).then_inc(vec_in, 16)
            sp.dma_start(const[:, :], consts).then_inc(const_in, 16)
            load_chunk(0)
            sp.dma_start(X[:, :, :], a["x"][0].rearrange("(t p) d -> p t d", p=P)).then_inc(x_in, 16)
            sp.dma_start(xc, a["ctx"][0].rearrange("(t p) d -> p t d", p=P)).then_inc(ctx_in, 16)
            sp.dma_start(lg[:, 0, 0:4], a["ret_decay_f"][0].partition_broadcast(P)).then_inc(lg_in, 16)
            sp.dma_start(lg[:, 0, 4:8], a["ret_decay_b"][0].partition_broadcast(P)).then_inc(lg_in, 16)
            load_chunk(1)
            load_chunk(2)
            sp.wait_ge(gap_zeroed, 2)
            for d in (FWD, BWD):
                sp.dma_start(w_lr[:, :, 32 * d:32 * d + RANK],
                             a["w_in"][0].rearrange("(k p) n -> p k n", p=P)[:, :, W_LR + RANK * d:W_LR + RANK * (d + 1)]
                             ).then_inc(lr_in, 16)
                up, bias = (a["gla_gk_up_f"], a["gla_gk_bias_f"]) if d == FWD else (a["gla_gk_up_b"], a["gla_gk_bias_b"])
                sp.dma_start(gk_up[32 * d:32 * d + RANK, 256 * d:256 * (d + 1)], up[0]).then_inc(lr_in, 16)
                sp.dma_start(gk_up[32 * d + RANK:32 * d + RANK + 1, 256 * d:256 * (d + 1)], bias).then_inc(lr_in, 16)
            sp.dma_start(row_a[:, :], a["b_mod"][0, 2 * D:3 * D].partition_broadcast(P)).then_inc(row_a_in, 16)
            sp.dma_start(row_b[:, :], a["b_mod"][0, 5 * D:6 * D].partition_broadcast(P)).then_inc(row_b_in, 16)
            for n in range(3, chunk_number("w_out", CW) + 1):
                load_chunk(n)
            full(sp, "yT", KT - 1)
            sp.dma_start(w_q, a["peer_w_q"][0].rearrange("(k p) n -> p k n", p=P)).then_inc(w_q_in, 16)
            for n in range(chunk_number("w_mod", CW * 6), chunk_number("keys") + 1):
                load_chunk(n)
            all_empty(sp, "wo", TT - 1, 1)
            sp.dma_start(row_a[:, :], a["norm_f_w"].partition_broadcast(P)).then_inc(row_a_in, 16)

            sp.wait_ge(q_done, TT * PH)
            sp.dma_start(w_q, a["w_q_2"][0].rearrange("(k p) n -> p k n", p=P)).then_inc(w_q_in, 16)
            sp.wait_ge(x_added, 1 + TT)
            sp.dma_start(row_b[:, :], a["g_final_2"].partition_broadcast(P)).then_inc(row_b_in, 16)
            sp.dma_start(inv_cnt, inv_counts.partition_broadcast(P)).then_inc(inv_in, 16)
            sp.dma_start(pool_w, a["pool_w_2"][0].rearrange("g c d -> c g d")).then_inc(pool_w_in, 16)
            for n in range(chunk_number("w_in_2"), chunk_number("keys_2") + 1):
                load_chunk(n)
            sp.wait_ge(x_added, 1 + 2 * TT)
            sp.dma_start(p_rows, a["p_2"][0, 0].rearrange("(t p) d -> p t d", p=P)).then_inc(p_in, 16)
            for n in range(chunk_number("w_ple_gate_2"), len(CHUNKS)):
                load_chunk(n)
            for t in range(TT):
                sp.wait_ge(out_ready, t + 1)
                sp.dma_start(out[0, t * P:(t + 1) * P, :], xr[:, t, :]).then_inc(out_done, 16)
            sp.wait_ge(out_done, 16 * TT)

        @block.gpsimd
        def _(pool):
            nc.gpsimd.memset(w_lr[:, :, :], 0.0).then_inc(gap_zeroed, 1)
            nc.gpsimd.memset(gk_up, 0.0).then_inc(gap_zeroed, 1)
            for h in range(HEADS):
                for d in (FWD, BWD):
                    empty(pool, "gs", h, d)
                    v = g_p[2 * h + d]
                    sign = 1 if d == FWD else -1
                    nc.gpsimd.affine_select(out=v, in_=v, pattern=[[0, TT], [sign, P]], compare_op=ALU.is_ge, fill=0.0,
                                            base=0, channel_multiplier=-sign).then_inc(p_masked, 1)

            def gathers(layer, table_u, table_v):
                def u_gather(n, h, k):
                    hold(pool, u_used, n * TOPK + (k + 1))
                    nc.gpsimd.indirect_dma_start(u_rows[:, k % SLOTS, :], None, table_u,
                                                 bass.IndirectOffsetOnAxis(idx[:, h % IDX_SLOTS, k:k + 1], 0)
                                                 ).then_inc(u_loaded[k % SLOTS], 16)

                def v_gather(n, h, k):
                    hold(pool, v_used, n * TOPK + (k + 1 - SLOTS + V_CREDIT))
                    nc.gpsimd.indirect_dma_start(v_rows[:, k % SLOTS, :], None, table_v,
                                                 bass.IndirectOffsetOnAxis(idx[:, h % IDX_SLOTS, k:k + 1], 0)
                                                 ).then_inc(v_loaded[k % SLOTS], 16)

                with pool.Fori(0, TT) as b:
                    first = b * PH + layer * TT * PH
                    for h in range(PH):
                        hold(pool, routed, first + (h + 3))
                        for k in range(TOPK):
                            u_gather(first + h, h, k)
                            if h >= 1:
                                v_gather(first + (h - 1), h - 1, k)
                    for k in range(TOPK):
                        v_gather(first + (PH - 1), PH - 1, k)

            full(pool, "kT", 0, 3)
            gathers(0, a["peer_down"][0], a["peer_up"][0])
            full(pool, "norm", 2, KT - 1)
            for i in range(2):
                nc.gpsimd.memset(z_pad[i], 0.0).then_inc(pads_zeroed, 1)
                nc.gpsimd.memset(u_pad[i], 0.0).then_inc(pads_zeroed, 1)
            full(pool, "kT", 1, 3)
            gathers(1, a["expert_u_2"][0], a["expert_v_2"][0])

        @block.tensor
        def _(pe):
            state_pe = {"job": 0, "chunk": 0}

            def begin(*name):
                n = state_pe["job"]
                assert jobs.names[n] == name, (jobs.names[n], name)
                state_pe["job"] += 1
                if n >= 8:
                    pe.wait_ge(emptied[jobs.who[n - 8]], jobs.rank[n - 8])
                return psum[n % 8]

            def mm(o, lhsT, rhs, i, n):
                return nc.tensor.matmul(o, lhsT, rhs, start=(i == 0), stop=(i == n - 1))

            def use_chunk(name, c0):
                n = state_pe["chunk"]
                assert CHUNKS[n] == (name, c0)
                state_pe["chunk"] += 1
                loads = 16 * sum(2 if CHUNKS[m][0] == "keys" else 1 for m in range(n % RING, n + 1, RING))
                pe.wait_ge(chunk_in[n % RING], loads)
                return chunk(n)

            def norm_rows(i):
                pe.wait_ge(rows_scaled, ROWS_UPTO[NORM_R[i]])
                for k in range(KT):
                    o = begin("norm", i, k)
                    for t in range(TT):
                        last = nc.tensor.transpose(o[:, t * P:(t + 1) * P], xr[:, t, k * P:(k + 1) * P], ident)
                    last.then_inc(bank_ready, 1)

            def to_rows(names, src, w, tiles):
                for name, t in zip(names, range(tiles)):
                    o = begin(*name)
                    for k in range(KT):
                        last = mm(o[:, :], src[:, k, t * P:(t + 1) * P], w[:, k, :], k, KT)
                    last.then_inc(bank_ready, 1)

            def to_cols(names, src, w, n):
                for j, name in enumerate(names):
                    o = begin(*name)
                    for k in range(KT):
                        last = mm(o[:, 0:n], w[:, k, j * P:(j + 1) * P], src[:, k, :], k, KT)
                    last.then_inc(bank_ready, 1)

            pe.sem_inc(v_used, V_CREDIT)

            pe.wait_ge(vec_in, 16 * len(VEC))
            pe.wait_ge(const_in, 16)
            o = begin("cols")
            nc.tensor.transpose(o[:, 0:N_VEC], vrows[:, :], ident[0:N_VEC, 0:N_VEC]).then_inc(bank_ready, 1)

            def modulation(name, c, c0):
                w = use_chunk("w_mod", c0)
                o = begin(name, c)
                for j in range(4):
                    for k in range(KT):
                        last = mm(o[:, 2 * j:2 * j + 2], w[:, k, j * P:(j + 1) * P], silu[:, :, k], k, KT)
                last.then_inc(bank_ready, 1)

            pe.wait_ge(silu_done, 1)
            for c in range(4):
                modulation("mod", c, CW * c)

            norm_rows(0)
            for k in range(KT):
                o = begin("normc", k)
                for t in range(TC):
                    last = nc.tensor.transpose(o[:, t * P:(t + 1) * P], xc[:, t, k * P:(k + 1) * P], ident)
                last.then_inc(bank_ready, 1)

            w = use_chunk("w_in", W_RK)
            empty(pe, "norm", 0, KT - 2)
            empty(pe, "norm", 0, KT - 1)
            to_cols([("rk", h) for h in range(HEADS)], hT, w, L)

            def rotate(name, src):
                for h in range(HEADS):
                    o = begin(name + "rot", h)
                    empty(pe, name, h)
                    mm(o[:, :], rot, src[:, h, :], 0, 1).then_inc(bank_ready, 1)

            rotate("rk", rkT)
            empty(pe, "normc", KT - 2)
            empty(pe, "normc", KT - 1)
            for g in range(2):
                o = begin("rkc", g)
                for j in range(2):
                    for k in range(KT):
                        last = mm(o[:, j * LC:(j + 1) * LC], w[:, k, (2 * g + j) * P:(2 * g + j + 1) * P], hTc[:, k, :], k, KT)
                last.then_inc(bank_ready, 1)
            w = use_chunk("w_in", W_RV)
            to_rows([("rv", t) for t in range(TT)], hT, w, TT)
            to_rows([("rvc", t) for t in range(TC)], hTc, w, TC)
            w = use_chunk("w_in", W_RQ)
            to_cols([("rq", h) for h in range(HEADS)], hT, w, L)
            rotate("rq", rqT)

            empty(pe, "rvc", TC - 1)
            empty(pe, "rkc", 1)
            pe.wait_ge(roped, 2 * HEADS)
            for h in range(HEADS):
                for j in range(TT + TC):
                    o = begin("rs", h, j)
                    keys = rkT[:, h, j * P:(j + 1) * P] if j < TT else rkTc[:, h, (j - TT) * P:(j - TT + 1) * P]
                    mm(o[:, :], keys, rqT[:, h, :], 0, 1).then_inc(bank_ready, 1)
                o = begin("ro", h)
                empty(pe, "rs", h, TT + TC - 1)
                for t in range(TT):
                    for j in range(TT + TC):
                        vals = rv[:, j, h * DV:(h + 1) * DV] if j < TT else rvc[:, j - TT, h * DV:(h + 1) * DV]
                        last = mm(o[:, t * P:(t + 1) * P], r_p[:, j, t * P:(t + 1) * P], vals, j, TT + TC)
                last.then_inc(bank_ready, 1)

            w = use_chunk("w_in", W_GQK)
            to_cols([("gq", p) for p in range(PAIRS)] + [("gk", p) for p in range(PAIRS)], hT, w, L)
            o = begin("gkc")
            for p in range(PAIRS):
                for k in range(KT):
                    last = mm(o[:, p * LC:(p + 1) * LC], w[:, k, (PAIRS + p) * P:(PAIRS + p + 1) * P], hTc[:, k, :], k, KT)
            last.then_inc(bank_ready, 1)
            w = use_chunk("w_in", W_GV)
            to_rows([("gv", t) for t in range(TT)], hT, w, TT)
            to_rows([("gvc", t) for t in range(TC)], hTc, w, TC)
            pe.wait_ge(lr_in, 16 * 6)
            for name, src, n in (("lr", hT, L), ("lrc", hTc, LC)):
                o = begin(name)
                for k in range(KT):
                    last = mm(o[0:64, 0:n], w_lr[:, k, :], src[:, k, :], k, KT)
                last.then_inc(bank_ready, 1)
            empty(pe, "lr")
            empty(pe, "lrc")
            for t in range(TT + TC):
                o = begin("la", t)
                mm(o[:, :], lrT[:, t * P:(t + 1) * P], gk_up, 0, 1).then_inc(bank_ready, 1)

            empty(pe, "la", TT + TC - 1)
            empty(pe, "gvc", 0)
            empty(pe, "gvc", 1)
            for p in range(PAIRS):
                for d in (FWD, BWD):
                    i = 2 * p + d
                    f = slice(d * 256 + p * P, d * 256 + (p + 1) * P)
                    o = begin("cum", p, d)
                    for c in range(TT):
                        last = mm(o[:, c * P:(c + 1) * P], la[:, c, f], tri(TRI_PREFIX if d == FWD else TRI_SUFFIX), 0, 1)
                    last.then_inc(bank_ready, 1)
                    o = begin("cumc", p, d)
                    own = tri(TRI_AFTER if d == FWD else TRI_BEFORE)
                    for t in range(TC):
                        other = t == (0 if d == FWD else TC - 1)
                        last = mm(o[:, t * P:(t + 1) * P], la[:, TT + t, f], own, 0, 1 + other)
                        if other:
                            last = mm(o[:, t * P:(t + 1) * P], la[:, TT + 1 - t, f], tri(TRI_ONES), 1, 2)
                    last.then_inc(bank_ready, 1)
                    o = begin("kcT", p, d)
                    pe.wait_ge(kc_mul, i + 1)
                    for t in range(TC):
                        last = nc.tensor.transpose(o[:, t * P:(t + 1) * P], kc_exp[:, t * P:(t + 1) * P], ident)
                    last.then_inc(bank_ready, 1)
                    o = begin("s0", p, d)
                    empty(pe, "kcT", p, d)
                    for t in range(TC):
                        last = mm(o[:, 0:256], kcT[:, t, :], gvc[:, t, p * 256:(p + 1) * 256], t, TC)
                    last.then_inc(bank_ready, 1)
                    o = begin("kdT", p, d)
                    pe.wait_ge(g_mul, 4 * (i + 1))
                    for c in range(TT):
                        last = nc.tensor.transpose(o[:, c * P:(c + 1) * P], G_last[:, c * P:(c + 1) * P], ident)
                    last.then_inc(bank_ready, 1)
                    empty(pe, "kdT", p, d)
                    for s in range(TT - 1):
                        o = begin("up", p, d, s)
                        c = s if d == FWD else TT - 1 - s
                        mm(o[:, 0:256], kdT[:, i, c, :], gv[:, c, p * 256:(p + 1) * 256], 0, 1).then_inc(bank_ready, 1)
            for h in range(HEADS):
                for d in (FWD, BWD):
                    o = begin("gs", h, d)
                    i, r = 2 * (h // 2) + d, slice(64 * (h % 2), 64 * (h % 2) + 64)
                    for c in range(TT):
                        cs = slice(c * P, (c + 1) * P)
                        last = mm(o[:, cs], k_in[r, i, cs], q_in[r, i, cs], 0, 1)
                    last.then_inc(bank_ready, 1)
            pe.wait_ge(p_masked, 2 * HEADS)
            empty(pe, "up", 1, BWD, TT - 2)
            for c in range(TT):
                cs = slice(c * P, (c + 1) * P)
                for odd in range(2):
                    o = begin("go", c, odd)
                    r = slice(64 * odd, 64 * odd + 64)
                    for p in range(PAIRS):
                        h, oh = 2 * p + odd, o[:, p * DV:(p + 1) * DV]
                        for d in (FWD, BWD):
                            mm(oh, g_p[2 * h + d][:, c, :], gv[:, c, h * DV:(h + 1) * DV], 2 * d, 4)
                            last = mm(oh, q_st[r, 2 * p + d, cs], state[r, 2 * p + d, c, :], 2 * d + 1, 4)
                    last.then_inc(bank_ready, 1)

            w = use_chunk("w_in", W_RG)
            to_rows([("rg", t) for t in range(TT)], hT, w, TT)
            w = use_chunk("w_in", W_GG)
            to_rows([("gg", t) for t in range(TT)], hT, w, TT)

            def gate_row(name, n, c0):
                w = use_chunk("w_mod", c0)
                o = begin(name, n)
                for k in range(KT):
                    last = mm(o[:, :], silu_b[:, k, :], w[:, k, :], k, KT)
                last.then_inc(bank_ready, 1)

            pe.wait_ge(silu_b_done, 1)
            for n in range(2):
                gate_row("g1", n, CW * (4 + n))

            pe.wait_ge(y_done, 2 * TT)
            for k in range(KT):
                o = begin("yT", k)
                src = o_ret if k < HEADS else o_gla
                for t in range(TT):
                    last = nc.tensor.transpose(o[:, t * P:(t + 1) * P], src[:, t, (k % HEADS) * P:(k % HEADS + 1) * P], ident)
                last.then_inc(bank_ready, 1)
            for n in range(2):
                w = use_chunk("w_out", CW * n)
                empty(pe, "yT", KT - 2)
                empty(pe, "yT", KT - 1)
                to_rows([("wo", t, n) for t in range(TT)], yT, w, TT)
            for c in range(4):
                modulation("mod2", c, CW * (6 + c))
            for n in range(2):
                gate_row("g2", n, CW * (10 + n))

            def keys(layer, name):
                n = state_pe["chunk"]
                use_chunk(name, 0)
                raw = at(ring, (n % RING) * KT * CW, 2 * PH, P)
                for g in range(4):
                    o = begin("kT", layer, g)
                    for j in range(4):
                        last = nc.tensor.transpose(o[:, j * P:(j + 1) * P], raw[:, 4 * g + j, :], ident)
                    last.then_inc(bank_ready, 1)

            def peer(layer):
                def scores(n, h):
                    q, s = psum[4 + h % 2], psum[6 + h % 2]
                    for half in range(2):
                        for k in range(KT):
                            c0 = (2 * h + half) * P
                            last = mm(q[:, half * P:(half + 1) * P], w_q[:, k, c0:c0 + P], x_cur[:, k, :], k, KT)
                    last.then_inc(q_done, 1)
                    pe.wait_ge(q_copied, n + 1)
                    for half in range(2):
                        last = mm(s[:, half * P:(half + 1) * P], peer_qT[:, h % 2, half, :], kT[:, 2 * h + half, :], 0, 1)
                    last.then_inc(s_done, 1)

                def block_rows():
                    for k in range(KT):
                        last = nc.tensor.transpose(psum[k // 4][:, (k % 4) * P:(k % 4 + 1) * P], x_cur[:, k, :], ident)
                    last.then_inc(xn_ready, 1)

                def add_up(n, h):
                    for k in range(TOPK):
                        pe.wait_ge(diag_set, n * TOPK + (k + 1))
                        pe.wait_ge(v_loaded[k % SLOTS], n * (16 * TOPK // SLOTS) + 16 * (k // SLOTS + 1))
                        for c in range(2):
                            last = nc.tensor.matmul(psum[2 + c][:, :], diag[:, k, :], v_rows[:, k % SLOTS, c * CW:(c + 1) * CW],
                                                    start=(h == 0 and k == 0), stop=(h == PH - 1 and k == TOPK - 1))
                        last.then_inc(v_used, 1)

                def token_block(it, more):
                    for h in range(PH):
                        if h < PH - 1:
                            scores(it * PH + (h + 1), h + 1)
                        elif more:
                            pe.wait_ge(x_cur_set, it + 2)
                            scores(it * PH + PH, 0)
                        if h == 1:
                            pe.wait_ge(x_added, it + 1)
                        if h >= 1:
                            add_up(it * PH + (h - 1), h - 1)
                    if more:
                        pe.wait_ge(u_used, it * (PH * TOPK) + (PH * TOPK + SLOTS))
                        block_rows()
                    add_up(it * PH + (PH - 1), PH - 1)

                all_empty(pe, "kT", layer, 3)
                pe.wait_ge(w_q_in, 16 * (layer + 1))
                pe.wait_ge(x_cur_set, layer * TT + 1)
                scores(layer * TT * PH, 0)
                block_rows()
                with pe.Fori(0, TT - 1) as b:
                    token_block(b + layer * TT, True)
                token_block(TT - 1 + layer * TT, False)
                pe.wait_ge(x_added, 1 + TT * (layer + 1))

            norm_rows(1)
            keys(0, "keys")
            peer(0)

            norm_rows(2)
            w = [use_chunk("w_in_2", CW * i) for i in range(3)]
            empty(pe, "norm", 2, KT - 2)
            empty(pe, "norm", 2, KT - 1)
            for j in range(4):
                for name, i in (("cc", 1), ("cv", 2), ("cb", 0)):
                    o = begin(name, j)
                    for k in range(KT):
                        last = mm(o[:, :], w[i][:, k, j * P:(j + 1) * P], hT[:, k, :], k, KT)
                    last.then_inc(bank_ready, 1)
            w = use_chunk("w_in_2", CW * 3)
            to_cols([("pu", g) for g in range(4)], hT, w, L)
            pe.wait_ge(pool_w_in, 16)
            for g in range(4):
                o = begin("py", g)
                pe.wait_ge(pooled, g + 1)
                mm(o[:, :], pool_w[:, g, :], yT2[:, 4 + g, :], 0, 1).then_inc(bank_ready, 1)
            empty(pe, "cb", 3)
            for n in range(2):
                w = use_chunk("w_o_2", CW * n)
                empty(pe, "py", 3)
                to_rows([("wo2", t, n) for t in range(TT)], yT2, w, TT)
            norm_rows(3)
            keys(1, "keys_2")
            peer(1)

            norm_rows(4)
            pe.wait_ge(p_in, 16)
            for k in range(2):
                o = begin("pT", k)
                for t in range(TT):
                    last = nc.tensor.transpose(o[:, t * P:(t + 1) * P], p_rows[:, t, k * P:(k + 1) * P], ident)
                last.then_inc(bank_ready, 1)
            w = [use_chunk("w_ple_gate_2", CW * i) for i in range(2)]
            use_chunk("w_ple_proj_2", 0)
            w_proj = at(ring, (chunk_number("w_ple_proj_2") % RING) * KT * CW, 2, D)
            empty(pe, "norm", 4, KT - 2)
            empty(pe, "norm", 4, KT - 1)
            empty(pe, "pT", 1)
            for n in range(2):
                for t in range(TT):
                    o = begin("gate", t, n)
                    for k in range(KT):
                        last = mm(o[:, :], hT[:, k, t * P:(t + 1) * P], w[n][:, k, :], k, KT)
                    last.then_inc(bank_ready, 1)
                    o = begin("pp", t, n)
                    for k in range(2):
                        last = mm(o[:, :], pT[:, k, t * P:(t + 1) * P], w_proj[:, k, n * CW:(n + 1) * CW], k, 2)
                    last.then_inc(bank_ready, 1)

        @block.scalar
        def _(act):
            def copy_out(dst, *name, scale=1.0):
                o = full(act, *name)
                n = int(np.prod(dst.shape[1:]))
                src = o[0:dst.shape[0], 0:n]
                if len(dst.shape) == 3:
                    src = src.rearrange("p (a b) -> p a b", b=dst.shape[2])
                return nc.scalar.activation(dst, src, ACT.Copy, scale=scale)

            def squares(r, wait_rows, tiles):
                for t, (rows, junk) in enumerate(tiles):
                    wait_rows(t)
                    nc.scalar.activation(junk, rows, ACT.Square, accum_out=stat[:, 0, t:t + 1]).then_inc(sumsq, 1)
                act.wait_ge(meansq, r + 1)
                nc.scalar.activation(stat[:, 2, 0:len(tiles)], stat[:, 1, 0:len(tiles)], ACT.Sqrt).then_inc(root, 1)

            x_tiles = [(X[:, t, :], xr[:, t, :]) for t in range(TT)]

            def transposed(i, gains, shifts):
                for k in range(0, KT, 2):
                    o = full(act, "norm", i, k)
                    nc.scalar.activation(hT[:, k, :], o[:, :], ACT.Identity, bias=shifts(k), scale=gains(k)
                                         ).then_inc(emptied["A"], 1)

            empty(act, "cols")
            nc.scalar.activation(silu[:, :, :].rearrange("p a k -> p (a k)"), cols[:, 0:2 * KT], ACT.Silu).then_inc(silu_done, 1)
            junk_c = at(scr, 23040, TC, D)
            squares(0, lambda t: act.wait_ge(x_in if t < TT else ctx_in, 16),
                    x_tiles + [(xc[:, t, :], junk_c[:, t, :]) for t in range(TC)])

            act.wait_ge(lg_in, 32)
            nc.scalar.activation(lg[:, 1, :], lg[:, 0, :], ACT.Abs).then_inc(lg_act, 1)
            act.wait_ge(lg_act, 1)
            nc.scalar.activation(lg[:, 1, :], lg[:, 1, :], ACT.Exp, scale=-1.0).then_inc(lg_act, 1)
            act.wait_ge(lg_act, 2)
            nc.scalar.activation(lg[:, 1, :], lg[:, 1, :], ACT.Ln, bias=1.0).then_inc(lg_act, 1)

            def decay_masks(h):
                if h >= 2:
                    empty(act, "rs", h - 2, TT + TC - 1)
                m, c = mask_m[h % 2], mask_c[h % 2]
                ahead, behind = const[:, C_AHEAD:C_AHEAD + 384 + L], const[:, C_BEHIND:C_BEHIND + 384 + L]
                since = const[:, C_AHEAD + 512:C_AHEAD + 512 + 640]
                nc.scalar.activation(m[:, 0, :], ahead, ACT.Exp, scale=lg[:, 3, h:h + 1]).then_inc(exps, 1)
                nc.scalar.activation(m[:, 1, :], behind, ACT.Exp, scale=lg[:, 3, 4 + h:5 + h]).then_inc(exps, 1)
                nc.scalar.activation(c[:, 0, :], since, ACT.Exp, scale=lg[:, 3, h:h + 1]).then_inc(exps, 1)
                nc.scalar.activation(c[:, 1, :], since, ACT.Exp, scale=lg[:, 1, 4 + h:5 + h], bias=lg[:, 2, 4 + h:5 + h]
                                     ).then_inc(exps, 1)

            act.wait_ge(lg_step, 4)
            decay_masks(0)
            decay_masks(1)

            act.wait_ge(gains_done, 2)
            transposed(0, lambda k: gain[:, 0, k:k + 1], lambda k: mod[:, k, 0:1])
            for k in range(0, KT, 2):
                o = full(act, "normc", k)
                nc.scalar.activation(hTc[:, k, :], o[:, 0:LC], ACT.Identity, bias=mod[:, k, 1:2], scale=gain[:, 1, k:k + 1]
                                     ).then_inc(emptied["A"], 1)
            for h in range(HEADS):
                copy_out(rkT[:, h, :], "rk", h, scale=RET_DK ** -0.5).then_inc(emptied["A"], 1)
            for g in range(2):
                copy_out(rkTc[:, 2 * g:2 * g + 2, :], "rkc", g, scale=RET_DK ** -0.5).then_inc(emptied["A"], 1)
            for t in range(TT):
                copy_out(rv[:, t, :], "rv", t).then_inc(emptied["A"], 1)
            for t in range(TC):
                copy_out(rvc[:, t, :], "rvc", t).then_inc(emptied["A"], 1)
            for h in range(HEADS):
                copy_out(rqT[:, h, :], "rq", h).then_inc(emptied["A"], 1)
            for h in range(HEADS):
                copy_out(o_ret[:, :, h * DV:(h + 1) * DV], "ro", h).then_inc(emptied["A"], 1)
                if h + 2 < HEADS:
                    decay_masks(h + 2)

            for p in range(PAIRS):
                copy_out(gqT[:, p, :], "gq", p, scale=GLA_DK ** -0.5).then_inc(emptied["A"], 1)
            for p in range(PAIRS):
                copy_out(gkT[:, p, :], "gk", p).then_inc(emptied["A"], 1)
            copy_out(gkTc, "gkc").then_inc(emptied["A"], 1)
            for t in range(0, TT, 2):
                copy_out(gv[:, t, :], "gv", t).then_inc(emptied["A"], 1)
            copy_out(gvc[:, 0, :], "gvc", 0).then_inc(emptied["A"], 1)
            act.wait_ge(ones_set, 1)
            for name, c0, n in (("lr", 0, L), ("lrc", L, LC)):
                o = full(act, name)
                nc.scalar.activation(lrT[0:RANK, c0:c0 + n], o[0:RANK, 0:n], ACT.Copy)
                nc.scalar.activation(lrT[32:32 + RANK, c0:c0 + n], o[32:32 + RANK, 0:n], ACT.Copy).then_inc(emptied["A"], 1)
            for t in range(TT + TC):
                if t >= 2:
                    empty(act, "la", t - 2)
                o, v = full(act, "la", t), la_tmp[:, t % 2, :]
                nc.scalar.activation(v, o[:, :], ACT.Abs).then_inc(la_act, 1)
                act.wait_ge(la_act, 3 * t + 1)
                nc.scalar.activation(v, v, ACT.Exp, scale=-1.0).then_inc(la_act, 1)
                act.wait_ge(la_act, 3 * t + 2)
                nc.scalar.activation(v, v, ACT.Ln, bias=1.0).then_inc(la_act, 1)
            for p in range(PAIRS):
                for d in (FWD, BWD):
                    i, last = 2 * p + d, P - 1 if d == FWD else 0
                    o = full(act, "cumc", p, d)
                    nc.scalar.activation(kc_exp, o[:, 0:LC], ACT.Exp).then_inc(emptied["A"], 1)
                    act.wait_ge(g_sub, 2 * (i + 1))
                    nc.scalar.activation(G_neg, G_mid, ACT.Exp, scale=-1.0).then_inc(g_exp, 1)
                    nc.scalar.activation(G_mid, G_mid, ACT.Exp).then_inc(g_exp, 1)
                    nc.scalar.activation(G_last, G_last, ACT.Exp, scale=-1.0).then_inc(g_exp, 1)
                    nc.scalar.activation(chunk_dec[:, i, :], G.rearrange("p (c t) -> p c t", t=P)[:, :, last], ACT.Exp
                                         ).then_inc(g_exp, 1)
                    act.wait_ge(g_exp, 5 * i + 4)
                    nc.scalar.activation(G, G, ACT.Exp).then_inc(g_exp, 1)
                    copy_out(kcT, "kcT", p, d).then_inc(emptied["A"], 1)
                    copy_out(kdT[:, i, :, :], "kdT", p, d).then_inc(emptied["A"], 1)
            for h in range(HEADS):
                for d in (FWD, BWD):
                    copy_out(g_p[2 * h + d], "gs", h, d).then_inc(emptied["A"], 1)
            for c in range(TT):
                for odd in range(2):
                    copy_out(o_gla[:, c, :].rearrange("p (a b v) -> p b a v", b=2, v=DV)[:, odd], "go", c, odd
                             ).then_inc(emptied["A"], 1)

            nc.scalar.activation(silu_b, silu[:, 0, :].unsqueeze(2).to_broadcast([P, KT, P]), ACT.Copy).then_inc(silu_b_done, 1)
            act.wait_ge(head_step, 4 * TT + 1)
            nc.scalar.activation(hstat[:, 2, :], hstat[:, 1, :], ACT.Sqrt).then_inc(head_root, 1)
            for u in range(2 * TT):
                if u >= 2:
                    act.wait_ge(y_done, u - 1)
                o = full(act, "rg" if u < TT else "gg", u % TT)
                nc.scalar.activation(gate_tmp[:, u % 2, :], o[:, :], ACT.Silu).then_inc(emptied["A"], 1)
            for k in range(0, KT, 2):
                copy_out(yT[:, k, :], "yT", k).then_inc(emptied["A"], 1)

            def added(name, t):
                empty(act, name, t, 1)

            squares(1, lambda t: added("wo", TT - 1), x_tiles)
            act.wait_ge(gains_done, 3)
            transposed(1, lambda k: gain[:, 2, k:k + 1], lambda k: mod[:, 16 + k, 0:1])
            for g in range(4):
                copy_out(kT[:, 4 * g:4 * g + 4, :], "kT", 0, g).then_inc(emptied["A"], 1)

            def peer(layer, gelu_func):
                def rows_of(it, b):
                    nc.scalar.activation(x_cur, hT[:, :, bass.ds(b * P, P)], ACT.Copy).then_inc(x_cur_set, 1)

                def scores_out(n, h):
                    act.wait_ge(q_done, n + 1)
                    nc.scalar.activation(peer_qT[:, h % 2, :, :].rearrange("p a b -> p (a b)"), psum[4 + h % 2][:, 0:2 * P],
                                         ACT.Copy).then_inc(q_copied, 1)
                    hold(act, routed, n + 1)
                    act.wait_ge(s_done, n + 1)
                    nc.scalar.activation(score[:, h % 2, :, :].rearrange("p a b -> p (a b)"), psum[6 + h % 2][:, 0:2 * P],
                                         ACT.Copy).then_inc(s_copied, 1)

                def softmax_exp(n):
                    act.wait_ge(topped, n + 1)
                    nc.scalar.activation(exp_s, top2, ACT.Exp, bias=neg_max, accum_out=exp_sum).then_inc(exp_done, 1)

                def token_block(it, b, more):
                    for h in range(PH):
                        n = it * PH + h
                        if h < PH - 1:
                            scores_out(n + 1, h + 1)
                            softmax_exp(n + 1)
                        elif more:
                            hold(act, q_done, it * PH + PH)
                            rows_of(it + 1, b + 1)
                            scores_out(n + 1, 0)
                            softmax_exp(n + 1)
                        act.wait_ge(u_used, n * TOPK + (TOPK + SLOTS))
                        nc.scalar.activation(gelu[:, h % 2, :], dots[:, h % 2, :], gelu_func).then_inc(gelu_done, 1)
                        hold(act, weighted, n + 1)
                        for k in range(TOPK):
                            act.wait_ge(v_used, n * TOPK + (k + 1 - TOPK + V_CREDIT))
                            nc.scalar.activation(diag[:, k, :], ident, ACT.Copy, scale=weight[:, h % 2, k:k + 1]
                                                 ).then_inc(diag_set, 1)

                empty(act, "norm", 1 if layer == 0 else 3, KT - 1)
                empty(act, "norm", 1 if layer == 0 else 3, KT - 2)
                nc.scalar.activation(x_cur, hT[:, :, 0:P], ACT.Copy).then_inc(x_cur_set, 1)
                scores_out(layer * TT * PH, 0)
                softmax_exp(layer * TT * PH)
                with act.Fori(0, TT - 1) as b:
                    token_block(b + layer * TT, b, True)
                token_block(TT - 1 + layer * TT, TT - 1, False)

            peer(0, ACT.Gelu)
            squares(2, lambda t: act.wait_ge(x_added, 1 + TT), x_tiles)
            squares(3, lambda t: act.wait_ge(x_new, t + 1), x_tiles)
            no_shift = lambda k: 0.0
            transposed(2, lambda k: col("g_mix_2", k), no_shift)
            for j in range(4):
                if j >= 2:
                    empty(act, "cv", j - 2)
                copy_out(c_gate[:, j % 2, :], "cc", j).then_inc(emptied["A"], 1)
            act.wait_ge(pads_zeroed, 4)
            for g in range(4):
                if g >= 2:
                    act.wait_ge(pooled, g - 1)
                copy_out(u_pad[g % 2][:, PAD:PAD + L], "pu", g).then_inc(emptied["A"], 1)
            for g in range(4):
                copy_out(yT2[:, 4 + g, :], "py", g, scale=col("pool_scale_2", g)).then_inc(emptied["A"], 1)
            squares(4, lambda t: added("wo2", t), x_tiles)
            transposed(3, lambda k: col("g_ffn_2", k), no_shift)
            for g in range(4):
                copy_out(kT[:, 4 * g:4 * g + 4, :], "kT", 1, g).then_inc(emptied["A"], 1)
            peer(1, ACT.Gelu_apprx_tanh)
            squares(5, lambda t: act.wait_ge(x_added, 1 + 2 * TT), x_tiles)
            transposed(4, lambda k: col("g_ple_2", k), no_shift)
            for k in range(2):
                copy_out(pT[:, k, :], "pT", k).then_inc(emptied["A"], 1)
            for u in range(2 * TT):
                t, n = u % TT, u // TT
                if u >= 2:
                    empty(act, "pp", (u - 2) % TT, (u - 2) // TT)
                o = full(act, "gate", t, n)
                nc.scalar.activation(ple_gate[:, u % 2, :], o[:, :], ACT.Sigmoid).then_inc(emptied["A"], 1)
            squares(6, lambda t: added("pp", t), x_tiles)

        @block.vector
        def _(dve):
            V = nc.vector
            dve.sem_inc(u_used, SLOTS)
            dve.sem_inc(routed, 2)
            dve.sem_inc(x_added, 1)

            def scale_rows(r, tiles):
                n = len(tiles)
                dve.wait_ge(sumsq, ROWS_UPTO[r])
                V.tensor_scalar(stat[:, 1, 0:n], stat[:, 0, 0:n], 1.0 / D, EPS, ALU.mult, ALU.add).then_inc(meansq, 1)
                dve.wait_ge(root, r + 1)
                V.reciprocal(stat[:, 3, 0:n], stat[:, 2, 0:n]).then_inc(rstd, 1)
                dve.wait_ge(rstd, r + 1)
                for t, (src, dst) in enumerate(tiles):
                    V.tensor_scalar(dst, src, stat[:, 3, t:t + 1], None, ALU.mult).then_inc(rows_scaled, 1)

            x_tiles = [(X[:, t, :], xr[:, t, :]) for t in range(TT)]

            def transposed(i, gains, shifts):
                for k in range(1, KT, 2):
                    o = full(dve, "norm", i, k)
                    if shifts is None:
                        ins = V.tensor_scalar(hT[:, k, :], o[:, :], gains(k), None, ALU.mult)
                    else:
                        ins = V.tensor_scalar(hT[:, k, :], o[:, :], gains(k), shifts(k), ALU.mult, ALU.add)
                    ins.then_inc(emptied["D"], 1)

            def modulation(name, c, first_tile, first_col):
                o = full(dve, name, c)
                V.tensor_tensor(mod[:, first_tile + 4 * c:first_tile + 4 * c + 4, :],
                                o[:, 0:8].rearrange("p (j v) -> p j v", v=2),
                                col("b_mod", first_col + 4 * c, 4).unsqueeze(2).to_broadcast([P, 4, 2]),
                                ALU.add).then_inc(emptied["D"], 1)

            def norm_gain(g, tile, v, name):
                V.scalar_tensor_tensor(gain[:, g, :], mod[:, tile:tile + KT, v], 1.0, col(name, 0, KT),
                                       ALU.add, ALU.mult).then_inc(gains_done, 1)

            o = full(dve, "cols")
            V.tensor_copy(cols[:, :], o[:, 0:N_VEC]).then_inc(emptied["D"], 1)
            scale_rows(0, x_tiles + [(xc[:, t, :], xc[:, t, :]) for t in range(TC)])

            dve.wait_ge(lg_in, 32)
            V.tensor_scalar(lg[:, 2, :], lg[:, 0, :], 0.0, None, ALU.min).then_inc(lg_step, 1)
            dve.wait_ge(lg_act, 3)
            dve.wait_ge(lg_step, 1)
            V.tensor_tensor(lg[:, 3, :], lg[:, 2, :], lg[:, 1, :], ALU.subtract).then_inc(lg_step, 1)
            dve.wait_ge(lg_step, 2)
            V.tensor_scalar(lg[:, 1, :], lg[:, 3, :], -1.0, None, ALU.mult).then_inc(lg_step, 1)
            V.tensor_scalar(lg[:, 2, :], lg[:, 3, :], float(L + LC), None, ALU.mult).then_inc(lg_step, 1)

            for c in range(4):
                modulation("mod", c, 0, 0)
            empty(dve, "mod", 3)
            norm_gain(0, KT, 0, "norm1_w")
            norm_gain(1, KT, 1, "norm1_w")
            dve.wait_ge(gains_done, 2)
            transposed(0, lambda k: gain[:, 0, k:k + 1], lambda k: mod[:, k, 0:1])
            for k in range(1, KT, 2):
                o = full(dve, "normc", k)
                V.tensor_scalar(hTc[:, k, :], o[:, 0:LC], gain[:, 1, k:k + 1], mod[:, k, 1:2], ALU.mult, ALU.add
                                ).then_inc(emptied["D"], 1)

            def rope(name, first):
                for h in range(HEADS):
                    x = (rkT if name == "rk" else rqT)[:, h, :]
                    tmp = rot_tmp[:, h % 2, :]
                    o = full(dve, name + "rot", h)
                    V.tensor_tensor(tmp, o[:, :], sin_t, ALU.mult).then_inc(emptied["D"], 1)
                    V.tensor_tensor(x, x, cos_t, ALU.mult).then_inc(rotating, 1)
                    dve.wait_ge(rotating, first + h + 1)
                    empty(dve, name + "rot", h)
                    V.tensor_tensor(x, x, tmp, ALU.add).then_inc(roped, 1)

            rope("rk", 0)
            rope("rq", HEADS)

            def masks(h):
                m, c = mask_m[h % 2], mask_c[h % 2]
                dve.wait_ge(exps, 4 * h + 4)
                V.tensor_tensor(m[:, 0, :], m[:, 0, :], m[:, 1, :], ALU.mult).then_inc(mask_step, 1)
                V.tensor_tensor(c[:, 0, :], c[:, 0, :], c[:, 1, :], ALU.add).then_inc(mask_step, 1)
                dve.wait_ge(mask_step, 3 * h + 1)
                V.tensor_tensor(m[:, 0, 384:512], m[:, 0, 384:512], const[:, C_TWICE:C_TWICE + P], ALU.mult).then_inc(mask_step, 1)

            masks(0)
            for h in range(HEADS):
                if h >= 1:
                    full(dve, "ro", h - 1)
                dve.wait_ge(mask_step, 3 * h + 3)
                for j in range(TT + TC):
                    o = full(dve, "rs", h, j)
                    if j < TT:
                        m = mask_m[h % 2][:, 0, 384 - P * j:384 - P * j + L]
                    else:
                        m = mask_c[h % 2][:, 0, P * (TC - 1 - (j - TT)):P * (TC - 1 - (j - TT)) + L]
                    V.tensor_tensor(r_p[:, j, :], o[:, :], m, ALU.mult).then_inc(emptied["D"], 1)
                if h + 1 < HEADS:
                    masks(h + 1)

            empty(dve, "rs", HEADS - 1, TT + TC - 1)
            V.memset(lrT, 1.0).then_inc(ones_set, 1)
            for t in range(1, TT, 2):
                o = full(dve, "gv", t)
                V.tensor_copy(gv[:, t, :], o[:, :]).then_inc(emptied["D"], 1)
            o = full(dve, "gvc", 1)
            V.tensor_copy(gvc[:, 1, :], o[:, :]).then_inc(emptied["D"], 1)
            for t in range(TT + TC):
                o = full(dve, "la", t)
                dve.wait_ge(la_act, 3 * t + 1)
                V.tensor_scalar(la[:, t, :], o[:, :], 0.0, 1.0 / GATE_NORM, ALU.min, ALU.mult).then_inc(la_min, 1)
                dve.wait_ge(la_min, t + 1)
                dve.wait_ge(la_act, 3 * (t + 1))
                V.scalar_tensor_tensor(la[:, t, :], la_tmp[:, t % 2, :], -1.0 / GATE_NORM, la[:, t, :], ALU.mult, ALU.add
                                       ).then_inc(emptied["D"], 1)
            for p in range(PAIRS):
                for d in (FWD, BWD):
                    i = 2 * p + d
                    mid, last = (P // 2 - 1, P - 1) if d == FWD else (P // 2, 0)
                    o = full(dve, "cum", p, d)
                    if i >= 1:
                        full(dve, "kdT", (i - 1) // 2, (i - 1) % 2)
                    V.tensor_copy(G, o[:, :]).then_inc(emptied["D"], 1)
                    empty(dve, "cum", p, d)
                    g3 = G.rearrange("p (c t) -> p c t", t=P)
                    for dst, at_t in ((G_mid, mid), (G_last, last)):
                        V.tensor_tensor(dst.rearrange("p (c t) -> p c t", t=P), g3,
                                        g3[:, :, at_t:at_t + 1].to_broadcast([P, TT, P]), ALU.subtract).then_inc(g_sub, 1)
                    empty(dve, "cumc", p, d)
                    V.tensor_tensor(kc_exp, kc_exp, gkTc[:, p, :], ALU.mult).then_inc(kc_mul, 1)
                    dve.wait_ge(g_exp, 5 * (i + 1))
                    V.tensor_tensor(G_last, G_last, gkT[:, p, :], ALU.mult).then_inc(g_mul, 1)
                    V.tensor_tensor(q_in[:, i, :], G_mid, gqT[:, p, :], ALU.mult).then_inc(g_mul, 1)
                    V.tensor_tensor(k_in[:, i, :], G_neg, gkT[:, p, :], ALU.mult).then_inc(g_mul, 1)
                    V.tensor_tensor(q_st[:, i, :], G, gqT[:, p, :], ALU.mult).then_inc(g_mul, 1)
                    c = 0 if d == FWD else TT - 1
                    o = full(dve, "s0", p, d)
                    V.tensor_copy(state[0:64, i, c, :], o[0:64, 0:DV]).then_inc(state_half, 1)
                    V.tensor_copy(state[64:128, i, c, :], o[64:128, DV:2 * DV]).then_inc(emptied["D"], 1)
                    for s in range(TT - 1):
                        to = c + 1 if d == FWD else c - 1
                        o = full(dve, "up", p, d, s)
                        dve.wait_ge(state_half, i * TT + s + 1)
                        if s == 0:
                            empty(dve, "s0", p, d)
                        else:
                            empty(dve, "up", p, d, s - 1)
                        for half, done in ((0, state_half), (1, emptied["D"])):
                            r = slice(64 * half, 64 * half + 64)
                            V.scalar_tensor_tensor(state[r, i, to, :], state[r, i, c, :], chunk_dec[r, i, c:c + 1],
                                                   o[r, half * DV:(half + 1) * DV], ALU.mult, ALU.add).then_inc(done, 1)
                        c = to

            empty(dve, "go", TT - 1, 1)
            steps = 0
            for u in range(2 * TT):
                src = (o_ret if u < TT else o_gla)[:, u % TT, :]
                V.tensor_tensor(sq_tmp[:, u % 2, :], src, src, ALU.mult).then_inc(head_step, 1)
                dve.wait_ge(head_step, 2 * u + 1)
                V.tensor_reduce(hstat[:, 0, 4 * u:4 * u + 4], sq_tmp[:, u % 2, :].rearrange("p (h v) -> p h v", v=DV),
                                AX_X, ALU.add).then_inc(head_step, 1)
            dve.wait_ge(head_step, 4 * TT)
            V.tensor_scalar(hstat[:, 1, :], hstat[:, 0, :], 1.0 / DV, EPS, ALU.mult, ALU.add).then_inc(head_step, 1)
            dve.wait_ge(head_root, 1)
            V.reciprocal(hstat[:, 3, :], hstat[:, 2, :]).then_inc(head_step, 1)
            dve.wait_ge(head_step, 4 * TT + 2)
            for u in range(2 * TT):
                src = (o_ret if u < TT else o_gla)[:, u % TT, :]
                s3 = src.rearrange("p (h v) -> p h v", v=DV)
                V.tensor_tensor(s3, s3, hstat[:, 3, 4 * u:4 * u + 4].unsqueeze(2).to_broadcast([P, HEADS, DV]), ALU.mult
                                ).then_inc(y_step, 1)
                dve.wait_ge(y_step, u + 1)
                empty(dve, "rg" if u < TT else "gg", u % TT)
                V.tensor_tensor(src, src, gate_tmp[:, u % 2, :], ALU.mult).then_inc(y_done, 1)
            dve.wait_ge(row_a_in, 16)
            for n in range(2):
                o, r = full(dve, "g1", n), row_a[:, n * CW:(n + 1) * CW]
                V.tensor_tensor(r, o[:, :], r, ALU.add).then_inc(emptied["D"], 1)
            for k in range(1, KT, 2):
                o = full(dve, "yT", k)
                V.tensor_copy(yT[:, k, :], o[:, :]).then_inc(emptied["D"], 1)
            empty(dve, "g1", 1)
            for n in range(2):
                for t in range(TT):
                    o, x = full(dve, "wo", t, n), X[:, t, n * CW:(n + 1) * CW]
                    V.tensor_tensor(o[:, :], o[:, :], row_a[:, n * CW:(n + 1) * CW], ALU.mult).then_inc(wo_mul, 1)
                    dve.wait_ge(wo_mul, n * TT + t + 1)
                    V.tensor_tensor(x, o[:, :], x, ALU.add).then_inc(emptied["D"], 1)
            empty(dve, "wo", TT - 1, 1)
            scale_rows(1, x_tiles)
            for c in range(4):
                modulation("mod2", c, 16, 24)
            dve.wait_ge(row_b_in, 16)
            for n in range(2):
                o, r = full(dve, "g2", n), row_b[:, n * CW:(n + 1) * CW]
                V.tensor_tensor(r, o[:, :], r, ALU.add).then_inc(emptied["D"], 1)
            empty(dve, "mod2", 3)
            norm_gain(2, 24, 0, "norm2_w")
            dve.wait_ge(gains_done, 3)
            transposed(1, lambda k: gain[:, 2, k:k + 1], lambda k: mod[:, 16 + k, 0:1])

            def peer(layer):
                def route(n, h):
                    step = [0]

                    def then(ins):
                        step[0] += 1
                        ins.then_inc(route_step, 1)

                    def after(k):
                        dve.wait_ge(route_step, k)

                    hold(dve, s_copied, n + 1)
                    hold(dve, v_used, n * TOPK + (V_CREDIT - (IDX_SLOTS - 1) * TOPK))
                    dve.sem_clear(route_step)
                    s = score[:, h % 2, :, :]
                    for half in range(2):
                        then(V.max(top1[:, half, 0:8], s[:, half, :]))
                    for half in range(2):
                        after(1 + half)
                        then(V.match_replace(score_rest[:, half, :], top1[:, half, 0:8], s[:, half, :], LOWEST))
                    for half in range(2):
                        then(V.max_index(key_i[:, half, 0:8], top1[:, half, 0:8], s[:, half, :]))
                    for half in range(2):
                        after(3 + half)
                        then(V.max(top1[:, half, 8:16], score_rest[:, half, :]))
                    after(8)
                    then(V.tensor_tensor(cand, top1[:, 0, :].unsqueeze(2).to_broadcast([P, TOPK, TOPK]),
                                         top1[:, 1, :].unsqueeze(1).to_broadcast([P, TOPK, TOPK]), ALU.add))
                    for half in range(2):
                        then(V.max_index(key_i[:, half, 8:16], top1[:, half, 8:16], score_rest[:, half, :]))
                    after(9)
                    flat = cand.rearrange("p a b -> p (a b)")
                    then(V.max(top2[:, 0:8], flat))
                    after(11)
                    then(V.tensor_copy(key_f.rearrange("p a b -> p (a b)"), key_i[:, :, :].rearrange("p a b -> p (a b)")))
                    after(12)
                    then(V.match_replace(cand_rest, top2[:, 0:8], flat, LOWEST))
                    then(V.max_index(pos_i[:, 0:8], top2[:, 0:8], flat))
                    after(14)
                    then(V.max(top2[:, 8:16], cand_rest))
                    then(V.tensor_scalar(neg_max, top2[:, 0:1], -1.0, None, ALU.mult))
                    after(17)
                    V.max_index(pos_i[:, 8:16], top2[:, 8:16], cand_rest).then_inc(topped, 1)
                    dve.wait_ge(topped, n + 1)
                    then(V.tensor_scalar(pos_ab[:, 0, :], pos_i[:, :], 4, None, ALU.logical_shift_right))
                    then(V.tensor_scalar(pos_ab[:, 1, :], pos_i[:, :], TOPK - 1, None, ALU.bitwise_and))
                    after(19)
                    hot = onehot.rearrange("p h k a -> p (h k) a")
                    then(V.tensor_tensor(hot, pos_ab[:, :, :].rearrange("p h k -> p (h k)").unsqueeze(2).to_broadcast([P, 2 * TOPK, TOPK]),
                                         const[:, C_IOTA:C_IOTA + TOPK].unsqueeze(1).to_broadcast([P, 2 * TOPK, TOPK]), ALU.is_equal))
                    after(20)
                    then(V.tensor_tensor(onehot, onehot, key_f.unsqueeze(2).to_broadcast([P, 2, TOPK, TOPK]), ALU.mult))
                    after(21)
                    then(V.tensor_reduce(picked.rearrange("p h k -> p (h k)"), hot, AX_X, ALU.add))
                    after(22)
                    then(V.scalar_tensor_tensor(idx_f, picked[:, 0, :], float(NKEYS), picked[:, 1, :], ALU.mult, ALU.add))
                    after(23)
                    V.tensor_copy(idx[:, h % IDX_SLOTS, :], idx_f).then_inc(routed, 1)

                def softmax(n, h):
                    hold(dve, exp_done, n + 1)
                    V.reciprocal(exp_inv, exp_sum).then_inc(route_step, 1)
                    dve.wait_ge(route_step, 24)
                    V.tensor_scalar(gate[:, h % 2, :], exp_s, exp_inv, None, ALU.mult).then_inc(route_step, 1)
                    dve.wait_ge(route_step, 25)

                def dot_products(n, h):
                    for k in range(TOPK):
                        dve.wait_ge(u_loaded[k % SLOTS], n * (16 * TOPK // SLOTS) + 16 * (k // SLOTS + 1))
                        V.tensor_tensor_reduce(u_rows[:, k % SLOTS, :], u_rows[:, k % SLOTS, :], xn, 1.0, 0.0, ALU.mult,
                                               ALU.add, dots[:, h % 2, k:k + 1]).then_inc(u_used, 1)

                def weights(n, h):
                    dve.wait_ge(gelu_done, n + 1)
                    V.tensor_tensor(weight[:, h % 2, :], gelu[:, h % 2, :], gate[:, h % 2, :], ALU.mult).then_inc(weighted, 1)

                def add_output(it, b):
                    dve.wait_ge(v_used, it * (PH * TOPK) + (PH * TOPK + V_CREDIT))
                    if layer == 0:
                        V.tensor_tensor(peer_sum, peer_sum, row_b[:, :], ALU.mult).then_inc(sum_scaled, 1)
                        dve.wait_ge(sum_scaled, it + 1)
                    x = X[:, bass.ds(b, 1), :].rearrange("p a d -> p (a d)")
                    V.tensor_tensor(x, peer_sum, x, ALU.add).then_inc(x_added, 1)

                def token_block(it, b, more):
                    hold(dve, xn_ready, it + 1)
                    for h in range(PH):
                        n = it * PH + h
                        if h < PH - 1 or more:
                            route(n + 1, (h + 1) % PH)
                        dot_products(n, h)
                        if h < PH - 1 or more:
                            softmax(n + 1, (h + 1) % PH)
                        weights(n, h)
                    add_output(it, b)

                n0 = layer * TT * PH
                route(n0, 0)
                softmax(n0, 0)
                with dve.Fori(0, TT - 1) as b:
                    token_block(b + layer * TT, b, True)
                token_block(TT - 1 + layer * TT, TT - 1, False)

            empty(dve, "g2", 1)
            peer(0)
            dve.wait_ge(x_added, 1 + TT)
            scale_rows(2, x_tiles)
            dve.wait_ge(row_a_in, 32)
            dve.wait_ge(rows_scaled, ROWS_UPTO[2])
            for t in range(TT):
                V.tensor_tensor(X[:, t, :], xr[:, t, :], row_a[:, :], ALU.mult).then_inc(x_new, 1)
            dve.wait_ge(x_new, TT)
            scale_rows(3, x_tiles)
            transposed(2, lambda k: col("g_mix_2", k), None)

            steps = 0
            dve.wait_ge(pads_zeroed, 4)
            for j in range(4):
                z, y = z_pad[j % 2], yT2[:, j, :]
                empty(dve, "cc", j)
                o = full(dve, "cv", j)
                V.tensor_tensor(z[:, 1:1 + L], o[:, :], c_gate[:, j % 2, :], ALU.mult).then_inc(emptied["D"], 1)
                empty(dve, "cv", j)
                V.tensor_scalar(y, z[:, 0:L], col("conv_w_2", j), None, ALU.mult).then_inc(conv_step, 1)
                for tap in (1, 2):
                    dve.wait_ge(conv_step, 3 * j + tap)
                    V.scalar_tensor_tensor(y, z[:, tap:tap + L], col("conv_w_2", 4 * tap + j), y, ALU.mult, ALU.add
                                           ).then_inc(conv_step, 1)
                dve.wait_ge(conv_step, 3 * j + 3)
                o = full(dve, "cb", j)
                V.tensor_tensor(y, o[:, :], y, ALU.mult).then_inc(emptied["D"], 1)
            dve.wait_ge(inv_in, 16)
            steps = 0
            for g, w in enumerate(WINDOWS):
                empty(dve, "pu", g)
                src, n, span, dst = u_pad[g % 2], L + 2 * PAD, 1, 0
                while span < w:
                    n -= span
                    V.tensor_tensor(win[dst][:, 0:n], src[:, 0:n], src[:, span:span + n], ALU.add).then_inc(pool_step, 1)
                    steps += 1
                    dve.wait_ge(pool_step, steps)
                    src, dst, span = win[dst], 1 - dst, 2 * span
                y = yT2[:, 4 + g, :]
                V.tensor_tensor(y, src[:, PAD - w // 2:PAD - w // 2 + L], inv_cnt[:, g, :], ALU.mult).then_inc(pool_step, 1)
                steps += 1
                dve.wait_ge(pool_step, steps)
                V.tensor_tensor(y, y, u_pad[g % 2][:, PAD:PAD + L], ALU.subtract).then_inc(pooled, 1)
            for n in range(2):
                for t in range(TT):
                    o, x = full(dve, "wo2", t, n), X[:, t, n * CW:(n + 1) * CW]
                    V.tensor_tensor(x, o[:, :], x, ALU.add).then_inc(emptied["D"], 1)
            empty(dve, "wo2", TT - 1, 1)
            scale_rows(4, x_tiles)
            transposed(3, lambda k: col("g_ffn_2", k), None)
            peer(1)
            dve.wait_ge(x_added, 1 + 2 * TT)
            scale_rows(5, x_tiles)
            transposed(4, lambda k: col("g_ple_2", k), None)
            for u in range(2 * TT):
                t, n = u % TT, u // TT
                empty(dve, "gate", t, n)
                o, x = full(dve, "pp", t, n), X[:, t, n * CW:(n + 1) * CW]
                V.tensor_tensor(o[:, :], o[:, :], ple_gate[:, u % 2, :], ALU.mult).then_inc(ple_mul, 1)
                dve.wait_ge(ple_mul, u + 1)
                V.tensor_tensor(x, o[:, :], x, ALU.add).then_inc(emptied["D"], 1)
            empty(dve, "pp", TT - 1, 1)
            scale_rows(6, x_tiles)
            dve.wait_ge(row_b_in, 32)
            dve.wait_ge(rows_scaled, ROWS_UPTO[6])
            for t in range(TT):
                V.tensor_tensor(xr[:, t, :], xr[:, t, :], row_b[:, :], ALU.mult).then_inc(out_ready, 1)


_INPUTS = ["x", "c", "ctx", "c_ctx", "w_mod", "b_mod", "norm1_w", "norm2_w", "w_in", "ret_decay_f", "ret_decay_b",
           "gla_gk_up_f", "gla_gk_bias_f", "gla_gk_up_b", "gla_gk_bias_b", "w_out", "peer_w_q", "peer_k1", "peer_k2",
           "peer_down", "peer_up", "norm_f_w", "p_2", "g_mix_2", "w_in_2", "conv_w_2", "pool_w_2", "pool_scale_2", "w_o_2",
           "g_ffn_2", "w_q_2", "sub_keys_2", "expert_u_2", "expert_v_2", "g_ple_2", "w_ple_gate_2", "w_ple_proj_2",
           "g_final_2"]


def kernel(**inputs):
    import concourse.bacc as bacc
    from concourse.bass_utils import run_bass_kernel_spmd

    nc = bacc.Bacc("TRN2", target_bir_lowering=False, num_devices=1)
    arrays = {f"in_{n}": np.ascontiguousarray(inputs[n]) for n in _INPUTS}
    arrays["shape_tables"], arrays["inverse_counts"] = shape_constants()
    aps = {n: nc.dram_tensor(n, v.shape, F32, kind="ExternalInput").ap() for n, v in arrays.items()}
    out = nc.dram_tensor("out", (1, L, D), F32, kind="ExternalOutput").ap()
    build(nc, {n: aps[f"in_{n}"] for n in _INPUTS}, aps["shape_tables"], aps["inverse_counts"], out)
    r = run_bass_kernel_spmd(nc, [arrays], core_ids=[0])
    return r.results[0]["out"]
```

```python
import numpy as np
from contextlib import ExitStack

import concourse.bass as bass
from concourse import mybir

P = 128
F32 = mybir.dt.float32
U32 = mybir.dt.uint32
ALU = mybir.AluOpType
ACT = mybir.ActivationFunctionType
AX_X = mybir.AxisListType.X

D = 1024
KT = D // P
L = 512
TT = L // P
LC = 256
TC = LC // P
HEADS = 4
DV = 128
RET_DK = 128
GLA_DK = 64
PAIRS = 2
RANK = 16
GATE_NORM = 16.0
EPS = 1e-6
GRID_W = 64
CW = 512
RING = 3
FWD, BWD = 0, 1
PH = 8
TOPK = 16
NKEYS = 128
PQ = PH * 2 * P
SLOTS = 8
IDX_SLOTS = 4
V_CREDIT = 64
WINDOWS = (2, 4, 8, 16)
PAD = 8
LOWEST = -3.0e38

WIDE = 384 + L + 256
C_IDENT, C_COS, C_SIN = 0, 128, 640
C_AHEAD, C_BEHIND = 1152, 1152 + WIDE
C_TRI = C_BEHIND + 384 + L
TRI_PREFIX, TRI_SUFFIX, TRI_AFTER, TRI_BEFORE, TRI_ONES = range(5)
C_ROT = C_TRI + 5 * 128
C_TWICE = C_ROT + 128
C_IOTA = C_TWICE + 128
N_CONST = C_IOTA + 16

VEC = [("c", 8), ("c_ctx", 8), ("b_mod", 48), ("norm1_w", 8), ("norm2_w", 8), ("g_mix_2", 8),
       ("g_ffn_2", 8), ("g_ple_2", 8), ("conv_w_2", 12), ("pool_scale_2", 4)]
VEC_AT = {}
for _name, _rows in VEC:
    VEC_AT[_name] = sum(r for n, r in VEC[:len(VEC_AT)])
N_VEC = sum(r for _, r in VEC)

W_RQ, W_RK, W_RV, W_RG, W_GQK, W_GV, W_GG, W_LR = 0, 512, 1024, 1536, 2048, 2560, 3072, 3584

CHUNKS = ([("w_mod", CW * i) for i in range(4)]
          + [("w_in", W_RK), ("w_mod", CW * 6), ("w_in", W_RV), ("w_mod", CW * 7), ("w_in", W_RQ), ("w_mod", CW * 8),
             ("w_in", W_GQK), ("w_mod", CW * 9), ("w_in", W_GV), ("w_mod", CW * 4), ("w_in", W_RG), ("w_mod", CW * 5),
             ("w_in", W_GG), ("w_mod", CW * 10), ("w_out", 0), ("w_mod", CW * 11), ("w_out", CW)]
          + [("w_in_2", CW * i) for i in range(4)] + [("w_o_2", 0), ("w_o_2", CW), ("keys_2", 0)]
          + [("w_ple_gate_2", 0), ("w_ple_gate_2", CW), ("w_ple_proj_2", 0)])


CHUNK_LAST_JOB = {("w_in", W_RK): ("rkc", 1), ("w_in", W_RV): ("rvc", TC - 1), ("w_in", W_RQ): ("rq", HEADS - 1),
                  ("w_in", W_GQK): ("gkc",), ("w_in", W_GV): ("gvc", TC - 1), ("w_in", W_RG): ("rg", 3),
                  ("w_in", W_GG): ("gg", TT - 1), ("keys_2", 0): ("kT", 1, 3),
                  ("w_in_2", CW * 3): ("pu", 3), ("w_ple_gate_2", 0): ("pp", TT - 1, 0)}
COLUMN_CHUNKS = (0, 1, 2, 3, 6, 7, 8, 9)
CHUNK_LAST_JOB.update({("w_mod", CW * i): ("mod", i) for i in COLUMN_CHUNKS})
for _n in range(2):
    CHUNK_LAST_JOB.update({("w_mod", CW * (4 + _n)): ("g1", _n), ("w_mod", CW * (10 + _n)): ("g2", _n),
                           ("w_out", CW * _n): ("wo", TT - 1, _n), ("w_o_2", CW * _n): ("wo2", TT - 1, _n)})
CHUNK_LAST_JOB.update({("w_in_2", CW * i): ("cb", 3) for i in range(3)})


def chunk_number(name, col=0):
    return CHUNKS.index((name, col))


def shape_constants():
    p = np.arange(P)[:, None].astype(np.float64)
    c = np.zeros((P, N_CONST), np.float32)
    c[:, C_IDENT:C_IDENT + P] = np.eye(P)
    n_freq = RET_DK // 4
    inv = np.float32(10000.0) ** (-np.arange(n_freq, dtype=np.float32) / np.float32(n_freq))
    t = np.arange(L)
    ang = np.concatenate([(t // GRID_W).astype(np.float32)[:, None] * inv,
                          (t % GRID_W).astype(np.float32)[:, None] * inv], axis=1).astype(np.float64)
    cos, sin = np.cos(ang).T, np.sin(ang).T
    c[:, C_COS:C_COS + L] = np.concatenate([cos, cos])
    c[:, C_SIN:C_SIN + L] = np.concatenate([-sin, sin])
    m = np.arange(WIDE)[None, :]
    c[:, C_AHEAD:C_AHEAD + WIDE] = np.maximum(m - 384 - p, 0)
    c[:, C_BEHIND:C_BEHIND + 384 + L] = np.maximum(p + 384 - m, 0)[:, :384 + L]
    q = np.arange(P)[None, :]
    for i, tri in enumerate([p <= q, p >= q, p > q, p < q, p >= 0]):
        c[:, C_TRI + i * P:C_TRI + (i + 1) * P] = tri
    c[:, C_ROT:C_ROT + P] = (p == (q + 64) % P)
    c[:, C_TWICE:C_TWICE + P] = 1 + np.eye(P)
    c[:, C_IOTA:C_IOTA + 16] = np.arange(16)
    counts = np.zeros((4, L), np.float64)
    for g, w in enumerate(WINDOWS):
        counts[g] = np.clip(t + w // 2, 0, L) - np.clip(t - w // 2, 0, L)
    return c, (1.0 / counts).astype(np.float32)


class PsumJobs:

    def __init__(self):
        self.names, self.who, self.rank, self.total = [], [], [], {"A": 0, "D": 0}

    def add(self, name, who):
        self.names.append(name)
        self.who.append(who)
        self.total[who] += 1
        self.rank.append(self.total[who])

    def number(self, *name):
        return self.names.index(name)

    def upto(self, n):
        return {w: sum(x == w for x in self.who[:n]) for w in "AD"}


def plan_jobs():
    jobs = PsumJobs()
    alternate = lambda i: "AD"[i % 2]
    jobs.add(("cols",), "D")
    for c in range(4):
        jobs.add(("mod", c), "D")
        if c >= 1:
            jobs.add(("modT", c - 1), "D")
    jobs.add(("modT", 3), "D")
    for k in range(KT):
        jobs.add(("norm", 0, k), alternate(k))
    for k in range(KT):
        jobs.add(("normc", k), alternate(k))
    for h in range(HEADS):
        jobs.add(("rk", h), "A")
    for h in range(HEADS):
        jobs.add(("rkrot", h), "D")
    for g in range(2):
        jobs.add(("rkc", g), "A")
    jobs.add(("mod", 6), "D")
    for t in range(TT):
        jobs.add(("rv", t), "A")
    for t in range(TC):
        jobs.add(("rvc", t), "A")
    jobs.add(("modT", 6), "D")
    jobs.add(("mod", 7), "D")
    for h in range(HEADS):
        jobs.add(("rq", h), "A")
    for h in range(HEADS):
        jobs.add(("rqrot", h), "D")
    jobs.add(("modT", 7), "D")
    jobs.add(("mod", 8), "D")
    for h in range(HEADS):
        for j in range(TT + TC):
            jobs.add(("rs", h, j), "D")
        jobs.add(("ro", h), "A")
    jobs.add(("modT", 8), "D")
    jobs.add(("lr",), "A")
    jobs.add(("lrc",), "A")
    for p in range(PAIRS):
        jobs.add(("gq", p), "A")
    for t in range(TT + TC):
        jobs.add(("la", t), "D")
    for p in range(PAIRS):
        jobs.add(("gk", p), "A")
    jobs.add(("gkc",), "A")
    jobs.add(("mod", 9), "D")
    for t in range(TT):
        jobs.add(("gv", t), alternate(t))
    for t in range(TC):
        jobs.add(("gvc", t), alternate(t))
    jobs.add(("modT", 9), "D")
    for p in range(PAIRS):
        for d in (FWD, BWD):
            jobs.add(("cum", p, d), "D")
            jobs.add(("cumc", p, d), "A")
            jobs.add(("rg", 2 * p + d), "A")
            jobs.add(("kcT", p, d), "A")
            jobs.add(("s0", p, d), "D")
            jobs.add(("kdT", p, d), "A")
            for s in range(TT - 1):
                jobs.add(("up", p, d, s), "D")
    for n in range(2):
        jobs.add(("g1", n), "D")
    for h in range(HEADS):
        for d in (FWD, BWD):
            jobs.add(("gs", h, d), "A")
    for c in range(TT):
        for odd in range(2):
            jobs.add(("go", c, odd), "A")
    for t in range(TT):
        jobs.add(("gg", t), "A")
    jobs.add(("g2", 0), "D")
    for k in range(KT):
        jobs.add(("yT", k), alternate(k))
    for t in range(TT):
        for n in range(2):
            jobs.add(("wo", t, n), "D")
    for g in range(4):
        jobs.add(("kT", 0, g), "A")
    jobs.add(("g2", 1), "D")
    for k in range(KT):
        jobs.add(("norm", 1, k), alternate(k))
    for k in range(KT):
        jobs.add(("norm", 2, k), alternate(k))
    for j in range(4):
        jobs.add(("cc", j), "A")
        jobs.add(("cv", j), "D")
        jobs.add(("cb", j), "D")
    for g in range(4):
        jobs.add(("pu", g), "A")
    for g in range(4):
        jobs.add(("py", g), "A")
    for n in range(2):
        for t in range(TT):
            jobs.add(("wo2", t, n), "D")
    for k in range(KT):
        jobs.add(("norm", 3, k), alternate(k))
    for g in range(4):
        jobs.add(("kT", 1, g), "A")
    for k in range(KT):
        jobs.add(("norm", 4, k), alternate(k))
    for k in range(2):
        jobs.add(("pT", k), "A")
    for n in range(2):
        for t in range(TT):
            jobs.add(("gate", t, n), "A")
            jobs.add(("pp", t, n), "D")
    return jobs


def build(nc, a, consts, inv_counts, out):
    jobs = plan_jobs()
    with ExitStack() as ctx:
        def sb(name, shape, dt=F32):
            return ctx.enter_context(nc.sbuf_tensor(name, shape, dt))

        def sem(name):
            return ctx.enter_context(nc.semaphore(name))

        X = sb("X", [P, TT, D])
        hT = sb("hT", [P, KT, L])
        ring = sb("ring", [P, RING * KT * CW])
        const = sb("const", [P, N_CONST])
        row_a = sb("row_a", [P, D])
        row_b = sb("row_b", [P, D])
        cols = sb("cols", [P, N_VEC])
        silu = sb("silu", [P, KT, 2])
        mod = sb("mod", [P, 6 * KT, 2])
        gain = sb("gain", [P, 3, KT])
        stat = sb("stat", [P, 4, 6])
        hstat = sb("hstat", [P, 4, 2 * TT * HEADS])
        lg = sb("lg", [P, 4, 8])
        chunk_dec = sb("chunk_dec", [P, 4, TT])
        SCR = 25600
        scr = sb("scr", [P, SCR])
        banks = ctx.enter_context(nc.psum_tensor("banks", [P, 8 * 512], F32))
        psum = [banks[:, 512 * i:512 * (i + 1)] for i in range(8)]
        xn = banks[:, 0:D]
        peer_sum = banks[:, D:2 * D]

        def at(base, off, *dims):
            n = int(np.prod(dims))
            v = base[:, off:off + n]
            if len(dims) == 1:
                return v
            if len(dims) == 2:
                return v.rearrange("p (a b) -> p a b", b=dims[1])
            return v.rearrange("p (a b c) -> p a b c", b=dims[1], c=dims[2])

        ident = const[:, C_IDENT:C_IDENT + P]
        cos_t, sin_t = const[:, C_COS:C_COS + L], const[:, C_SIN:C_SIN + L]
        rot = const[:, C_ROT:C_ROT + P]

        def tri(i):
            return const[:, C_TRI + i * P:C_TRI + (i + 1) * P]

        def chunk(n):
            return at(ring, (n % RING) * KT * CW, KT, CW)

        xr = at(scr, 0, TT, D)
        xc = at(scr, 8192, TC, D)
        vrows = at(scr, 21504, P)[0:N_VEC, :]
        rqT, rkT = at(scr, 0, HEADS, L), at(scr, 2048, HEADS, L)
        o_ret, o_gla = at(scr, 4096, TT, HEADS * DV), at(scr, 6144, TT, HEADS * DV)
        r_p = at(scr, 8192, TT + TC, L)
        rkTc, rv, rvc = at(scr, 11264, HEADS, LC), at(scr, 12288, TT, 512), at(scr, 14336, TC, 512)
        mask_m = [at(scr, 15360 + 3072 * i, 2, 384 + L) for i in range(2)]
        mask_c = [at(scr, 15360 + 3072 * i + 1792, 2, 640) for i in range(2)]
        rot_tmp = at(scr, 8192, 2, L)
        w_lr = at(scr, 22528, KT, 64)
        gk_up = at(scr, 22016, 512)[0:64, :]
        hTc = at(scr, 23040, KT, LC)
        q_in, k_in = at(scr, 0, 4, L), at(scr, 2048, 4, L)
        gqT, gkT, gkTc = at(scr, 8192, PAIRS, L), at(scr, 9216, PAIRS, L), at(scr, 10240, PAIRS, LC)
        gv, gvc = at(scr, 10752, TT, 512), at(scr, 12800, TC, 512)
        la = at(scr, 13824, TT + TC, 512)
        q_st = at(scr, 16896, 4, L)
        kdT = at(scr, 18944, 4, TT, P)
        state = at(scr, 20992, 4, TT, DV)
        g_p = [at(scr, 13824 + 512 * i, TT, P) for i in range(6)] + [at(scr, 8192 + 512 * i, TT, P) for i in range(2)]
        G = at(const, C_COS, L)
        G_mid, G_last, G_neg = at(const, C_AHEAD, L), at(const, C_AHEAD + 512, L), at(const, C_AHEAD + 1024, L)
        kc_exp, kcT = at(const, C_SIN, LC), at(const, C_SIN + LC, TC, P)
        lrT = at(scr, 18944, 768)[0:64, :]
        la_tmp = at(scr, 0, TT + TC, 512)
        ret_gate = at(scr, 23040, TT, 512)
        ret_sq = at(row_a, 0, 2, 512)
        gate_tmp = at(scr, 8192, 2, 512)
        yT = hT
        sq_tmp = at(scr, 9216, 2, 512)
        mod_rows = at(row_b, 0, 2, CW)[0:2]
        raw_keys = at(scr, 4096, PH, 2, P)
        u_rows = at(scr, 0, SLOTS, D)
        v_rows = at(ring, 0, SLOTS, D)
        w_q = at(scr, 8192, KT, PQ)
        diag = at(ring, 2 * KT * CW, TOPK, P)
        peer_qT = at(ring, 2 * KT * CW + 2048, 2, 2, P)
        x_cur = at(ring, 2 * KT * CW + 2560, KT, P)
        onehot = at(ring, 2 * KT * CW + 3584, 2, TOPK, TOPK)
        kT = at(const, C_AHEAD, 2 * PH, P)
        score = at(const, C_COS, 2, 2, NKEYS)
        score_rest = at(const, C_COS + 512, 2, NKEYS)
        cand = at(const, C_COS + 768, TOPK, TOPK)
        cand_rest = at(scr, 24576, TOPK * TOPK)
        o = 24832
        top1 = at(scr, o, 2, TOPK)
        key_f = at(scr, o + 32, 2, TOPK)
        top2 = at(scr, o + 64, TOPK)
        neg_max = at(scr, o + 80, 1)
        exp_s = at(scr, o + 96, TOPK)
        exp_sum = at(scr, o + 112, 1)
        exp_inv = at(scr, o + 113, 1)
        gate = at(scr, o + 128, 2, TOPK)
        picked = at(scr, o + 160, 2, TOPK)
        idx_f = at(scr, o + 192, TOPK)
        dots = at(scr, o + 208, 2, TOPK)
        gelu = at(scr, o + 240, 2, TOPK)
        weight = at(scr, o + 272, 2, TOPK)
        key_i = sb("key_i", [P, 2, TOPK], U32)
        pos_i = sb("pos_i", [P, TOPK], U32)
        pos_ab = sb("pos_ab", [P, 2, TOPK], U32)
        idx = sb("idx", [P, IDX_SLOTS, TOPK], U32)
        yT2 = at(scr, 4096, KT, L)
        z_pad = [at(scr, 514 * i, 514) for i in range(2)]
        u_pad = [at(scr, 1028 + 528 * i, 528) for i in range(2)]
        win = [at(scr, 2084 + 528 * i, 528) for i in range(2)]
        c_gate = at(const, C_COS, 2, L)
        inv_cnt = at(const, C_AHEAD, 4, L)
        pool_w = at(scr, 24576, 4, P)
        p_rows = at(scr, 8192, TT, 256)
        pT = at(scr, 9216, 2, L)
        ple_gate = at(scr, 10240, 2, CW)

        def col(name, k, n=1):
            return cols[:, VEC_AT[name] + k:VEC_AT[name] + k + n]

        bank_ready = sem("bank_ready")
        emptied = {"A": sem("act_emptied"), "D": sem("dve_emptied")}
        ident_in, const_in, vec_in, x_in, ctx_in, lg_in = sem("ident_in"), sem("const_in"), sem("vec_in"), sem("x_in"), sem("ctx_in"), sem("lg_in")
        lr_in, row_a_in, row_b_in = sem("lr_in"), sem("row_a_in"), sem("row_b_in")
        gap_zeroed = sem("gap_zeroed")
        chunk_in = [sem(f"chunk_in{i}") for i in range(RING)]
        w_q_in, inv_in, pool_w_in, p_in, out_done = (sem("w_q_in"), sem("inv_in"), sem("pool_w_in"), sem("p_in"),
                                                     sem("out_done"))
        silu_done, gains_done, keys_in = sem("silu_done"), sem("gains_done"), sem("keys_in")
        sumsq, meansq, root, rstd, rows_scaled = sem("sumsq"), sem("meansq"), sem("root"), sem("rstd"), sem("rows_scaled")
        x_new = sem("x_new")
        rotating, roped = sem("rotating"), sem("roped")
        lg_act, lg_step = sem("lg_act"), sem("lg_step")
        exps, mask_step = sem("exps"), sem("mask_step")
        ones_set = sem("ones_set")
        la_abs, la_exp, la_ln, la_min, la_done = sem("la_abs"), sem("la_exp"), sem("la_ln"), sem("la_min"), sem("la_done")
        rg_silu = sem("rg_silu")
        g_sub, g_exp, g_mul, kc_mul = sem("g_sub"), sem("g_exp"), sem("g_mul"), sem("kc_mul")
        state_half, p_masked = sem("state_half"), sem("p_masked")
        head_step, head_root, y_step, y_done = sem("head_step"), sem("head_root"), sem("y_step"), sem("y_done")
        wo_mul = sem("wo_mul")
        pads_zeroed, conv_step, pool_step, pooled = sem("pads_zeroed"), sem("conv_step"), sem("pool_step"), sem("pooled")
        ple_mul, out_ready = sem("ple_mul"), sem("out_ready")
        u_loaded = [sem(f"u_loaded{i}") for i in range(SLOTS)]
        v_loaded = [sem(f"v_loaded{i}") for i in range(SLOTS)]
        u_used = sem("u_used")
        v_used = sem("v_used")
        x_cur_set, xn_ready = sem("x_cur_set"), sem("xn_ready")
        q_done, q_copied, s_done, s_copied = sem("q_done"), sem("q_copied"), sem("s_done"), sem("s_copied")
        topped = sem("topped")
        exp_done, gelu_done, weighted = sem("exp_done"), sem("gelu_done"), sem("weighted")
        routed = sem("routed")
        diag_set = sem("diag_set")
        x_added = sem("x_added")
        route_step = sem("route_step")
        sum_scaled = sem("sum_scaled")
        passed = sem("passed")

        def full(eng, *name):
            n = jobs.number(*name)
            eng.wait_ge(bank_ready, n + 1)
            return psum[n % 8]

        def empty(eng, *name):
            n = jobs.number(*name)
            eng.wait_ge(emptied[jobs.who[n]], jobs.rank[n])

        def all_empty(eng, *last):
            for w, n in jobs.upto(jobs.number(*last) + 1).items():
                eng.wait_ge(emptied[w], n)

        def chunk_read(eng, n):
            eng.wait_ge(bank_ready, jobs.number(*CHUNK_LAST_JOB[CHUNKS[n]]) + 1)

        def hold(eng, s, value):
            eng.wait_ge(s, value)
            eng.sem_inc(passed, 1)

        NORM_TILES = [TT + TC, TT, TT, TT, TT, TT, TT]
        ROWS_UPTO = [sum(NORM_TILES[:i + 1]) for i in range(len(NORM_TILES))]
        NORM_R = {0: 0, 1: 1, 2: 3, 3: 4, 4: 5}

        block = ctx.enter_context(nc.Block())

        @block.sync
        def _(sp):
            wide = {"w_mod": a["w_mod"][0], "w_in": a["w_in"][0], "w_out": a["w_out"][0],
                    "w_in_2": a["w_in_2"][0], "w_o_2": a["w_o_2"][0], "w_ple_gate_2": a["w_ple_gate_2"][0]}

            def load_chunk(n):
                name, c0 = CHUNKS[n]
                if n >= RING:
                    chunk_read(sp, n - RING)
                s = chunk_in[n % RING]
                if name in wide:
                    sp.dma_start(chunk(n), wide[name].rearrange("(k p) n -> p k n", p=P)[:, :, c0:c0 + CW]).then_inc(s, 16)
                elif name == "keys_2":
                    raw = at(ring, (n % RING) * KT * CW, 2 * PH, P)
                    sp.dma_start(raw, a["sub_keys_2"][0].rearrange("h s n d -> n (h s) d")).then_inc(s, 16)
                else:
                    raw = at(ring, (n % RING) * KT * CW, 2, D)
                    sp.dma_start(raw, a["w_ple_proj_2"][0].rearrange("(k p) n -> p k n", p=P)).then_inc(s, 16)

            for name, rows in VEC:
                src = a[name]
                dims = " ".join("abcd"[:len(src.shape)])
                flat = src.rearrange(f"{dims} -> ({dims})") if len(src.shape) > 1 else src
                sp.dma_start(vrows[VEC_AT[name]:VEC_AT[name] + rows, :],
                             flat.rearrange("(r p) -> r p", p=P)).then_inc(vec_in, 16)
            sp.dma_start(ident, consts[:, C_IDENT:C_IDENT + P]).then_inc(ident_in, 16)
            for n in range(RING):
                load_chunk(n)
            sp.dma_start(X[:, :, :], a["x"][0].rearrange("(t p) d -> p t d", p=P)).then_inc(x_in, 16)
            sp.dma_start(xc, a["ctx"][0].rearrange("(t p) d -> p t d", p=P)).then_inc(ctx_in, 16)
            sp.dma_start(lg[:, 0, 0:4], a["ret_decay_f"][0].partition_broadcast(P)).then_inc(lg_in, 16)
            sp.dma_start(lg[:, 0, 4:8], a["ret_decay_b"][0].partition_broadcast(P)).then_inc(lg_in, 16)
            sp.dma_start(const[:, P:], consts[:, P:]).then_inc(const_in, 16)
            for n in range(3, 5):
                load_chunk(n)
            sp.wait_ge(gap_zeroed, 2)
            for d in (FWD, BWD):
                sp.dma_start(w_lr[:, :, 32 * d:32 * d + RANK],
                             a["w_in"][0].rearrange("(k p) n -> p k n", p=P)[:, :, W_LR + RANK * d:W_LR + RANK * (d + 1)]
                             ).then_inc(lr_in, 16)
                up, bias = (a["gla_gk_up_f"], a["gla_gk_bias_f"]) if d == FWD else (a["gla_gk_up_b"], a["gla_gk_bias_b"])
                sp.dma_start(gk_up[32 * d:32 * d + RANK, 256 * d:256 * (d + 1)], up[0]).then_inc(lr_in, 16)
                sp.dma_start(gk_up[32 * d + RANK:32 * d + RANK + 1, 256 * d:256 * (d + 1)], bias).then_inc(lr_in, 16)
            for n in range(5, chunk_number("w_in", W_RG) + 1):
                load_chunk(n)
            sp.wait_ge(head_step, 2 * TT)
            sp.dma_start(row_a[:, :], a["b_mod"][0, 2 * D:3 * D].partition_broadcast(P)).then_inc(row_a_in, 16)
            full(sp, "modT", 9)
            sp.dma_start(row_b[:, :], a["b_mod"][0, 5 * D:6 * D].partition_broadcast(P)).then_inc(row_b_in, 16)
            for n in range(chunk_number("w_mod", CW * 5), chunk_number("w_out", CW) + 1):
                load_chunk(n)
            full(sp, "yT", KT - 1)
            sp.dma_start(raw_keys[:, :, 0, :], a["peer_k1"][0].rearrange("h n d -> n h d")).then_inc(keys_in, 16)
            sp.dma_start(raw_keys[:, :, 1, :], a["peer_k2"][0].rearrange("h n d -> n h d")).then_inc(keys_in, 16)
            sp.dma_start(w_q, a["peer_w_q"][0].rearrange("(k p) n -> p k n", p=P)).then_inc(w_q_in, 16)
            all_empty(sp, "wo", TT - 1, 1)
            sp.dma_start(row_a[:, :], a["norm_f_w"].partition_broadcast(P)).then_inc(row_a_in, 16)

            sp.wait_ge(q_done, TT * PH)
            sp.dma_start(w_q, a["w_q_2"][0].rearrange("(k p) n -> p k n", p=P)).then_inc(w_q_in, 16)
            sp.wait_ge(x_added, 1 + TT)
            sp.dma_start(row_b[:, :], a["g_final_2"].partition_broadcast(P)).then_inc(row_b_in, 16)
            sp.dma_start(inv_cnt, inv_counts.partition_broadcast(P)).then_inc(inv_in, 16)
            sp.dma_start(pool_w, a["pool_w_2"][0].rearrange("g c d -> c g d")).then_inc(pool_w_in, 16)
            for n in range(chunk_number("w_in_2"), chunk_number("keys_2") + 1):
                load_chunk(n)
            sp.wait_ge(x_added, 1 + 2 * TT)
            sp.dma_start(p_rows, a["p_2"][0, 0].rearrange("(t p) d -> p t d", p=P)).then_inc(p_in, 16)
            for n in range(chunk_number("w_ple_gate_2"), len(CHUNKS)):
                load_chunk(n)
            for t in range(TT):
                sp.wait_ge(out_ready, t + 1)
                sp.dma_start(out[0, t * P:(t + 1) * P, :], xr[:, t, :]).then_inc(out_done, 16)
            sp.wait_ge(out_done, 16 * TT)

        @block.gpsimd
        def _(pool):
            nc.gpsimd.memset(w_lr[:, :, :], 0.0).then_inc(gap_zeroed, 1)
            nc.gpsimd.memset(gk_up, 0.0).then_inc(gap_zeroed, 1)
            for h in range(HEADS):
                for d in (FWD, BWD):
                    empty(pool, "gs", h, d)
                    v = g_p[2 * h + d]
                    sign = 1 if d == FWD else -1
                    nc.gpsimd.affine_select(out=v, in_=v, pattern=[[0, TT], [sign, P]], compare_op=ALU.is_ge, fill=0.0,
                                            base=0, channel_multiplier=-sign).then_inc(p_masked, 1)

            def gathers(layer, table_u, table_v):
                def u_gather(n, h, k):
                    hold(pool, u_used, n * TOPK + (k + 1))
                    nc.gpsimd.indirect_dma_start(u_rows[:, k % SLOTS, :], None, table_u,
                                                 bass.IndirectOffsetOnAxis(idx[:, h % IDX_SLOTS, k:k + 1], 0)
                                                 ).then_inc(u_loaded[k % SLOTS], 16)

                def v_gather(n, h, k):
                    hold(pool, v_used, n * TOPK + (k + 1 - SLOTS + V_CREDIT))
                    nc.gpsimd.indirect_dma_start(v_rows[:, k % SLOTS, :], None, table_v,
                                                 bass.IndirectOffsetOnAxis(idx[:, h % IDX_SLOTS, k:k + 1], 0)
                                                 ).then_inc(v_loaded[k % SLOTS], 16)

                def token_block(first, more):
                    for h in range(PH):
                        u_too = h < PH - 1 or more
                        if u_too:
                            hold(pool, routed, first + (h + 4))
                        for k in range(TOPK):
                            if u_too:
                                u_gather(first + (h + 1), (h + 1) % PH, k)
                            v_gather(first + h, h, k)

                n0 = layer * TT * PH
                pool.wait_ge(routed, n0 + 3)
                for k in range(TOPK):
                    u_gather(n0, 0, k)
                with pool.Fori(0, TT - 1) as b:
                    token_block(b * PH + n0, True)
                token_block(n0 + (TT - 1) * PH, False)

            full(pool, "norm", 1, KT - 1)
            gathers(0, a["peer_down"][0], a["peer_up"][0])
            full(pool, "norm", 2, KT - 1)
            for i in range(2):
                nc.gpsimd.memset(z_pad[i], 0.0).then_inc(pads_zeroed, 1)
                nc.gpsimd.memset(u_pad[i], 0.0).then_inc(pads_zeroed, 1)
            full(pool, "kT", 1, 3)
            gathers(1, a["expert_u_2"][0], a["expert_v_2"][0])

        @block.tensor
        def _(pe):
            state_pe = {"job": 0}

            def begin(*name):
                n = state_pe["job"]
                assert jobs.names[n] == name, (jobs.names[n], name)
                state_pe["job"] += 1
                if n >= 8:
                    pe.wait_ge(emptied[jobs.who[n - 8]], jobs.rank[n - 8])
                return psum[n % 8]

            def mm(o, lhsT, rhs, i, n):
                return nc.tensor.matmul(o, lhsT, rhs, start=(i == 0), stop=(i == n - 1))

            def use_chunk(name, c0):
                n = chunk_number(name, c0)
                pe.wait_ge(chunk_in[n % RING], 16 * (n // RING + 1))
                return chunk(n)

            def norm_rows(i):
                pe.wait_ge(rows_scaled, ROWS_UPTO[NORM_R[i]])
                for k in range(KT):
                    o = begin("norm", i, k)
                    for t in range(TT):
                        last = nc.tensor.transpose(o[:, t * P:(t + 1) * P], xr[:, t, k * P:(k + 1) * P], ident)
                    last.then_inc(bank_ready, 1)

            def to_rows(names, src, w, tiles):
                for name, t in zip(names, range(tiles)):
                    o = begin(*name)
                    for k in range(KT):
                        last = mm(o[:, :], src[:, k, t * P:(t + 1) * P], w[:, k, :], k, KT)
                    last.then_inc(bank_ready, 1)

            def to_cols(names, src, w, n):
                for j, name in enumerate(names):
                    o = begin(*name)
                    for k in range(KT):
                        last = mm(o[:, 0:n], w[:, k, j * P:(j + 1) * P], src[:, k, :], k, KT)
                    last.then_inc(bank_ready, 1)

            pe.sem_inc(v_used, V_CREDIT)

            pe.wait_ge(vec_in, 16 * len(VEC))
            pe.wait_ge(ident_in, 16)
            o = begin("cols")
            nc.tensor.transpose(o[:, 0:N_VEC], vrows[:, :], ident[0:N_VEC, 0:N_VEC]).then_inc(bank_ready, 1)

            def modulation(c):
                w = use_chunk("w_mod", CW * c)
                o = begin("mod", c)
                for k in range(KT):
                    last = mm(o[0:2, :], silu[:, k, :], w[:, k, :], k, KT)
                last.then_inc(bank_ready, 1)

            def modulation_cols(c):
                o = begin("modT", c)
                empty(pe, "mod", c)
                for j in range(4):
                    last = nc.tensor.transpose(o[:, 2 * j:2 * j + 2], mod_rows[:, c % 2, j * P:(j + 1) * P], ident[0:2, 0:2])
                last.then_inc(bank_ready, 1)

            def gate_row(name, n, c0):
                w = use_chunk("w_mod", c0)
                o = begin(name, n)
                for k in range(KT):
                    last = mm(o[:, :], silu[:, k, 0:1].to_broadcast([P, P]), w[:, k, :], k, KT)
                last.then_inc(bank_ready, 1)

            pe.wait_ge(silu_done, 1)
            for c in range(4):
                modulation(c)
                if c >= 1:
                    modulation_cols(c - 1)
            modulation_cols(3)

            norm_rows(0)
            for k in range(KT):
                o = begin("normc", k)
                for t in range(TC):
                    last = nc.tensor.transpose(o[:, t * P:(t + 1) * P], xc[:, t, k * P:(k + 1) * P], ident)
                last.then_inc(bank_ready, 1)

            w = use_chunk("w_in", W_RK)
            empty(pe, "norm", 0, KT - 2)
            empty(pe, "norm", 0, KT - 1)
            to_cols([("rk", h) for h in range(HEADS)], hT, w, L)

            def rotate(name, src):
                for h in range(HEADS):
                    o = begin(name + "rot", h)
                    empty(pe, name, h)
                    mm(o[:, :], rot, src[:, h, :], 0, 1).then_inc(bank_ready, 1)

            pe.wait_ge(const_in, 16)
            rotate("rk", rkT)
            empty(pe, "normc", KT - 2)
            empty(pe, "normc", KT - 1)
            for g in range(2):
                o = begin("rkc", g)
                for j in range(2):
                    for k in range(KT):
                        last = mm(o[:, j * LC:(j + 1) * LC], w[:, k, (2 * g + j) * P:(2 * g + j + 1) * P], hTc[:, k, :], k, KT)
                last.then_inc(bank_ready, 1)
            modulation(6)
            w = use_chunk("w_in", W_RV)
            to_rows([("rv", t) for t in range(TT)], hT, w, TT)
            to_rows([("rvc", t) for t in range(TC)], hTc, w, TC)
            modulation_cols(6)
            modulation(7)
            w = use_chunk("w_in", W_RQ)
            to_cols([("rq", h) for h in range(HEADS)], hT, w, L)
            rotate("rq", rqT)
            modulation_cols(7)
            modulation(8)

            empty(pe, "rvc", TC - 1)
            empty(pe, "rkc", 1)
            pe.wait_ge(roped, 2 * HEADS)
            for h in range(HEADS):
                for j in range(TT + TC):
                    o = begin("rs", h, j)
                    keys = rkT[:, h, j * P:(j + 1) * P] if j < TT else rkTc[:, h, (j - TT) * P:(j - TT + 1) * P]
                    mm(o[:, :], keys, rqT[:, h, :], 0, 1).then_inc(bank_ready, 1)
                o = begin("ro", h)
                empty(pe, "rs", h, TT + TC - 1)
                for t in range(TT):
                    for j in range(TT + TC):
                        vals = rv[:, j, h * DV:(h + 1) * DV] if j < TT else rvc[:, j - TT, h * DV:(h + 1) * DV]
                        last = mm(o[:, t * P:(t + 1) * P], r_p[:, j, t * P:(t + 1) * P], vals, j, TT + TC)
                last.then_inc(bank_ready, 1)

            modulation_cols(8)
            pe.wait_ge(lr_in, 16 * 6)
            for name, src, n in (("lr", hT, L), ("lrc", hTc, LC)):
                o = begin(name)
                for k in range(KT):
                    last = mm(o[0:64, 0:n], w_lr[:, k, :], src[:, k, :], k, KT)
                last.then_inc(bank_ready, 1)
            w = use_chunk("w_in", W_GQK)
            to_cols([("gq", p) for p in range(PAIRS)], hT, w, L)
            empty(pe, "lr")
            empty(pe, "lrc")
            for t in range(TT + TC):
                o = begin("la", t)
                mm(o[:, :], lrT[:, t * P:(t + 1) * P], gk_up, 0, 1).then_inc(bank_ready, 1)
            to_cols([("gk", p) for p in range(PAIRS)], hT, w[:, :, PAIRS * P:], L)
            o = begin("gkc")
            for p in range(PAIRS):
                for k in range(KT):
                    last = mm(o[:, p * LC:(p + 1) * LC], w[:, k, (PAIRS + p) * P:(PAIRS + p + 1) * P], hTc[:, k, :], k, KT)
            last.then_inc(bank_ready, 1)
            modulation(9)
            w = use_chunk("w_in", W_GV)
            to_rows([("gv", t) for t in range(TT)], hT, w, TT)
            to_rows([("gvc", t) for t in range(TC)], hTc, w, TC)
            modulation_cols(9)

            w_rg = use_chunk("w_in", W_RG)
            pe.wait_ge(la_done, 2)
            empty(pe, "gvc", 0)
            empty(pe, "gvc", 1)
            for p in range(PAIRS):
                for d in (FWD, BWD):
                    i = 2 * p + d
                    f = slice(d * 256 + p * P, d * 256 + (p + 1) * P)
                    o = begin("cum", p, d)
                    for c in range(TT):
                        last = mm(o[:, c * P:(c + 1) * P], la[:, c, f], tri(TRI_PREFIX if d == FWD else TRI_SUFFIX), 0, 1)
                    last.then_inc(bank_ready, 1)
                    o = begin("cumc", p, d)
                    own = tri(TRI_AFTER if d == FWD else TRI_BEFORE)
                    for t in range(TC):
                        other = t == (0 if d == FWD else TC - 1)
                        last = mm(o[:, t * P:(t + 1) * P], la[:, TT + t, f], own, 0, 1 + other)
                        if other:
                            last = mm(o[:, t * P:(t + 1) * P], la[:, TT + 1 - t, f], tri(TRI_ONES), 1, 2)
                    last.then_inc(bank_ready, 1)
                    o = begin("rg", i)
                    for k in range(KT):
                        last = mm(o[:, :], hT[:, k, i * P:(i + 1) * P], w_rg[:, k, :], k, KT)
                    last.then_inc(bank_ready, 1)
                    o = begin("kcT", p, d)
                    pe.wait_ge(kc_mul, i + 1)
                    for t in range(TC):
                        last = nc.tensor.transpose(o[:, t * P:(t + 1) * P], kc_exp[:, t * P:(t + 1) * P], ident)
                    last.then_inc(bank_ready, 1)
                    o = begin("s0", p, d)
                    empty(pe, "kcT", p, d)
                    for t in range(TC):
                        last = mm(o[:, 0:256], kcT[:, t, :], gvc[:, t, p * 256:(p + 1) * 256], t, TC)
                    last.then_inc(bank_ready, 1)
                    o = begin("kdT", p, d)
                    pe.wait_ge(g_mul, 4 * (i + 1))
                    for c in range(TT):
                        last = nc.tensor.transpose(o[:, c * P:(c + 1) * P], G_last[:, c * P:(c + 1) * P], ident)
                    last.then_inc(bank_ready, 1)
                    empty(pe, "kdT", p, d)
                    for s in range(TT - 1):
                        o = begin("up", p, d, s)
                        c = s if d == FWD else TT - 1 - s
                        mm(o[:, 0:256], kdT[:, i, c, :], gv[:, c, p * 256:(p + 1) * 256], 0, 1).then_inc(bank_ready, 1)
            for n in range(2):
                gate_row("g1", n, CW * (4 + n))
            for h in range(HEADS):
                for d in (FWD, BWD):
                    o = begin("gs", h, d)
                    i, r = 2 * (h // 2) + d, slice(64 * (h % 2), 64 * (h % 2) + 64)
                    for c in range(TT):
                        cs = slice(c * P, (c + 1) * P)
                        last = mm(o[:, cs], k_in[r, i, cs], q_in[r, i, cs], 0, 1)
                    last.then_inc(bank_ready, 1)
            pe.wait_ge(p_masked, 2 * HEADS)
            empty(pe, "up", 1, BWD, TT - 2)
            for c in range(TT):
                cs = slice(c * P, (c + 1) * P)
                for odd in range(2):
                    o = begin("go", c, odd)
                    r = slice(64 * odd, 64 * odd + 64)
                    for p in range(PAIRS):
                        h, oh = 2 * p + odd, o[:, p * DV:(p + 1) * DV]
                        for d in (FWD, BWD):
                            mm(oh, g_p[2 * h + d][:, c, :], gv[:, c, h * DV:(h + 1) * DV], 2 * d, 4)
                            last = mm(oh, q_st[r, 2 * p + d, cs], state[r, 2 * p + d, c, :], 2 * d + 1, 4)
                    last.then_inc(bank_ready, 1)

            w = use_chunk("w_in", W_GG)
            to_rows([("gg", t) for t in range(TT)], hT, w, TT)

            gate_row("g2", 0, CW * 10)

            for k in range(KT):
                o = begin("yT", k)
                pe.wait_ge(y_done, 1 if k < HEADS else 1 + TT)
                src = o_ret if k < HEADS else o_gla
                for t in range(TT):
                    last = nc.tensor.transpose(o[:, t * P:(t + 1) * P], src[:, t, (k % HEADS) * P:(k % HEADS + 1) * P], ident)
                last.then_inc(bank_ready, 1)
            w = [use_chunk("w_out", CW * n) for n in range(2)]
            empty(pe, "yT", KT - 2)
            empty(pe, "yT", KT - 1)
            for t in range(TT):
                for n in range(2):
                    o = begin("wo", t, n)
                    for k in range(KT):
                        last = mm(o[:, :], yT[:, k, t * P:(t + 1) * P], w[n][:, k, :], k, KT)
                    last.then_inc(bank_ready, 1)

            def keys(layer, raw):
                for g in range(4):
                    o = begin("kT", layer, g)
                    for j in range(4):
                        last = nc.tensor.transpose(o[:, j * P:(j + 1) * P], raw[:, 4 * g + j, :], ident)
                    last.then_inc(bank_ready, 1)

            def peer(layer):
                def scores(n, h):
                    q, s = psum[4 + h % 2], psum[6 + h % 2]
                    for half in range(2):
                        for k in range(KT):
                            c0 = (2 * h + half) * P
                            last = mm(q[:, half * P:(half + 1) * P], w_q[:, k, c0:c0 + P], x_cur[:, k, :], k, KT)
                    last.then_inc(q_done, 1)
                    pe.wait_ge(q_copied, n + 1)
                    for half in range(2):
                        last = mm(s[:, half * P:(half + 1) * P], peer_qT[:, h % 2, half, :], kT[:, 2 * h + half, :], 0, 1)
                    last.then_inc(s_done, 1)

                def block_rows():
                    for k in range(KT):
                        last = nc.tensor.transpose(psum[k // 4][:, (k % 4) * P:(k % 4 + 1) * P], x_cur[:, k, :], ident)
                    last.then_inc(xn_ready, 1)

                def add_up(n, h):
                    for k in range(TOPK):
                        pe.wait_ge(diag_set, n * TOPK + (k + 1))
                        pe.wait_ge(v_loaded[k % SLOTS], n * (16 * TOPK // SLOTS) + 16 * (k // SLOTS + 1))
                        for c in range(2):
                            last = nc.tensor.matmul(psum[2 + c][:, :], diag[:, k, :], v_rows[:, k % SLOTS, c * CW:(c + 1) * CW],
                                                    start=(h == 0 and k == 0), stop=(h == PH - 1 and k == TOPK - 1))
                        last.then_inc(v_used, 1)

                def token_block(it, more):
                    for h in range(PH):
                        if h == PH - 2 and more:
                            pe.wait_ge(x_cur_set, it + 2)
                        if h < PH - 2 or more:
                            scores(it * PH + (h + 2), (h + 2) % PH)
                        if h == 0:
                            pe.wait_ge(x_added, it + 1)
                        if h == PH - 1 and more:
                            pe.wait_ge(u_used, it * (PH * TOPK) + (PH * TOPK + SLOTS))
                            block_rows()
                        add_up(it * PH + h, h)

                all_empty(pe, "kT", layer, 3)
                pe.wait_ge(w_q_in, 16 * (layer + 1))
                pe.wait_ge(x_cur_set, layer * TT + 1)
                scores(layer * TT * PH, 0)
                block_rows()
                scores(layer * TT * PH + 1, 1)
                with pe.Fori(0, TT - 1) as b:
                    token_block(b + layer * TT, True)
                token_block(TT - 1 + layer * TT, False)
                pe.wait_ge(x_added, 1 + TT * (layer + 1))

            pe.wait_ge(keys_in, 32)
            keys(0, raw_keys.rearrange("p h s d -> p (h s) d"))
            gate_row("g2", 1, CW * 11)
            norm_rows(1)
            peer(0)

            norm_rows(2)
            w = [use_chunk("w_in_2", CW * i) for i in range(3)]
            empty(pe, "norm", 2, KT - 2)
            empty(pe, "norm", 2, KT - 1)
            for j in range(4):
                for name, i in (("cc", 1), ("cv", 2), ("cb", 0)):
                    o = begin(name, j)
                    for k in range(KT):
                        last = mm(o[:, :], w[i][:, k, j * P:(j + 1) * P], hT[:, k, :], k, KT)
                    last.then_inc(bank_ready, 1)
            w = use_chunk("w_in_2", CW * 3)
            to_cols([("pu", g) for g in range(4)], hT, w, L)
            pe.wait_ge(pool_w_in, 16)
            for g in range(4):
                o = begin("py", g)
                pe.wait_ge(pooled, g + 1)
                mm(o[:, :], pool_w[:, g, :], yT2[:, 4 + g, :], 0, 1).then_inc(bank_ready, 1)
            empty(pe, "cb", 3)
            for n in range(2):
                w = use_chunk("w_o_2", CW * n)
                empty(pe, "py", 3)
                to_rows([("wo2", t, n) for t in range(TT)], yT2, w, TT)
            norm_rows(3)
            use_chunk("keys_2", 0)
            keys(1, at(ring, (chunk_number("keys_2") % RING) * KT * CW, 2 * PH, P))
            peer(1)

            norm_rows(4)
            pe.wait_ge(p_in, 16)
            for k in range(2):
                o = begin("pT", k)
                for t in range(TT):
                    last = nc.tensor.transpose(o[:, t * P:(t + 1) * P], p_rows[:, t, k * P:(k + 1) * P], ident)
                last.then_inc(bank_ready, 1)
            w = [use_chunk("w_ple_gate_2", CW * i) for i in range(2)]
            use_chunk("w_ple_proj_2", 0)
            w_proj = at(ring, (chunk_number("w_ple_proj_2") % RING) * KT * CW, 2, D)
            empty(pe, "norm", 4, KT - 2)
            empty(pe, "norm", 4, KT - 1)
            empty(pe, "pT", 1)
            for n in range(2):
                for t in range(TT):
                    o = begin("gate", t, n)
                    for k in range(KT):
                        last = mm(o[:, :], hT[:, k, t * P:(t + 1) * P], w[n][:, k, :], k, KT)
                    last.then_inc(bank_ready, 1)
                    o = begin("pp", t, n)
                    for k in range(2):
                        last = mm(o[:, :], pT[:, k, t * P:(t + 1) * P], w_proj[:, k, n * CW:(n + 1) * CW], k, 2)
                    last.then_inc(bank_ready, 1)

        @block.scalar
        def _(act):
            def copy_out(dst, *name, scale=1.0):
                o = full(act, *name)
                n = int(np.prod(dst.shape[1:]))
                src = o[0:dst.shape[0], 0:n]
                if len(dst.shape) == 3:
                    src = src.rearrange("p (a b) -> p a b", b=dst.shape[2])
                return nc.scalar.activation(dst, src, ACT.Copy, scale=scale)

            def squares(r, wait_rows, tiles):
                for t, (rows, junk) in enumerate(tiles):
                    wait_rows(t)
                    nc.scalar.activation(junk, rows, ACT.Square, accum_out=stat[:, 0, t:t + 1]).then_inc(sumsq, 1)
                act.wait_ge(meansq, r + 1)
                nc.scalar.activation(stat[:, 2, 0:len(tiles)], stat[:, 1, 0:len(tiles)], ACT.Sqrt).then_inc(root, 1)

            x_tiles = [(X[:, t, :], xr[:, t, :]) for t in range(TT)]

            def transposed(i, gains, shifts):
                for k in range(0, KT, 2):
                    o = full(act, "norm", i, k)
                    nc.scalar.activation(hT[:, k, :], o[:, :], ACT.Identity, bias=shifts(k), scale=gains(k)
                                         ).then_inc(emptied["A"], 1)

            empty(act, "cols")
            nc.scalar.activation(silu[:, :, :].rearrange("p k a -> p a k"),
                                 cols[:, 0:2 * KT].rearrange("p (a k) -> p a k", k=KT), ACT.Silu).then_inc(silu_done, 1)
            junk_c = at(scr, 23040, TC, D)
            squares(0, lambda t: act.wait_ge(x_in if t < TT else ctx_in, 16),
                    x_tiles + [(xc[:, t, :], junk_c[:, t, :]) for t in range(TC)])

            act.wait_ge(lg_in, 32)
            nc.scalar.activation(lg[:, 1, :], lg[:, 0, :], ACT.Abs).then_inc(lg_act, 1)
            act.wait_ge(lg_act, 1)
            nc.scalar.activation(lg[:, 1, :], lg[:, 1, :], ACT.Exp, scale=-1.0).then_inc(lg_act, 1)
            act.wait_ge(lg_act, 2)
            nc.scalar.activation(lg[:, 1, :], lg[:, 1, :], ACT.Ln, bias=1.0).then_inc(lg_act, 1)

            def decay_masks(h):
                if h >= 2:
                    empty(act, "rs", h - 2, TT + TC - 1)
                m, c = mask_m[h % 2], mask_c[h % 2]
                ahead, behind = const[:, C_AHEAD:C_AHEAD + 384 + L], const[:, C_BEHIND:C_BEHIND + 384 + L]
                since = const[:, C_AHEAD + 512:C_AHEAD + 512 + 640]
                nc.scalar.activation(m[:, 0, :], ahead, ACT.Exp, scale=lg[:, 3, h:h + 1]).then_inc(exps, 1)
                nc.scalar.activation(m[:, 1, :], behind, ACT.Exp, scale=lg[:, 3, 4 + h:5 + h]).then_inc(exps, 1)
                nc.scalar.activation(c[:, 0, :], since, ACT.Exp, scale=lg[:, 3, h:h + 1]).then_inc(exps, 1)
                nc.scalar.activation(c[:, 1, :], since, ACT.Exp, scale=lg[:, 1, 4 + h:5 + h], bias=lg[:, 2, 4 + h:5 + h]
                                     ).then_inc(exps, 1)

            act.wait_ge(lg_step, 4)
            act.wait_ge(const_in, 16)
            decay_masks(0)
            decay_masks(1)

            act.wait_ge(gains_done, 2)
            transposed(0, lambda k: gain[:, 0, k:k + 1], lambda k: mod[:, k, 0:1])
            for k in range(0, KT, 2):
                o = full(act, "normc", k)
                nc.scalar.activation(hTc[:, k, :], o[:, 0:LC], ACT.Identity, bias=mod[:, k, 1:2], scale=gain[:, 1, k:k + 1]
                                     ).then_inc(emptied["A"], 1)
            for h in range(HEADS):
                copy_out(rkT[:, h, :], "rk", h, scale=RET_DK ** -0.5).then_inc(emptied["A"], 1)
            for g in range(2):
                copy_out(rkTc[:, 2 * g:2 * g + 2, :], "rkc", g, scale=RET_DK ** -0.5).then_inc(emptied["A"], 1)
            for t in range(TT):
                copy_out(rv[:, t, :], "rv", t).then_inc(emptied["A"], 1)
            for t in range(TC):
                copy_out(rvc[:, t, :], "rvc", t).then_inc(emptied["A"], 1)
            for h in range(HEADS):
                copy_out(rqT[:, h, :], "rq", h).then_inc(emptied["A"], 1)
            for h in range(HEADS):
                copy_out(o_ret[:, :, h * DV:(h + 1) * DV], "ro", h).then_inc(emptied["A"], 1)
                if h + 2 < HEADS:
                    decay_masks(h + 2)

            act.wait_ge(ones_set, 1)
            for name, c0, n in (("lr", 0, L), ("lrc", L, LC)):
                o = full(act, name)
                nc.scalar.activation(lrT[0:RANK, c0:c0 + n], o[0:RANK, 0:n], ACT.Copy)
                nc.scalar.activation(lrT[32:32 + RANK, c0:c0 + n], o[32:32 + RANK, 0:n], ACT.Copy).then_inc(emptied["A"], 1)
            for p in range(PAIRS):
                copy_out(gqT[:, p, :], "gq", p, scale=GLA_DK ** -0.5).then_inc(emptied["A"], 1)
            for t in range(TT + TC):
                o = full(act, "la", t)
                nc.scalar.activation(la_tmp[:, t, :], o[:, :], ACT.Abs).then_inc(la_abs, 1)
            act.wait_ge(la_abs, TT + TC)
            nc.scalar.activation(la_tmp, la_tmp, ACT.Exp, scale=-1.0).then_inc(la_exp, 1)
            act.wait_ge(la_exp, 1)
            for part in (slice(0, TT), slice(TT, TT + TC)):
                nc.scalar.activation(la_tmp[:, part, :], la_tmp[:, part, :], ACT.Ln, bias=1.0).then_inc(la_ln, 1)
            for p in range(PAIRS):
                copy_out(gkT[:, p, :], "gk", p).then_inc(emptied["A"], 1)
            copy_out(gkTc, "gkc").then_inc(emptied["A"], 1)
            act.wait_ge(head_step, 2 * TT + 1)
            nc.scalar.activation(hstat[:, 2, 0:TT * HEADS], hstat[:, 1, 0:TT * HEADS], ACT.Sqrt).then_inc(head_root, 1)
            for t in range(0, TT, 2):
                copy_out(gv[:, t, :], "gv", t).then_inc(emptied["A"], 1)
            copy_out(gvc[:, 0, :], "gvc", 0).then_inc(emptied["A"], 1)
            for p in range(PAIRS):
                for d in (FWD, BWD):
                    i, last = 2 * p + d, P - 1 if d == FWD else 0
                    o = full(act, "cumc", p, d)
                    nc.scalar.activation(kc_exp, o[:, 0:LC], ACT.Exp).then_inc(emptied["A"], 1)
                    act.wait_ge(g_sub, 2 * (i + 1))
                    nc.scalar.activation(G_neg, G_mid, ACT.Exp, scale=-1.0).then_inc(g_exp, 1)
                    nc.scalar.activation(G_mid, G_mid, ACT.Exp).then_inc(g_exp, 1)
                    nc.scalar.activation(G_last, G_last, ACT.Exp, scale=-1.0).then_inc(g_exp, 1)
                    nc.scalar.activation(chunk_dec[:, i, :], G.rearrange("p (c t) -> p c t", t=P)[:, :, last], ACT.Exp
                                         ).then_inc(g_exp, 1)
                    act.wait_ge(g_exp, 5 * i + 4)
                    nc.scalar.activation(G, G, ACT.Exp).then_inc(g_exp, 1)
                    copy_out(ret_gate[:, i, :], "rg", i).then_inc(emptied["A"], 1)
                    copy_out(kcT, "kcT", p, d).then_inc(emptied["A"], 1)
                    copy_out(kdT[:, i, :, :], "kdT", p, d).then_inc(emptied["A"], 1)
            for h in range(HEADS):
                for d in (FWD, BWD):
                    copy_out(g_p[2 * h + d], "gs", h, d).then_inc(emptied["A"], 1)
            empty(act, "rg", TT - 1)
            nc.scalar.activation(ret_gate, ret_gate, ACT.Silu).then_inc(rg_silu, 1)
            for c in range(TT):
                for odd in range(2):
                    copy_out(o_gla[:, c, :].rearrange("p (a b v) -> p b a v", b=2, v=DV)[:, odd], "go", c, odd
                             ).then_inc(emptied["A"], 1)

            act.wait_ge(head_step, 4 * TT + 3)
            nc.scalar.activation(hstat[:, 2, TT * HEADS:], hstat[:, 1, TT * HEADS:], ACT.Sqrt).then_inc(head_root, 1)
            for t in range(TT):
                if t >= 2:
                    act.wait_ge(y_done, 1 + t - 1)
                o = full(act, "gg", t)
                nc.scalar.activation(gate_tmp[:, t % 2, :], o[:, :], ACT.Silu).then_inc(emptied["A"], 1)
            for k in range(0, KT, 2):
                copy_out(yT[:, k, :], "yT", k).then_inc(emptied["A"], 1)

            def added(name, t):
                empty(act, name, t, 1)

            squares(1, lambda t: added("wo", t), x_tiles)
            for g in range(4):
                copy_out(kT[:, 4 * g:4 * g + 4, :], "kT", 0, g).then_inc(emptied["A"], 1)
            act.wait_ge(gains_done, 3)
            transposed(1, lambda k: gain[:, 2, k:k + 1], lambda k: mod[:, 3 * KT + k, 0:1])

            def peer(layer, gelu_func):
                def rows_of(it, b):
                    nc.scalar.activation(x_cur, hT[:, :, bass.ds(b * P, P)], ACT.Copy).then_inc(x_cur_set, 1)

                def scores_out(n, h):
                    act.wait_ge(q_done, n + 1)
                    nc.scalar.activation(peer_qT[:, h % 2, :, :].rearrange("p a b -> p (a b)"), psum[4 + h % 2][:, 0:2 * P],
                                         ACT.Copy).then_inc(q_copied, 1)
                    hold(act, routed, n + 1)
                    act.wait_ge(s_done, n + 1)
                    nc.scalar.activation(score[:, h % 2, :, :].rearrange("p a b -> p (a b)"), psum[6 + h % 2][:, 0:2 * P],
                                         ACT.Copy).then_inc(s_copied, 1)

                def softmax_exp(n):
                    act.wait_ge(topped, n + 1)
                    nc.scalar.activation(exp_s, top2, ACT.Exp, bias=neg_max, accum_out=exp_sum).then_inc(exp_done, 1)

                def head(n, h, more=True):
                    if more:
                        scores_out(n + 1, (h + 1) % PH)
                        softmax_exp(n + 1)
                    act.wait_ge(u_used, n * TOPK + (TOPK + SLOTS))
                    nc.scalar.activation(gelu[:, h % 2, :], dots[:, h % 2, :], gelu_func).then_inc(gelu_done, 1)
                    hold(act, weighted, n + 1)
                    for k in range(TOPK):
                        act.wait_ge(v_used, n * TOPK + (k + 1 - TOPK + V_CREDIT))
                        nc.scalar.activation(diag[:, k, :], ident, ACT.Copy, scale=weight[:, h % 2, k:k + 1]
                                             ).then_inc(diag_set, 1)

                def token_block(it, b, more):
                    for h in range(1, PH):
                        if h == PH - 1 and more:
                            hold(act, q_done, it * PH + PH)
                            rows_of(it + 1, b + 1)
                        head(it * PH + h, h, h < PH - 1 or more)
                    if more:
                        head(it * PH + PH, 0)

                empty(act, "norm", 1 if layer == 0 else 3, KT - 1)
                empty(act, "norm", 1 if layer == 0 else 3, KT - 2)
                nc.scalar.activation(x_cur, hT[:, :, 0:P], ACT.Copy).then_inc(x_cur_set, 1)
                scores_out(layer * TT * PH, 0)
                softmax_exp(layer * TT * PH)
                head(layer * TT * PH, 0)
                with act.Fori(0, TT - 1) as b:
                    token_block(b + layer * TT, b, True)
                token_block(TT - 1 + layer * TT, TT - 1, False)

            peer(0, ACT.Gelu)
            squares(2, lambda t: act.wait_ge(x_added, 1 + TT), x_tiles)
            squares(3, lambda t: act.wait_ge(x_new, t + 1), x_tiles)
            no_shift = lambda k: 0.0
            transposed(2, lambda k: col("g_mix_2", k), no_shift)
            for j in range(4):
                if j >= 2:
                    empty(act, "cv", j - 2)
                copy_out(c_gate[:, j % 2, :], "cc", j).then_inc(emptied["A"], 1)
            act.wait_ge(pads_zeroed, 4)
            for g in range(4):
                if g >= 2:
                    act.wait_ge(pooled, g - 1)
                copy_out(u_pad[g % 2][:, PAD:PAD + L], "pu", g).then_inc(emptied["A"], 1)
            for g in range(4):
                copy_out(yT2[:, 4 + g, :], "py", g, scale=col("pool_scale_2", g)).then_inc(emptied["A"], 1)
            squares(4, lambda t: added("wo2", t), x_tiles)
            transposed(3, lambda k: col("g_ffn_2", k), no_shift)
            for g in range(4):
                copy_out(kT[:, 4 * g:4 * g + 4, :], "kT", 1, g).then_inc(emptied["A"], 1)
            peer(1, ACT.Gelu_apprx_tanh)
            squares(5, lambda t: act.wait_ge(x_added, 1 + 2 * TT), x_tiles)
            transposed(4, lambda k: col("g_ple_2", k), no_shift)
            for k in range(2):
                copy_out(pT[:, k, :], "pT", k).then_inc(emptied["A"], 1)
            for u in range(2 * TT):
                t, n = u % TT, u // TT
                if u >= 2:
                    empty(act, "pp", (u - 2) % TT, (u - 2) // TT)
                o = full(act, "gate", t, n)
                nc.scalar.activation(ple_gate[:, u % 2, :], o[:, :], ACT.Sigmoid).then_inc(emptied["A"], 1)
            squares(6, lambda t: added("pp", t), x_tiles)

        @block.vector
        def _(dve):
            V = nc.vector
            dve.sem_inc(u_used, SLOTS)
            dve.sem_inc(routed, 2)
            dve.sem_inc(x_added, 1)

            def scale_rows(r, tiles):
                n = len(tiles)
                dve.wait_ge(sumsq, ROWS_UPTO[r])
                V.tensor_scalar(stat[:, 1, 0:n], stat[:, 0, 0:n], 1.0 / D, EPS, ALU.mult, ALU.add).then_inc(meansq, 1)
                dve.wait_ge(root, r + 1)
                V.reciprocal(stat[:, 3, 0:n], stat[:, 2, 0:n]).then_inc(rstd, 1)
                dve.wait_ge(rstd, r + 1)
                for t, (src, dst) in enumerate(tiles):
                    V.tensor_scalar(dst, src, stat[:, 3, t:t + 1], None, ALU.mult).then_inc(rows_scaled, 1)

            x_tiles = [(X[:, t, :], xr[:, t, :]) for t in range(TT)]

            def transposed(i, gains, shifts):
                for k in range(1, KT, 2):
                    o = full(dve, "norm", i, k)
                    if shifts is None:
                        ins = V.tensor_scalar(hT[:, k, :], o[:, :], gains(k), None, ALU.mult)
                    else:
                        ins = V.tensor_scalar(hT[:, k, :], o[:, :], gains(k), shifts(k), ALU.mult, ALU.add)
                    ins.then_inc(emptied["D"], 1)

            def modulation(c):
                o = full(dve, "mod", c)
                if c % 4 >= 2 or c >= 6:
                    full(dve, "modT", c - 2 if c != 6 and c != 7 else c - 4)
                V.tensor_copy(mod_rows[:, c % 2, :], o[0:2, :]).then_inc(emptied["D"], 1)

            def modulation_cols(c):
                o = full(dve, "modT", c)
                V.tensor_tensor(mod[:, 4 * c:4 * c + 4, :], o[:, 0:8].rearrange("p (j v) -> p j v", v=2),
                                col("b_mod", 4 * c, 4).unsqueeze(2).to_broadcast([P, 4, 2]),
                                ALU.add).then_inc(emptied["D"], 1)

            def norm_gain(g, tile, v, name):
                V.scalar_tensor_tensor(gain[:, g, :], mod[:, tile:tile + KT, v], 1.0, col(name, 0, KT),
                                       ALU.add, ALU.mult).then_inc(gains_done, 1)

            o = full(dve, "cols")
            V.tensor_copy(cols[:, :], o[:, 0:N_VEC]).then_inc(emptied["D"], 1)
            empty(dve, "cols")
            modulation(0)
            modulation(1)
            modulation_cols(0)
            modulation(2)
            modulation_cols(1)
            scale_rows(0, x_tiles + [(xc[:, t, :], xc[:, t, :]) for t in range(TC)])

            dve.wait_ge(lg_in, 32)
            V.tensor_scalar(lg[:, 2, :], lg[:, 0, :], 0.0, None, ALU.min).then_inc(lg_step, 1)
            dve.wait_ge(lg_act, 3)
            dve.wait_ge(lg_step, 1)
            V.tensor_tensor(lg[:, 3, :], lg[:, 2, :], lg[:, 1, :], ALU.subtract).then_inc(lg_step, 1)
            dve.wait_ge(lg_step, 2)
            V.tensor_scalar(lg[:, 1, :], lg[:, 3, :], -1.0, None, ALU.mult).then_inc(lg_step, 1)
            V.tensor_scalar(lg[:, 2, :], lg[:, 3, :], float(L + LC), None, ALU.mult).then_inc(lg_step, 1)

            modulation(3)
            modulation_cols(2)
            modulation_cols(3)
            empty(dve, "modT", 3)
            norm_gain(0, KT, 0, "norm1_w")
            norm_gain(1, KT, 1, "norm1_w")
            dve.wait_ge(gains_done, 2)
            transposed(0, lambda k: gain[:, 0, k:k + 1], lambda k: mod[:, k, 0:1])
            for k in range(1, KT, 2):
                o = full(dve, "normc", k)
                V.tensor_scalar(hTc[:, k, :], o[:, 0:LC], gain[:, 1, k:k + 1], mod[:, k, 1:2], ALU.mult, ALU.add
                                ).then_inc(emptied["D"], 1)

            def rope(name, first):
                for h in range(HEADS):
                    x = (rkT if name == "rk" else rqT)[:, h, :]
                    tmp = rot_tmp[:, h % 2, :]
                    o = full(dve, name + "rot", h)
                    V.tensor_tensor(tmp, o[:, :], sin_t, ALU.mult).then_inc(emptied["D"], 1)
                    V.tensor_tensor(x, x, cos_t, ALU.mult).then_inc(rotating, 1)
                    dve.wait_ge(rotating, first + h + 1)
                    empty(dve, name + "rot", h)
                    V.tensor_tensor(x, x, tmp, ALU.add).then_inc(roped, 1)

            def masks(h):
                m, c = mask_m[h % 2], mask_c[h % 2]
                dve.wait_ge(exps, 4 * h + 4)
                V.tensor_tensor(m[:, 0, :], m[:, 0, :], m[:, 1, :], ALU.mult).then_inc(mask_step, 1)
                V.tensor_tensor(c[:, 0, :], c[:, 0, :], c[:, 1, :], ALU.add).then_inc(mask_step, 1)
                dve.wait_ge(mask_step, 3 * h + 1)
                V.tensor_tensor(m[:, 0, 384:512], m[:, 0, 384:512], const[:, C_TWICE:C_TWICE + P], ALU.mult).then_inc(mask_step, 1)

            dve.wait_ge(const_in, 16)
            rope("rk", 0)
            modulation(6)
            masks(0)
            modulation_cols(6)
            modulation(7)
            rope("rq", HEADS)
            modulation_cols(7)
            modulation(8)
            for h in range(HEADS):
                if h >= 1:
                    full(dve, "ro", h - 1)
                dve.wait_ge(mask_step, 3 * h + 3)
                for j in range(TT + TC):
                    o = full(dve, "rs", h, j)
                    if j < TT:
                        m = mask_m[h % 2][:, 0, 384 - P * j:384 - P * j + L]
                    else:
                        m = mask_c[h % 2][:, 0, P * (TC - 1 - (j - TT)):P * (TC - 1 - (j - TT)) + L]
                    V.tensor_tensor(r_p[:, j, :], o[:, :], m, ALU.mult).then_inc(emptied["D"], 1)
                if h + 1 < HEADS:
                    masks(h + 1)

            modulation_cols(8)
            empty(dve, "rs", HEADS - 1, TT + TC - 1)
            V.memset(lrT, 1.0).then_inc(ones_set, 1)

            def gate_row(name, n, row, bias_in):
                dve.wait_ge(bias_in, 16)
                o, r = full(dve, name, n), row[:, n * CW:(n + 1) * CW]
                V.tensor_tensor(r, o[:, :], r, ALU.add).then_inc(emptied["D"], 1)

            def head_squares(u):
                src, sq = ((o_ret, ret_sq) if u < TT else (o_gla, sq_tmp))
                V.tensor_tensor(sq[:, u % 2, :], src[:, u % TT, :], src[:, u % TT, :], ALU.mult).then_inc(head_step, 1)
                dve.wait_ge(head_step, 2 * u + 1 + (u >= TT) * 2)
                V.tensor_reduce(hstat[:, 0, 4 * u:4 * u + 4], sq[:, u % 2, :].rearrange("p (h v) -> p h v", v=DV),
                                AX_X, ALU.add).then_inc(head_step, 1)

            def head_means(i):
                s = slice(i * TT * HEADS, (i + 1) * TT * HEADS)
                dve.wait_ge(head_step, 2 * TT * (i + 1) + 2 * i)
                V.tensor_scalar(hstat[:, 1, s], hstat[:, 0, s], 1.0 / DV, EPS, ALU.mult, ALU.add).then_inc(head_step, 1)

            def head_roots(i):
                s = slice(i * TT * HEADS, (i + 1) * TT * HEADS)
                dve.wait_ge(head_root, i + 1)
                V.reciprocal(hstat[:, 3, s], hstat[:, 2, s]).then_inc(head_step, 1)
                dve.wait_ge(head_step, (2 * TT + 2) * (i + 1))

            def head_scale(u):
                src = (o_ret if u < TT else o_gla)[:, u % TT, :].rearrange("p (h v) -> p h v", v=DV)
                V.tensor_tensor(src, src, hstat[:, 3, 4 * u:4 * u + 4].unsqueeze(2).to_broadcast([P, HEADS, DV]), ALU.mult
                                ).then_inc(y_step, 1)

            for t in range(TT + TC):
                o = full(dve, "la", t)
                dve.wait_ge(la_abs, t + 1)
                V.tensor_scalar(la[:, t, :], o[:, :], 0.0, 1.0 / GATE_NORM, ALU.min, ALU.mult).then_inc(emptied["D"], 1)
            empty(dve, "la", TT + TC - 1)
            for i, part in enumerate((slice(0, TT), slice(TT, TT + TC))):
                dve.wait_ge(la_ln, i + 1)
                V.scalar_tensor_tensor(la[:, part, :], la_tmp[:, part, :], -1.0 / GATE_NORM, la[:, part, :], ALU.mult, ALU.add
                                       ).then_inc(la_done, 1)
            empty(dve, "ro", HEADS - 1)
            for u in range(TT):
                head_squares(u)
            head_means(0)
            modulation(9)
            for t in range(1, TT, 2):
                o = full(dve, "gv", t)
                V.tensor_copy(gv[:, t, :], o[:, :]).then_inc(emptied["D"], 1)
            head_roots(0)
            o = full(dve, "gvc", 1)
            V.tensor_copy(gvc[:, 1, :], o[:, :]).then_inc(emptied["D"], 1)
            for u in range(TT):
                head_scale(u)
            modulation_cols(9)
            for p in range(PAIRS):
                for d in (FWD, BWD):
                    i = 2 * p + d
                    mid, last = (P // 2 - 1, P - 1) if d == FWD else (P // 2, 0)
                    o = full(dve, "cum", p, d)
                    if i >= 1:
                        full(dve, "kdT", (i - 1) // 2, (i - 1) % 2)
                    V.tensor_copy(G, o[:, :]).then_inc(emptied["D"], 1)
                    empty(dve, "cum", p, d)
                    g3 = G.rearrange("p (c t) -> p c t", t=P)
                    for dst, at_t in ((G_mid, mid), (G_last, last)):
                        V.tensor_tensor(dst.rearrange("p (c t) -> p c t", t=P), g3,
                                        g3[:, :, at_t:at_t + 1].to_broadcast([P, TT, P]), ALU.subtract).then_inc(g_sub, 1)
                    empty(dve, "cumc", p, d)
                    V.tensor_tensor(kc_exp, kc_exp, gkTc[:, p, :], ALU.mult).then_inc(kc_mul, 1)
                    dve.wait_ge(g_exp, 5 * (i + 1))
                    V.tensor_tensor(G_last, G_last, gkT[:, p, :], ALU.mult).then_inc(g_mul, 1)
                    V.tensor_tensor(q_in[:, i, :], G_mid, gqT[:, p, :], ALU.mult).then_inc(g_mul, 1)
                    V.tensor_tensor(k_in[:, i, :], G_neg, gkT[:, p, :], ALU.mult).then_inc(g_mul, 1)
                    V.tensor_tensor(q_st[:, i, :], G, gqT[:, p, :], ALU.mult).then_inc(g_mul, 1)
                    c = 0 if d == FWD else TT - 1
                    o = full(dve, "s0", p, d)
                    V.tensor_copy(state[0:64, i, c, :], o[0:64, 0:DV]).then_inc(state_half, 1)
                    V.tensor_copy(state[64:128, i, c, :], o[64:128, DV:2 * DV]).then_inc(emptied["D"], 1)
                    for s in range(TT - 1):
                        to = c + 1 if d == FWD else c - 1
                        o = full(dve, "up", p, d, s)
                        dve.wait_ge(state_half, i * TT + s + 1)
                        if s == 0:
                            empty(dve, "s0", p, d)
                        else:
                            empty(dve, "up", p, d, s - 1)
                        for half, done in ((0, state_half), (1, emptied["D"])):
                            r = slice(64 * half, 64 * half + 64)
                            V.scalar_tensor_tensor(state[r, i, to, :], state[r, i, c, :], chunk_dec[r, i, c:c + 1],
                                                   o[r, half * DV:(half + 1) * DV], ALU.mult, ALU.add).then_inc(done, 1)
                        c = to

            for n in range(2):
                gate_row("g1", n, row_a, row_a_in)
            dve.wait_ge(rg_silu, 1)
            dve.wait_ge(y_step, TT)
            V.tensor_tensor(o_ret, o_ret, ret_gate, ALU.mult).then_inc(y_done, 1)
            empty(dve, "modT", 9)
            norm_gain(2, 4 * KT, 0, "norm2_w")
            for t in range(TT):
                empty(dve, "go", t, 1)
                head_squares(TT + t)
            head_means(1)
            head_roots(1)
            for t in range(TT):
                head_scale(TT + t)
                dve.wait_ge(y_step, TT + t + 1)
                empty(dve, "gg", t)
                V.tensor_tensor(o_gla[:, t, :], o_gla[:, t, :], gate_tmp[:, t % 2, :], ALU.mult).then_inc(y_done, 1)
            gate_row("g2", 0, row_b, row_b_in)
            for k in range(1, KT, 2):
                o = full(dve, "yT", k)
                V.tensor_copy(yT[:, k, :], o[:, :]).then_inc(emptied["D"], 1)
            empty(dve, "g1", 1)
            for t in range(TT):
                for n in range(2):
                    o, x = full(dve, "wo", t, n), X[:, t, n * CW:(n + 1) * CW]
                    V.tensor_tensor(o[:, :], o[:, :], row_a[:, n * CW:(n + 1) * CW], ALU.mult).then_inc(wo_mul, 1)
                    dve.wait_ge(wo_mul, 2 * t + n + 1)
                    V.tensor_tensor(x, o[:, :], x, ALU.add).then_inc(emptied["D"], 1)
            empty(dve, "wo", TT - 1, 1)
            scale_rows(1, x_tiles)
            gate_row("g2", 1, row_b, row_b_in)
            dve.wait_ge(gains_done, 3)
            transposed(1, lambda k: gain[:, 2, k:k + 1], lambda k: mod[:, 3 * KT + k, 0:1])

            def peer(layer):
                def route(n, h):
                    step = [0]

                    def then(ins):
                        step[0] += 1
                        ins.then_inc(route_step, 1)

                    def after(k):
                        dve.wait_ge(route_step, k)

                    hold(dve, s_copied, n + 1)
                    hold(dve, v_used, n * TOPK + (V_CREDIT - (IDX_SLOTS - 1) * TOPK))
                    dve.sem_clear(route_step)
                    s = score[:, h % 2, :, :]
                    for half in range(2):
                        then(V.max(top1[:, half, 0:8], s[:, half, :]))
                    for half in range(2):
                        after(1 + half)
                        then(V.match_replace(score_rest[:, half, :], top1[:, half, 0:8], s[:, half, :], LOWEST))
                    for half in range(2):
                        then(V.max_index(key_i[:, half, 0:8], top1[:, half, 0:8], s[:, half, :]))
                    for half in range(2):
                        after(3 + half)
                        then(V.max(top1[:, half, 8:16], score_rest[:, half, :]))
                    after(8)
                    then(V.tensor_tensor(cand, top1[:, 0, :].unsqueeze(2).to_broadcast([P, TOPK, TOPK]),
                                         top1[:, 1, :].unsqueeze(1).to_broadcast([P, TOPK, TOPK]), ALU.add))
                    for half in range(2):
                        then(V.max_index(key_i[:, half, 8:16], top1[:, half, 8:16], score_rest[:, half, :]))
                    after(9)
                    flat = cand.rearrange("p a b -> p (a b)")
                    then(V.max(top2[:, 0:8], flat))
                    after(11)
                    then(V.tensor_copy(key_f.rearrange("p a b -> p (a b)"), key_i[:, :, :].rearrange("p a b -> p (a b)")))
                    after(12)
                    then(V.match_replace(cand_rest, top2[:, 0:8], flat, LOWEST))
                    then(V.max_index(pos_i[:, 0:8], top2[:, 0:8], flat))
                    after(14)
                    then(V.max(top2[:, 8:16], cand_rest))
                    then(V.tensor_scalar(neg_max, top2[:, 0:1], -1.0, None, ALU.mult))
                    after(17)
                    V.max_index(pos_i[:, 8:16], top2[:, 8:16], cand_rest).then_inc(topped, 1)
                    dve.wait_ge(topped, n + 1)
                    then(V.tensor_scalar(pos_ab[:, 0, :], pos_i[:, :], 4, None, ALU.logical_shift_right))
                    then(V.tensor_scalar(pos_ab[:, 1, :], pos_i[:, :], TOPK - 1, None, ALU.bitwise_and))
                    after(19)
                    hot = onehot.rearrange("p h k a -> p (h k) a")
                    then(V.tensor_tensor(hot, pos_ab[:, :, :].rearrange("p h k -> p (h k)").unsqueeze(2).to_broadcast([P, 2 * TOPK, TOPK]),
                                         const[:, C_IOTA:C_IOTA + TOPK].unsqueeze(1).to_broadcast([P, 2 * TOPK, TOPK]), ALU.is_equal))
                    after(20)
                    then(V.tensor_tensor(onehot, onehot, key_f.unsqueeze(2).to_broadcast([P, 2, TOPK, TOPK]), ALU.mult))
                    after(21)
                    then(V.tensor_reduce(picked.rearrange("p h k -> p (h k)"), hot, AX_X, ALU.add))
                    after(22)
                    then(V.scalar_tensor_tensor(idx_f, picked[:, 0, :], float(NKEYS), picked[:, 1, :], ALU.mult, ALU.add))
                    after(23)
                    V.tensor_copy(idx[:, h % IDX_SLOTS, :], idx_f).then_inc(routed, 1)

                def softmax(n, h):
                    hold(dve, exp_done, n + 1)
                    V.reciprocal(exp_inv, exp_sum).then_inc(route_step, 1)
                    dve.wait_ge(route_step, 24)
                    V.tensor_scalar(gate[:, h % 2, :], exp_s, exp_inv, None, ALU.mult).then_inc(route_step, 1)
                    dve.wait_ge(route_step, 25)

                def dot_products(n, h):
                    for k in range(TOPK):
                        dve.wait_ge(u_loaded[k % SLOTS], n * (16 * TOPK // SLOTS) + 16 * (k // SLOTS + 1))
                        V.tensor_tensor_reduce(u_rows[:, k % SLOTS, :], u_rows[:, k % SLOTS, :], xn, 1.0, 0.0, ALU.mult,
                                               ALU.add, dots[:, h % 2, k:k + 1]).then_inc(u_used, 1)

                def weights(n, h):
                    dve.wait_ge(gelu_done, n + 1)
                    V.tensor_tensor(weight[:, h % 2, :], gelu[:, h % 2, :], gate[:, h % 2, :], ALU.mult).then_inc(weighted, 1)

                def add_output(it, b):
                    dve.wait_ge(v_used, it * (PH * TOPK) + (PH * TOPK + V_CREDIT))
                    if layer == 0:
                        V.tensor_tensor(peer_sum, peer_sum, row_b[:, :], ALU.mult).then_inc(sum_scaled, 1)
                        dve.wait_ge(sum_scaled, it + 1)
                    x = X[:, bass.ds(b, 1), :].rearrange("p a d -> p (a d)")
                    V.tensor_tensor(x, peer_sum, x, ALU.add).then_inc(x_added, 1)

                def head(n, h, more=True, blocks=None):
                    if more:
                        route(n + 1, (h + 1) % PH)
                    if h == 0:
                        hold(dve, xn_ready, blocks)
                    dot_products(n, h)
                    if more:
                        softmax(n + 1, (h + 1) % PH)
                    weights(n, h)

                def token_block(it, b, more):
                    for h in range(1, PH):
                        head(it * PH + h, h, h < PH - 1 or more)
                    if more:
                        head(it * PH + PH, 0, blocks=it + 2)
                    add_output(it, b)

                n0 = layer * TT * PH
                route(n0, 0)
                softmax(n0, 0)
                head(n0, 0, blocks=layer * TT + 1)
                with dve.Fori(0, TT - 1) as b:
                    token_block(b + layer * TT, b, True)
                token_block(TT - 1 + layer * TT, TT - 1, False)

            empty(dve, "g2", 1)
            peer(0)
            dve.wait_ge(x_added, 1 + TT)
            scale_rows(2, x_tiles)
            dve.wait_ge(row_a_in, 32)
            dve.wait_ge(rows_scaled, ROWS_UPTO[2])
            for t in range(TT):
                V.tensor_tensor(X[:, t, :], xr[:, t, :], row_a[:, :], ALU.mult).then_inc(x_new, 1)
            dve.wait_ge(x_new, TT)
            scale_rows(3, x_tiles)
            transposed(2, lambda k: col("g_mix_2", k), None)

            dve.wait_ge(pads_zeroed, 4)
            for j in range(4):
                z, y = z_pad[j % 2], yT2[:, j, :]
                empty(dve, "cc", j)
                o = full(dve, "cv", j)
                V.tensor_tensor(z[:, 1:1 + L], o[:, :], c_gate[:, j % 2, :], ALU.mult).then_inc(emptied["D"], 1)
                empty(dve, "cv", j)
                V.tensor_scalar(y, z[:, 0:L], col("conv_w_2", j), None, ALU.mult).then_inc(conv_step, 1)
                for tap in (1, 2):
                    dve.wait_ge(conv_step, 3 * j + tap)
                    V.scalar_tensor_tensor(y, z[:, tap:tap + L], col("conv_w_2", 4 * tap + j), y, ALU.mult, ALU.add
                                           ).then_inc(conv_step, 1)
                dve.wait_ge(conv_step, 3 * j + 3)
                o = full(dve, "cb", j)
                V.tensor_tensor(y, o[:, :], y, ALU.mult).then_inc(emptied["D"], 1)
            dve.wait_ge(inv_in, 16)
            steps = 0
            for g, w in enumerate(WINDOWS):
                empty(dve, "pu", g)
                src, n, span, dst = u_pad[g % 2], L + 2 * PAD, 1, 0
                while span < w:
                    n -= span
                    V.tensor_tensor(win[dst][:, 0:n], src[:, 0:n], src[:, span:span + n], ALU.add).then_inc(pool_step, 1)
                    steps += 1
                    dve.wait_ge(pool_step, steps)
                    src, dst, span = win[dst], 1 - dst, 2 * span
                y = yT2[:, 4 + g, :]
                V.tensor_tensor(y, src[:, PAD - w // 2:PAD - w // 2 + L], inv_cnt[:, g, :], ALU.mult).then_inc(pool_step, 1)
                steps += 1
                dve.wait_ge(pool_step, steps)
                V.tensor_tensor(y, y, u_pad[g % 2][:, PAD:PAD + L], ALU.subtract).then_inc(pooled, 1)
            for n in range(2):
                for t in range(TT):
                    o, x = full(dve, "wo2", t, n), X[:, t, n * CW:(n + 1) * CW]
                    V.tensor_tensor(x, o[:, :], x, ALU.add).then_inc(emptied["D"], 1)
            empty(dve, "wo2", TT - 1, 1)
            scale_rows(4, x_tiles)
            transposed(3, lambda k: col("g_ffn_2", k), None)
            peer(1)
            dve.wait_ge(x_added, 1 + 2 * TT)
            scale_rows(5, x_tiles)
            transposed(4, lambda k: col("g_ple_2", k), None)
            for u in range(2 * TT):
                t, n = u % TT, u // TT
                empty(dve, "gate", t, n)
                o, x = full(dve, "pp", t, n), X[:, t, n * CW:(n + 1) * CW]
                V.tensor_tensor(o[:, :], o[:, :], ple_gate[:, u % 2, :], ALU.mult).then_inc(ple_mul, 1)
                dve.wait_ge(ple_mul, u + 1)
                V.tensor_tensor(x, o[:, :], x, ALU.add).then_inc(emptied["D"], 1)
            empty(dve, "pp", TT - 1, 1)
            scale_rows(6, x_tiles)
            dve.wait_ge(row_b_in, 32)
            dve.wait_ge(rows_scaled, ROWS_UPTO[6])
            for t in range(TT):
                V.tensor_tensor(xr[:, t, :], xr[:, t, :], row_b[:, :], ALU.mult).then_inc(out_ready, 1)


_INPUTS = ["x", "c", "ctx", "c_ctx", "w_mod", "b_mod", "norm1_w", "norm2_w", "w_in", "ret_decay_f", "ret_decay_b",
           "gla_gk_up_f", "gla_gk_bias_f", "gla_gk_up_b", "gla_gk_bias_b", "w_out", "peer_w_q", "peer_k1", "peer_k2",
           "peer_down", "peer_up", "norm_f_w", "p_2", "g_mix_2", "w_in_2", "conv_w_2", "pool_w_2", "pool_scale_2", "w_o_2",
           "g_ffn_2", "w_q_2", "sub_keys_2", "expert_u_2", "expert_v_2", "g_ple_2", "w_ple_gate_2", "w_ple_proj_2",
           "g_final_2"]


def kernel(**inputs):
    import concourse.bacc as bacc
    from concourse.bass_utils import run_bass_kernel_spmd

    nc = bacc.Bacc("TRN2", target_bir_lowering=False, num_devices=1)
    arrays = {f"in_{n}": np.ascontiguousarray(inputs[n]) for n in _INPUTS}
    arrays["shape_tables"], arrays["inverse_counts"] = shape_constants()
    aps = {n: nc.dram_tensor(n, v.shape, F32, kind="ExternalInput").ap() for n, v in arrays.items()}
    out = nc.dram_tensor("out", (1, L, D), F32, kind="ExternalOutput").ap()
    build(nc, {n: aps[f"in_{n}"] for n in _INPUTS}, aps["shape_tables"], aps["inverse_counts"], out)
    r = run_bass_kernel_spmd(nc, [arrays], core_ids=[0])
    return r.results[0]["out"]
```

```python
import numpy as np
from contextlib import ExitStack

import concourse.bass as bass
from concourse import mybir

P = 128
F32 = mybir.dt.float32
U32 = mybir.dt.uint32
ALU = mybir.AluOpType
ACT = mybir.ActivationFunctionType
AX_X = mybir.AxisListType.X

D = 1024
KT = D // P
L = 512
TT = L // P
LC = 256
TC = LC // P
HEADS = 4
DV = 128
RET_DK = 128
GLA_DK = 64
PAIRS = 2
RANK = 16
GATE_NORM = 16.0
EPS = 1e-6
GRID_W = 64
CW = 512
RING = 3
FWD, BWD = 0, 1
PH = 8
TOPK = 16
NKEYS = 128
PQ = PH * 2 * P
SLOTS = 8
IDX_SLOTS = 4
V_CREDIT = 64
WINDOWS = (2, 4, 8, 16)
PAD = 8
LOWEST = -3.0e38

WIDE = 384 + L + 256
C_IDENT, C_COS, C_SIN = 0, 128, 640
C_AHEAD, C_BEHIND = 1152, 1152 + WIDE
C_TRI = C_BEHIND + 384 + L
TRI_PREFIX, TRI_SUFFIX, TRI_AFTER, TRI_BEFORE, TRI_ONES = range(5)
C_ROT = C_TRI + 5 * 128
C_TWICE = C_ROT + 128
C_IOTA = C_TWICE + 128
N_CONST = C_IOTA + 16

VEC = [("c", 8), ("c_ctx", 8), ("b_mod", 48), ("norm1_w", 8), ("norm2_w", 8), ("g_mix_2", 8),
       ("g_ffn_2", 8), ("g_ple_2", 8), ("conv_w_2", 12), ("pool_scale_2", 4)]
VEC_AT = {}
for _name, _rows in VEC:
    VEC_AT[_name] = sum(r for n, r in VEC[:len(VEC_AT)])
N_VEC = sum(r for _, r in VEC)

W_RQ, W_RK, W_RV, W_RG, W_GQK, W_GV, W_GG, W_LR = 0, 512, 1024, 1536, 2048, 2560, 3072, 3584

CHUNKS = ([("w_mod", CW * i) for i in range(4)]
          + [("w_in", W_RK), ("w_mod", CW * 6), ("w_in", W_RQ), ("w_mod", CW * 7), ("w_in", W_RV), ("w_mod", CW * 8),
             ("w_in", W_GQK), ("w_mod", CW * 9), ("w_in", W_GV), ("w_mod", CW * 4), ("w_in", W_RG), ("w_mod", CW * 5),
             ("w_in", W_GG), ("w_mod", CW * 10), ("w_out", 0), ("w_mod", CW * 11), ("w_out", CW)]
          + [("w_o_2", 0), ("keys_2", 0), ("w_o_2", CW)])


CHUNK_LAST_JOB = {("w_in", W_RK): ("rkc", 1), ("w_in", W_RV): ("rvc", TC - 1), ("w_in", W_RQ): ("rq", HEADS - 1),
                  ("w_in", W_GQK): ("gkc",), ("w_in", W_GV): ("gvc", TC - 1), ("w_in", W_RG): ("rg", 3),
                  ("w_in", W_GG): ("gg", TT - 1), ("keys_2", 0): ("kT", 1, 3)}
CHUNK_LAST_JOB.update({("w_mod", CW * i): ("mod", i) for i in range(4)})
CHUNK_LAST_JOB.update({("w_mod", CW * i): ("modT", i) for i in range(6, 10)})
SUMMED_CHUNKS = (6, 7, 8, 9, 4, 5, 10, 11)
for _n in range(2):
    CHUNK_LAST_JOB.update({("w_mod", CW * (4 + _n)): ("g1", _n), ("w_mod", CW * (10 + _n)): ("g2", _n),
                           ("w_out", CW * _n): ("wo", TT - 1, _n), ("w_o_2", CW * _n): ("wo2", TT - 1, _n)})


def chunk_number(name, col=0):
    return CHUNKS.index((name, col))


def shape_constants():
    p = np.arange(P)[:, None].astype(np.float64)
    c = np.zeros((P, N_CONST), np.float32)
    c[:, C_IDENT:C_IDENT + P] = np.eye(P)
    n_freq = RET_DK // 4
    inv = np.float32(10000.0) ** (-np.arange(n_freq, dtype=np.float32) / np.float32(n_freq))
    t = np.arange(L)
    ang = np.concatenate([(t // GRID_W).astype(np.float32)[:, None] * inv,
                          (t % GRID_W).astype(np.float32)[:, None] * inv], axis=1).astype(np.float64)
    cos, sin = np.cos(ang).T, np.sin(ang).T
    c[:, C_COS:C_COS + L] = np.concatenate([cos, cos])
    c[:, C_SIN:C_SIN + L] = np.concatenate([-sin, sin])
    m = np.arange(WIDE)[None, :]
    c[:, C_AHEAD:C_AHEAD + WIDE] = np.maximum(m - 384 - p, 0)
    c[:, C_BEHIND:C_BEHIND + 384 + L] = np.maximum(p + 384 - m, 0)[:, :384 + L]
    q = np.arange(P)[None, :]
    for i, tri in enumerate([p <= q, p >= q, p > q, p < q, p >= 0]):
        c[:, C_TRI + i * P:C_TRI + (i + 1) * P] = tri
    c[:, C_ROT:C_ROT + P] = (p == (q + 64) % P)
    c[:, C_TWICE:C_TWICE + P] = 1 + np.eye(P)
    c[:, C_IOTA:C_IOTA + 16] = np.arange(16)
    counts = np.zeros((4, L), np.float64)
    for g, w in enumerate(WINDOWS):
        counts[g] = np.clip(t + w // 2, 0, L) - np.clip(t - w // 2, 0, L)
    return c, (1.0 / counts).astype(np.float32)


STATS = ([("n1", t) for t in range(TT)] + [("nf", t) for t in range(TT - 1)] + [("gm", t) for t in range(TT - 1)]
         + [("nf", TT - 1), ("gm", TT - 1)] + [("gf", t) for t in range(TT)] + [("gp", t) for t in range(TT)]
         + [("fin", t) for t in range(TT)])
DIAGS = [s for s in STATS if s[0] not in ("nf", "fin")]


class PsumJobs:

    def __init__(self):
        self.names, self.who, self.rank, self.total = [], [], [], {"A": 0, "D": 0}
        self.bank, self.before, self.turn, self.last_in = [], [], 0, {}

    def add(self, name, who, bank=None):
        if bank is None:
            bank, self.turn = self.turn, (self.turn + 1) % 8
        self.bank.append(bank)
        self.before.append(self.last_in.get(bank))
        self.last_in[bank] = len(self.names)
        self.names.append(name)
        self.who.append(who)
        self.total[who] += 1
        self.rank.append(self.total[who])

    def number(self, *name):
        return self.names.index(name)

    def upto(self, n):
        return {w: sum(x == w for x in self.who[:n]) for w in "AD"}


def plan_jobs():
    jobs = PsumJobs()

    def tile(name, t, banks=(None, None), engines="AD"):
        for half, (who, bank) in enumerate(zip(engines, banks)):
            jobs.add(("nt", name, t, half), who, bank)

    alternate = lambda i: "AD"[i % 2]

    jobs.add(("cols",), "D")
    for c in range(4):
        jobs.add(("mod", c), "D")
        if c >= 1:
            jobs.add(("modT", c - 1), "D")
    jobs.add(("modT", 3), "D")
    for k in range(KT):
        jobs.add(("norm", 0, k), alternate(k))
    for k in range(KT):
        jobs.add(("normc", k), alternate(k))
    for name in ("rk", "rq"):
        for h in range(HEADS):
            jobs.add((name, h), "A")
    jobs.add(("modT", 6), "D")
    for name in ("rkrot", "rqrot"):
        for h in range(HEADS):
            jobs.add((name, h), "D")
    for g in range(2):
        jobs.add(("rkc", g), "A")
    for t in range(TT):
        jobs.add(("rv", t), "A")
    for t in range(TC):
        jobs.add(("rvc", t), "A")
    for c in (7, 8):
        jobs.add(("modT", c), "D")
    for h in range(HEADS):
        for j in range(TT + TC):
            jobs.add(("rs", h, j), "D")
        jobs.add(("ro", h), "A")
    jobs.add(("modT", 9), "D")
    jobs.add(("lr",), "A")
    jobs.add(("lrc",), "A")
    for p in range(PAIRS):
        jobs.add(("gq", p), "A")
    for t in range(TT + TC):
        jobs.add(("la", t), "D")
    for p in range(PAIRS):
        jobs.add(("gk", p), "A")
    jobs.add(("gkc",), "A")
    for t in range(TT):
        jobs.add(("gv", t), alternate(t))
    for t in range(TC):
        jobs.add(("gvc", t), alternate(t))
    jobs.add(("g1", 0), "D")
    for p in range(PAIRS):
        for d in (FWD, BWD):
            jobs.add(("cum", p, d), "D")
            jobs.add(("cumc", p, d), "A")
            jobs.add(("rg", 2 * p + d), "A")
            jobs.add(("kcT", p, d), "A")
            jobs.add(("s0", p, d), "D")
            jobs.add(("kdT", p, d), "A")
            for s in range(TT - 1):
                jobs.add(("up", p, d, s), "D")
    jobs.add(("g1", 1), "D")
    for h in range(HEADS):
        for d in (FWD, BWD):
            jobs.add(("gs", h, d), "A")
    for c in range(TT):
        for odd in range(2):
            jobs.add(("go", c, odd), "A")
    jobs.add(("g2", 0), "D")
    for t in range(TT):
        jobs.add(("gg", t), "A")
    for k in range(KT):
        jobs.add(("yT", k), alternate(k))

    def project_and_normalise(name, keys, norm):
        for n in range(2):
            jobs.add((name, 0, n), "D")
        for g in range(4):
            jobs.add(("kT", keys, g), "A")
        if keys == 0:
            jobs.add(("g2", 1), "D")
        jobs.add((name, 1, 0), "D")
        tile(norm, 0)
        jobs.add((name, 1, 1), "D", 6)
        for t in (2, 3):
            for n in range(2):
                jobs.add((name, t, n), "D", 2 + n)
            tile(norm, t - 1, (6, 7), "AD" if t == 2 else "AA")
        tile(norm, 3, (2, 3), "AA")

    project_and_normalise("wo", 0, "n1")
    for t in range(TT):
        tile("gm", t, (6, 7) if t < TT - 1 else (0, 1))
    for j in range(4):
        jobs.add(("cc", j), "A", 4 + 2 * j if j < 2 else None)
        jobs.add(("cv", j), "D", 5 + 2 * j if j < 2 else None)
    for g in range(4):
        jobs.add(("pu", g), "A")
    for j in range(4):
        jobs.add(("cb", j), "D")
    for g in range(4):
        jobs.add(("py", g), "A")
    project_and_normalise("wo2", 1, "gf")
    for t in range(TT - 1):
        tile("gp", t, (6, 7))

    def gates(t):
        for n in range(2):
            jobs.add(("gate", t, n), "A", (4 if t == 1 else 6) + n)

    def products(t):
        for n in range(2):
            jobs.add(("pp", t, n), "D", (0 if t == 1 else 4) + n)

    gates(0)
    gates(1)
    for k in range(2):
        jobs.add(("pT", k), "A", 6 + k)
    gates(2)
    for t in range(TT - 1):
        products(t)
    tile("gp", TT - 1, (0, 1))
    gates(3)
    products(3)
    return jobs


def build(nc, a, consts, inv_counts, out):
    jobs = plan_jobs()
    with ExitStack() as ctx:
        def sb(name, shape, dt=F32):
            return ctx.enter_context(nc.sbuf_tensor(name, shape, dt))

        def sem(name):
            return ctx.enter_context(nc.semaphore(name))

        X = sb("X", [P, TT, D])
        hT = sb("hT", [P, KT, L])
        ring = sb("ring", [P, RING * KT * CW])
        const = sb("const", [P, N_CONST])
        row_a = sb("row_a", [P, D])
        row_b = sb("row_b", [P, D])
        cols = sb("cols", [P, N_VEC])
        silu = sb("silu", [P, KT, 2])
        mod = sb("mod", [P, 6 * KT, 2])
        gain = sb("gain", [P, 3, KT])
        stat = sb("stat", [P, 4, TT + TC])
        tstat = sb("tstat", [P, 4, TT])
        hstat = sb("hstat", [P, 4, 2 * TT * HEADS])
        lg = sb("lg", [P, 4, 8])
        chunk_dec = sb("chunk_dec", [P, 4, TT])
        SCR = 25600
        scr = sb("scr", [P, SCR])
        banks = ctx.enter_context(nc.psum_tensor("banks", [P, 8 * 512], F32))
        psum = [banks[:, 512 * i:512 * (i + 1)] for i in range(8)]
        xn = banks[:, 0:D]
        peer_sum = banks[:, D:2 * D]

        def at(base, off, *dims):
            n = int(np.prod(dims))
            v = base[:, off:off + n]
            if len(dims) == 1:
                return v
            if len(dims) == 2:
                return v.rearrange("p (a b) -> p a b", b=dims[1])
            return v.rearrange("p (a b c) -> p a b c", b=dims[1], c=dims[2])

        ident = const[:, C_IDENT:C_IDENT + P]
        cos_t, sin_t = const[:, C_COS:C_COS + L], const[:, C_SIN:C_SIN + L]
        rot = const[:, C_ROT:C_ROT + P]

        def tri(i):
            return const[:, C_TRI + i * P:C_TRI + (i + 1) * P]

        def chunk(n):
            return at(ring, (n % RING) * KT * CW, KT, CW)

        xr = at(scr, 0, TT, D)
        xc = at(scr, 8192, TC, D)
        vrows = at(scr, 21504, P)[0:N_VEC, :]
        rqT, rkT = at(scr, 0, HEADS, L), at(scr, 2048, HEADS, L)
        o_ret, o_gla = at(scr, 4096, TT, HEADS * DV), at(scr, 6144, TT, HEADS * DV)
        r_p = at(scr, 8192, TT + TC, L)
        rkTc, rv, rvc = at(scr, 11264, HEADS, LC), at(scr, 12288, TT, 512), at(scr, 14336, TC, 512)
        mask_m = [at(scr, 15360 + 3072 * i, 2, 384 + L) for i in range(2)]
        mask_c = [at(scr, 15360 + 3072 * i + 1792, 2, 640) for i in range(2)]
        rot_tmp = at(scr, 8192, 2, L)
        w_lr = at(scr, 22528, KT, 64)
        gk_up = at(scr, 22016, 512)[0:64, :]
        hTc = at(scr, 23040, KT, LC)
        q_in, k_in = at(scr, 0, 4, L), at(scr, 2048, 4, L)
        gqT, gkT, gkTc = at(scr, 8192, PAIRS, L), at(scr, 9216, PAIRS, L), at(scr, 10240, PAIRS, LC)
        gv, gvc = at(scr, 10752, TT, 512), at(scr, 12800, TC, 512)
        la = at(scr, 13824, TT + TC, 512)
        q_st = at(scr, 16896, 4, L)
        kdT = at(scr, 18944, 4, TT, P)
        state = at(scr, 20992, 4, TT, DV)
        g_p = [at(scr, 13824 + 512 * i, TT, P) for i in range(6)] + [at(scr, 8192 + 512 * i, TT, P) for i in range(2)]
        G = at(const, C_COS, L)
        G_mid, G_last, G_neg = at(const, C_AHEAD, L), at(const, C_AHEAD + 512, L), at(const, C_AHEAD + 1024, L)
        kc_exp, kcT = at(const, C_SIN, LC), at(const, C_SIN + LC, TC, P)
        lrT = at(scr, 18944, 768)[0:64, :]
        la_tmp = at(scr, 0, TT + TC, 512)
        ret_gate = at(scr, 23040, TT, 512)
        ret_sq = at(row_a, 0, 2, 512)
        gate_tmp = at(scr, 8192, 2, 512)
        yT = hT
        sq_tmp = at(scr, 9216, 2, 512)
        mod_rows = at(row_b, 0, 2, CW)[0:2]
        raw_keys = at(scr, 4096, PH, 2, P)
        u_rows = at(scr, 0, SLOTS, D)
        v_rows = [at(ring, D * k if k < SLOTS // 2 else 2 * KT * CW + D * (k - SLOTS // 2), D) for k in range(SLOTS)]
        w_q = at(scr, 8192, KT, PQ)
        diag = at(ring, KT * CW, TOPK, P)
        peer_qT = at(ring, KT * CW + 2048, 2, 2, P)
        x_cur = at(ring, KT * CW + 2560, KT, P)
        onehot = at(ring, KT * CW + 3584, 2, TOPK, TOPK)
        kT = at(const, C_AHEAD, 2 * PH, P)
        score = at(const, C_COS, 2, 2, NKEYS)
        score_rest = at(const, C_COS + 512, 2, NKEYS)
        cand = at(const, C_COS + 768, TOPK, TOPK)
        cand_rest = at(scr, 24576, TOPK * TOPK)
        o = 24832
        top1 = at(scr, o, 2, TOPK)
        key_f = at(scr, o + 32, 2, TOPK)
        top2 = at(scr, o + 64, TOPK)
        neg_max = at(scr, o + 80, 1)
        exp_s = at(scr, o + 96, TOPK)
        exp_sum = at(scr, o + 112, 1)
        exp_inv = at(scr, o + 113, 1)
        gate = at(scr, o + 128, 2, TOPK)
        picked = at(scr, o + 160, 2, TOPK)
        idx_f = at(scr, o + 192, TOPK)
        dots = at(scr, o + 208, 2, TOPK)
        gelu = at(scr, o + 240, 2, TOPK)
        weight = at(scr, o + 272, 2, TOPK)
        tile_diag = at(scr, o + 384, 3, P)
        key_i = sb("key_i", [P, 2, TOPK], U32)
        pos_i = sb("pos_i", [P, TOPK], U32)
        pos_ab = sb("pos_ab", [P, 2, TOPK], U32)
        idx = sb("idx", [P, IDX_SLOTS, TOPK], U32)
        mix = at(scr, 4096, KT, L)
        w_in_2 = w_q
        z_pad = [at(scr, 514 * i, 514) for i in range(2)]
        u_pad = [at(scr, 1028 + 528 * i, 528) for i in range(2)]
        win = [at(scr, 2084 + 528 * i, 528) for i in range(2)]
        c_gate = at(const, C_COS, 2, L)
        inv_cnt = at(const, C_AHEAD, 4, L)
        pool_w = at(scr, 24576, 4, P)
        w_ple, w_proj = w_q[:, :, 0:D], w_q[:, 0:2, D:2 * D]
        p_rows = w_q[:, 2, D:2 * D].rearrange("p (t d) -> p t d", d=256)
        pT = w_q[:, 3, D:2 * D].rearrange("p (k t) -> p k t", t=L)
        ple_gate = w_q[:, 4:8, D:2 * D].rearrange("p t (n c) -> p t n c", c=CW)

        def col(name, k, n=1):
            return cols[:, VEC_AT[name] + k:VEC_AT[name] + k + n]

        bank_ready = sem("bank_ready")
        emptied = {"A": sem("act_emptied"), "D": sem("dve_emptied")}
        ident_in, const_in, vec_in, x_in, ctx_in, lg_in = sem("ident_in"), sem("const_in"), sem("vec_in"), sem("x_in"), sem("ctx_in"), sem("lg_in")
        lr_in, row_a_in, row_b_in = sem("lr_in"), sem("row_a_in"), sem("row_b_in")
        gap_zeroed = sem("gap_zeroed")
        chunk_in = [sem(f"chunk_in{i}") for i in range(RING)]
        w_q_in, w_mix_in, w_proj_in, inv_in, pool_w_in, p_in, out_done = (sem("w_q_in"), sem("w_mix_in"), sem("w_proj_in"), sem("inv_in"), sem("pool_w_in"), sem("p_in"),
                                                     sem("out_done"))
        silu_done, mod_step, mod_sum, gains_done, keys_in = sem("silu_done"), sem("mod_step"), sem("mod_sum"), sem("gains_done"), sem("keys_in")
        sumsq, meansq, root, rstd, rows_scaled = sem("sumsq"), sem("meansq"), sem("root"), sem("rstd"), sem("rows_scaled")
        t_sq, t_mean, t_root, t_rstd, t_diag = sem("t_sq"), sem("t_mean"), sem("t_root"), sem("t_rstd"), sem("t_diag")
        x_new = sem("x_new")
        rotating, roped = sem("rotating"), sem("roped")
        lg_act, lg_step = sem("lg_act"), sem("lg_step")
        exps, mask_step = sem("exps"), sem("mask_step")
        ones_set = sem("ones_set")
        la_abs, la_exp, la_ln, la_done = sem("la_abs"), sem("la_exp"), sem("la_ln"), sem("la_done")
        rg_silu = sem("rg_silu")
        g_sub, g_exp, g_mul, kc_mul = sem("g_sub"), sem("g_exp"), sem("g_mul"), sem("kc_mul")
        state_half, p_masked = sem("state_half"), sem("p_masked")
        head_step, head_root, y_step, y_done = sem("head_step"), sem("head_root"), sem("y_step"), sem("y_done")
        wo_mul = sem("wo_mul")
        pads_zeroed, conv_step, pool_step, pooled = sem("pads_zeroed"), sem("conv_step"), sem("pool_step"), sem("pooled")
        ple_mul, out_ready = sem("ple_mul"), sem("out_ready")
        u_loaded = [sem(f"u_loaded{i}") for i in range(SLOTS)]
        v_loaded = [sem(f"v_loaded{i}") for i in range(SLOTS)]
        u_used = sem("u_used")
        v_used = sem("v_used")
        x_cur_set, xn_ready = sem("x_cur_set"), sem("xn_ready")
        q_done, q_copied, s_done, s_copied = sem("q_done"), sem("q_copied"), sem("s_done"), sem("s_copied")
        topped = sem("topped")
        exp_done, gelu_done, weighted = sem("exp_done"), sem("gelu_done"), sem("weighted")
        routed = sem("routed")
        diag_set = sem("diag_set")
        x_added = sem("x_added")
        route_step = sem("route_step")
        sum_scaled = sem("sum_scaled")
        passed = sem("passed")

        def full(eng, *name):
            n = jobs.number(*name)
            eng.wait_ge(bank_ready, n + 1)
            return psum[jobs.bank[n]]

        def empty(eng, *name):
            n = jobs.number(*name)
            eng.wait_ge(emptied[jobs.who[n]], jobs.rank[n])

        def all_empty(eng, *last):
            for w, n in jobs.upto(jobs.number(*last) + 1).items():
                eng.wait_ge(emptied[w], n)

        def chunk_read(eng, n):
            eng.wait_ge(bank_ready, jobs.number(*CHUNK_LAST_JOB[CHUNKS[n]]) + 1)

        def hold(eng, s, value):
            eng.wait_ge(s, value)
            eng.sem_inc(passed, 1)

        block = ctx.enter_context(nc.Block())

        @block.sync
        def _(sp):
            wide = {"w_mod": a["w_mod"][0], "w_in": a["w_in"][0], "w_out": a["w_out"][0],
                    "w_o_2": a["w_o_2"][0]}

            def load_chunk(n):
                name, c0 = CHUNKS[n]
                if n >= RING:
                    chunk_read(sp, n - RING)
                s = chunk_in[n % RING]
                if name in wide:
                    sp.dma_start(chunk(n), wide[name].rearrange("(k p) n -> p k n", p=P)[:, :, c0:c0 + CW]).then_inc(s, 16)
                else:
                    raw = at(ring, (n % RING) * KT * CW, 2 * PH, P)
                    sp.dma_start(raw, a["sub_keys_2"][0].rearrange("h s n d -> n (h s) d")).then_inc(s, 16)

            for name, rows in VEC:
                src = a[name]
                dims = " ".join("abcd"[:len(src.shape)])
                flat = src.rearrange(f"{dims} -> ({dims})") if len(src.shape) > 1 else src
                sp.dma_start(vrows[VEC_AT[name]:VEC_AT[name] + rows, :],
                             flat.rearrange("(r p) -> r p", p=P)).then_inc(vec_in, 16)
            sp.dma_start(ident, consts[:, C_IDENT:C_IDENT + P]).then_inc(ident_in, 16)
            for n in range(RING):
                load_chunk(n)
            sp.dma_start(X[:, :, :], a["x"][0].rearrange("(t p) d -> p t d", p=P)).then_inc(x_in, 16)
            sp.dma_start(xc, a["ctx"][0].rearrange("(t p) d -> p t d", p=P)).then_inc(ctx_in, 16)
            sp.dma_start(lg[:, 0, 0:4], a["ret_decay_f"][0].partition_broadcast(P)).then_inc(lg_in, 16)
            sp.dma_start(lg[:, 0, 4:8], a["ret_decay_b"][0].partition_broadcast(P)).then_inc(lg_in, 16)
            load_chunk(3)
            sp.dma_start(const[:, P:], consts[:, P:]).then_inc(const_in, 16)
            load_chunk(4)
            sp.wait_ge(gap_zeroed, 2)
            for d in (FWD, BWD):
                sp.dma_start(w_lr[:, :, 32 * d:32 * d + RANK],
                             a["w_in"][0].rearrange("(k p) n -> p k n", p=P)[:, :, W_LR + RANK * d:W_LR + RANK * (d + 1)]
                             ).then_inc(lr_in, 16)
                up, bias = (a["gla_gk_up_f"], a["gla_gk_bias_f"]) if d == FWD else (a["gla_gk_up_b"], a["gla_gk_bias_b"])
                sp.dma_start(gk_up[32 * d:32 * d + RANK, 256 * d:256 * (d + 1)], up[0]).then_inc(lr_in, 16)
                sp.dma_start(gk_up[32 * d + RANK:32 * d + RANK + 1, 256 * d:256 * (d + 1)], bias).then_inc(lr_in, 16)
            for n in (5, 6, 8, 7):
                load_chunk(n)
            for n in range(9, chunk_number("w_in", W_RG) + 1):
                load_chunk(n)
            sp.wait_ge(head_step, 2 * TT)
            sp.dma_start(row_a[:, :], a["b_mod"][0, 2 * D:3 * D].partition_broadcast(P)).then_inc(row_a_in, 16)
            sp.dma_start(row_b[:, :], a["b_mod"][0, 5 * D:6 * D].partition_broadcast(P)).then_inc(row_b_in, 16)
            for n in range(chunk_number("w_mod", CW * 5), chunk_number("w_out") + 1):
                load_chunk(n)
            load_chunk(chunk_number("w_out", CW))
            load_chunk(chunk_number("w_mod", CW * 11))
            full(sp, "yT", KT - 1)
            sp.dma_start(raw_keys[:, :, 0, :], a["peer_k1"][0].rearrange("h n d -> n h d")).then_inc(keys_in, 16)
            sp.dma_start(raw_keys[:, :, 1, :], a["peer_k2"][0].rearrange("h n d -> n h d")).then_inc(keys_in, 16)
            sp.dma_start(w_q, a["peer_w_q"][0].rearrange("(k p) n -> p k n", p=P)).then_inc(w_q_in, 16)
            all_empty(sp, "wo", TT - 1, 1)
            sp.dma_start(row_a[:, :], a["norm_f_w"].partition_broadcast(P)).then_inc(row_a_in, 16)

            sp.wait_ge(q_done, TT * PH - PH // 2)
            w_in_2_rows = a["w_in_2"][0].rearrange("(k p) n -> p k n", p=P)
            sp.dma_start(w_in_2[:, :, 0:2 * CW], w_in_2_rows[:, :, CW:3 * CW]).then_inc(w_q_in, 16)
            sp.wait_ge(x_added, 1 + TT)
            for g, source in ((2, 3), (3, 0)):
                sp.dma_start(w_in_2[:, :, g * CW:(g + 1) * CW], w_in_2_rows[:, :, source * CW:(source + 1) * CW]
                             ).then_inc(w_mix_in, 16)
            sp.dma_start(inv_cnt, inv_counts.partition_broadcast(P)).then_inc(inv_in, 16)
            sp.dma_start(pool_w, a["pool_w_2"][0].rearrange("g c d -> c g d")).then_inc(pool_w_in, 16)
            for n in range(chunk_number("w_o_2"), len(CHUNKS)):
                load_chunk(n)
            sp.dma_start(row_b[:, :], a["g_final_2"].partition_broadcast(P)).then_inc(row_b_in, 16)
            full(sp, "cb", 3)
            sp.dma_start(w_q, a["w_q_2"][0].rearrange("(k p) n -> p k n", p=P)).then_inc(w_q_in, 16)
            sp.wait_ge(q_done, 2 * TT * PH - PH // 2)
            sp.dma_start(w_ple, a["w_ple_gate_2"][0].rearrange("(k p) n -> p k n", p=P)).then_inc(w_q_in, 16)
            sp.wait_ge(q_done, 2 * TT * PH)
            sp.dma_start(p_rows, a["p_2"][0, 0].rearrange("(t p) d -> p t d", p=P)).then_inc(p_in, 16)
            sp.dma_start(w_proj, a["w_ple_proj_2"][0].rearrange("(k p) n -> p k n", p=P)).then_inc(w_proj_in, 16)
            for t in range(TT):
                sp.wait_ge(out_ready, t + 1)
                sp.dma_start(out[0, t * P:(t + 1) * P, :], X[:, t, :]).then_inc(out_done, 16)
            sp.wait_ge(out_done, 16 * TT)

        @block.gpsimd
        def _(pool):
            nc.gpsimd.memset(w_lr[:, :, :], 0.0).then_inc(gap_zeroed, 1)
            nc.gpsimd.memset(gk_up, 0.0).then_inc(gap_zeroed, 1)

            def sum_chunks(which):
                for c in which:
                    n, i = chunk_number("w_mod", CW * c), SUMMED_CHUNKS.index(c)
                    pool.wait_ge(chunk_in[n % RING], 16 * (n // RING + 1))
                    w = chunk(n)
                    nc.gpsimd.tensor_tensor(w, w, silu[:, :, 0:1].to_broadcast([P, KT, CW]), ALU.mult).then_inc(mod_step, 1)
                    for step, half in enumerate((4, 2, 1)):
                        pool.wait_ge(mod_step, 3 * i + step + 1)
                        nc.gpsimd.tensor_tensor(w[:, 0:half, :], w[:, 0:half, :], w[:, half:2 * half, :], ALU.add
                                                ).then_inc(mod_step if half > 1 else mod_sum, 1)

            pool.wait_ge(silu_done, 1)
            sum_chunks(SUMMED_CHUNKS[:6])
            for h in range(HEADS):
                for d in (FWD, BWD):
                    empty(pool, "gs", h, d)
                    v = g_p[2 * h + d]
                    sign = 1 if d == FWD else -1
                    nc.gpsimd.affine_select(out=v, in_=v, pattern=[[0, TT], [sign, P]], compare_op=ALU.is_ge, fill=0.0,
                                            base=0, channel_multiplier=-sign).then_inc(p_masked, 1)

            sum_chunks(SUMMED_CHUNKS[6:])

            def gathers(layer, table_u, table_v, last_projection):
                def u_gather(n, h, k):
                    hold(pool, u_used, n * TOPK + (k + 1))
                    nc.gpsimd.indirect_dma_start(u_rows[:, k % SLOTS, :], None, table_u,
                                                 bass.IndirectOffsetOnAxis(idx[:, h % IDX_SLOTS, k:k + 1], 0)
                                                 ).then_inc(u_loaded[k % SLOTS], 16)

                def v_gather(n, h, k):
                    hold(pool, v_used, n * TOPK + (k + 1 - SLOTS + V_CREDIT))
                    nc.gpsimd.indirect_dma_start(v_rows[k % SLOTS], None, table_v,
                                                 bass.IndirectOffsetOnAxis(idx[:, h % IDX_SLOTS, k:k + 1], 0)
                                                 ).then_inc(v_loaded[k % SLOTS], 16)

                def token_block(first, more):
                    for h in range(PH):
                        u_too = h < PH - 1 or more
                        if u_too:
                            hold(pool, routed, first + (h + 4))
                        for k in range(TOPK):
                            if u_too:
                                u_gather(first + (h + 1), (h + 1) % PH, k)
                            v_gather(first + h, h, k)

                n0 = layer * TT * PH
                pool.wait_ge(routed, n0 + 3)
                for k in range(TOPK):
                    u_gather(n0, 0, k)
                full(pool, *last_projection)
                with pool.Fori(0, TT - 1) as b:
                    token_block(b * PH + n0, True)
                token_block(n0 + (TT - 1) * PH, False)

            gathers(0, a["peer_down"][0], a["peer_up"][0], ("wo", TT - 1, 1))
            pool.wait_ge(u_used, TT * PH * TOPK + SLOTS)
            for i in range(2):
                nc.gpsimd.memset(z_pad[i], 0.0).then_inc(pads_zeroed, 1)
                nc.gpsimd.memset(u_pad[i], 0.0).then_inc(pads_zeroed, 1)
            gathers(1, a["expert_u_2"][0], a["expert_v_2"][0], ("wo2", TT - 1, 1))

        @block.tensor
        def _(pe):
            state_pe = {"job": 0}

            def begin(*name):
                n = state_pe["job"]
                assert jobs.names[n] == name, (jobs.names[n], name)
                state_pe["job"] += 1
                if jobs.before[n] is not None:
                    empty(pe, *jobs.names[jobs.before[n]])
                return psum[jobs.bank[n]]

            def mm(o, lhsT, rhs, i, n):
                return nc.tensor.matmul(o, lhsT, rhs, start=(i == 0), stop=(i == n - 1))

            def use_chunk(name, c0):
                n = chunk_number(name, c0)
                pe.wait_ge(chunk_in[n % RING], 16 * (n // RING + 1))
                return chunk(n)

            def tile_rows(name, t):
                i = DIAGS.index((name, t))
                pe.wait_ge(t_diag, i + 1)
                for half in range(2):
                    o = begin("nt", name, t, half)
                    for k in range(4):
                        c0 = (4 * half + k) * P
                        last = mm(o[:, k * P:(k + 1) * P], X[:, t, c0:c0 + P], tile_diag[:, i % 3, :], 0, 1)
                    last.then_inc(bank_ready, 1)

            def to_rows(names, src, w, tiles):
                for name, t in zip(names, range(tiles)):
                    o = begin(*name)
                    for k in range(KT):
                        last = mm(o[:, :], src[:, k, t * P:(t + 1) * P], w[:, k, :], k, KT)
                    last.then_inc(bank_ready, 1)

            def to_cols(names, src, w, n):
                for j, name in enumerate(names):
                    o = begin(*name)
                    for k in range(KT):
                        last = mm(o[:, 0:n], w[:, k, j * P:(j + 1) * P], src[:, k, :], k, KT)
                    last.then_inc(bank_ready, 1)

            pe.sem_inc(v_used, V_CREDIT)

            pe.wait_ge(vec_in, 16 * len(VEC))
            pe.wait_ge(ident_in, 16)
            o = begin("cols")
            nc.tensor.transpose(o[:, 0:N_VEC], vrows[:, :], ident[0:N_VEC, 0:N_VEC]).then_inc(bank_ready, 1)

            def modulation(c):
                w = use_chunk("w_mod", CW * c)
                o = begin("mod", c)
                for k in range(KT):
                    last = mm(o[0:2, :], silu[:, k, :], w[:, k, :], k, KT)
                last.then_inc(bank_ready, 1)

            def modulation_cols(c):
                o = begin("modT", c)
                empty(pe, "mod", c)
                for j in range(4):
                    last = nc.tensor.transpose(o[:, 2 * j:2 * j + 2], mod_rows[:, c % 2, j * P:(j + 1) * P], ident[0:2, 0:2])
                last.then_inc(bank_ready, 1)

            def summed(c):
                pe.wait_ge(mod_sum, SUMMED_CHUNKS.index(c) + 1)
                return chunk(chunk_number("w_mod", CW * c))[:, 0, :]

            def summed_cols(c):
                o, w = begin("modT", c), summed(c)
                for j in range(4):
                    last = mm(o[:, j:j + 1], w[:, j * P:(j + 1) * P], tri(TRI_ONES)[:, 0:1], 0, 1)
                last.then_inc(bank_ready, 1)

            def gate_row(name, n, c):
                o = begin(name, n)
                mm(o[:, :], tri(TRI_ONES), summed(c), 0, 1).then_inc(bank_ready, 1)

            pe.wait_ge(silu_done, 1)
            for c in range(4):
                modulation(c)
                if c >= 1:
                    modulation_cols(c - 1)
            modulation_cols(3)

            pe.wait_ge(rows_scaled, TT + TC)
            for k in range(KT):
                o = begin("norm", 0, k)
                for t in range(TT):
                    last = nc.tensor.transpose(o[:, t * P:(t + 1) * P], xr[:, t, k * P:(k + 1) * P], ident)
                last.then_inc(bank_ready, 1)
            for k in range(KT):
                o = begin("normc", k)
                for t in range(TC):
                    last = nc.tensor.transpose(o[:, t * P:(t + 1) * P], xc[:, t, k * P:(k + 1) * P], ident)
                last.then_inc(bank_ready, 1)

            pe.wait_ge(const_in, 16)
            w = use_chunk("w_in", W_RK)
            empty(pe, "norm", 0, KT - 2)
            empty(pe, "norm", 0, KT - 1)
            to_cols([("rk", h) for h in range(HEADS)], hT, w, L)
            to_cols([("rq", h) for h in range(HEADS)], hT, use_chunk("w_in", W_RQ), L)
            summed_cols(6)

            def rotate(name, src):
                for h in range(HEADS):
                    o = begin(name + "rot", h)
                    empty(pe, name, h)
                    mm(o[:, :], rot, src[:, h, :], 0, 1).then_inc(bank_ready, 1)

            rotate("rk", rkT)
            rotate("rq", rqT)
            empty(pe, "normc", KT - 2)
            empty(pe, "normc", KT - 1)
            for g in range(2):
                o = begin("rkc", g)
                for j in range(2):
                    for k in range(KT):
                        last = mm(o[:, j * LC:(j + 1) * LC], w[:, k, (2 * g + j) * P:(2 * g + j + 1) * P], hTc[:, k, :], k, KT)
                last.then_inc(bank_ready, 1)
            w = use_chunk("w_in", W_RV)
            to_rows([("rv", t) for t in range(TT)], hT, w, TT)
            to_rows([("rvc", t) for t in range(TC)], hTc, w, TC)
            summed_cols(7)
            summed_cols(8)

            empty(pe, "rvc", TC - 1)
            empty(pe, "rkc", 1)
            pe.wait_ge(roped, 2 * HEADS)
            for h in range(HEADS):
                for j in range(TT + TC):
                    o = begin("rs", h, j)
                    keys = rkT[:, h, j * P:(j + 1) * P] if j < TT else rkTc[:, h, (j - TT) * P:(j - TT + 1) * P]
                    mm(o[:, :], keys, rqT[:, h, :], 0, 1).then_inc(bank_ready, 1)
                o = begin("ro", h)
                empty(pe, "rs", h, TT + TC - 1)
                for t in range(TT):
                    for j in range(TT + TC):
                        vals = rv[:, j, h * DV:(h + 1) * DV] if j < TT else rvc[:, j - TT, h * DV:(h + 1) * DV]
                        last = mm(o[:, t * P:(t + 1) * P], r_p[:, j, t * P:(t + 1) * P], vals, j, TT + TC)
                last.then_inc(bank_ready, 1)

            summed_cols(9)
            pe.wait_ge(lr_in, 16 * 6)
            for name, src, n in (("lr", hT, L), ("lrc", hTc, LC)):
                o = begin(name)
                for k in range(KT):
                    last = mm(o[0:64, 0:n], w_lr[:, k, :], src[:, k, :], k, KT)
                last.then_inc(bank_ready, 1)
            w = use_chunk("w_in", W_GQK)
            to_cols([("gq", p) for p in range(PAIRS)], hT, w, L)
            empty(pe, "lr")
            empty(pe, "lrc")
            for t in range(TT + TC):
                o = begin("la", t)
                mm(o[:, :], lrT[:, t * P:(t + 1) * P], gk_up, 0, 1).then_inc(bank_ready, 1)
            to_cols([("gk", p) for p in range(PAIRS)], hT, w[:, :, PAIRS * P:], L)
            o = begin("gkc")
            for p in range(PAIRS):
                for k in range(KT):
                    last = mm(o[:, p * LC:(p + 1) * LC], w[:, k, (PAIRS + p) * P:(PAIRS + p + 1) * P], hTc[:, k, :], k, KT)
            last.then_inc(bank_ready, 1)
            w = use_chunk("w_in", W_GV)
            to_rows([("gv", t) for t in range(TT)], hT, w, TT)
            to_rows([("gvc", t) for t in range(TC)], hTc, w, TC)
            gate_row("g1", 0, 4)

            w_rg = use_chunk("w_in", W_RG)
            pe.wait_ge(la_done, 2)
            empty(pe, "gvc", 0)
            empty(pe, "gvc", 1)
            for p in range(PAIRS):
                for d in (FWD, BWD):
                    i = 2 * p + d
                    f = slice(d * 256 + p * P, d * 256 + (p + 1) * P)
                    o = begin("cum", p, d)
                    for c in range(TT):
                        last = mm(o[:, c * P:(c + 1) * P], la[:, c, f], tri(TRI_PREFIX if d == FWD else TRI_SUFFIX), 0, 1)
                    last.then_inc(bank_ready, 1)
                    o = begin("cumc", p, d)
                    own = tri(TRI_AFTER if d == FWD else TRI_BEFORE)
                    for t in range(TC):
                        other = t == (0 if d == FWD else TC - 1)
                        last = mm(o[:, t * P:(t + 1) * P], la[:, TT + t, f], own, 0, 1 + other)
                        if other:
                            last = mm(o[:, t * P:(t + 1) * P], la[:, TT + 1 - t, f], tri(TRI_ONES), 1, 2)
                    last.then_inc(bank_ready, 1)
                    o = begin("rg", i)
                    for k in range(KT):
                        last = mm(o[:, :], hT[:, k, i * P:(i + 1) * P], w_rg[:, k, :], k, KT)
                    last.then_inc(bank_ready, 1)
                    o = begin("kcT", p, d)
                    pe.wait_ge(kc_mul, i + 1)
                    for t in range(TC):
                        last = nc.tensor.transpose(o[:, t * P:(t + 1) * P], kc_exp[:, t * P:(t + 1) * P], ident)
                    last.then_inc(bank_ready, 1)
                    o = begin("s0", p, d)
                    empty(pe, "kcT", p, d)
                    for t in range(TC):
                        last = mm(o[:, 0:256], kcT[:, t, :], gvc[:, t, p * 256:(p + 1) * 256], t, TC)
                    last.then_inc(bank_ready, 1)
                    o = begin("kdT", p, d)
                    pe.wait_ge(g_mul, 4 * (i + 1))
                    for c in range(TT):
                        last = nc.tensor.transpose(o[:, c * P:(c + 1) * P], G_last[:, c * P:(c + 1) * P], ident)
                    last.then_inc(bank_ready, 1)
                    empty(pe, "kdT", p, d)
                    for s in range(TT - 1):
                        o = begin("up", p, d, s)
                        c = s if d == FWD else TT - 1 - s
                        mm(o[:, 0:256], kdT[:, i, c, :], gv[:, c, p * 256:(p + 1) * 256], 0, 1).then_inc(bank_ready, 1)
            gate_row("g1", 1, 5)
            for h in range(HEADS):
                for d in (FWD, BWD):
                    o = begin("gs", h, d)
                    i, r = 2 * (h // 2) + d, slice(64 * (h % 2), 64 * (h % 2) + 64)
                    for c in range(TT):
                        cs = slice(c * P, (c + 1) * P)
                        last = mm(o[:, cs], k_in[r, i, cs], q_in[r, i, cs], 0, 1)
                    last.then_inc(bank_ready, 1)
            pe.wait_ge(p_masked, 2 * HEADS)
            empty(pe, "up", 1, BWD, TT - 2)
            for c in range(TT):
                cs = slice(c * P, (c + 1) * P)
                for odd in range(2):
                    o = begin("go", c, odd)
                    r = slice(64 * odd, 64 * odd + 64)
                    for p in range(PAIRS):
                        h, oh = 2 * p + odd, o[:, p * DV:(p + 1) * DV]
                        for d in (FWD, BWD):
                            mm(oh, g_p[2 * h + d][:, c, :], gv[:, c, h * DV:(h + 1) * DV], 2 * d, 4)
                            last = mm(oh, q_st[r, 2 * p + d, cs], state[r, 2 * p + d, c, :], 2 * d + 1, 4)
                    last.then_inc(bank_ready, 1)

            gate_row("g2", 0, 10)
            w = use_chunk("w_in", W_GG)
            to_rows([("gg", t) for t in range(TT)], hT, w, TT)


            for k in range(KT):
                o = begin("yT", k)
                pe.wait_ge(y_done, 1 if k < HEADS else 1 + TT)
                src = o_ret if k < HEADS else o_gla
                for t in range(TT):
                    last = nc.tensor.transpose(o[:, t * P:(t + 1) * P], src[:, t, (k % HEADS) * P:(k % HEADS + 1) * P], ident)
                last.then_inc(bank_ready, 1)
            def project(name, t, w, halves=(0, 1)):
                for n in halves:
                    o = begin(name, t, n)
                    for k in range(KT):
                        last = mm(o[:, :], yT[:, k, t * P:(t + 1) * P], w[n][:, k, :], k, KT)
                    last.then_inc(bank_ready, 1)

            def keys(layer, raw):
                for g in range(4):
                    o = begin("kT", layer, g)
                    for j in range(4):
                        last = nc.tensor.transpose(o[:, j * P:(j + 1) * P], raw[:, 4 * g + j, :], ident)
                    last.then_inc(bank_ready, 1)

            def peer(layer, raw_keys, name, w, norm, beside):
                def scores(n, h, first=False):
                    q, s = psum[4 + h % 2][:, 0:2 * P], psum[4 + h % 2][:, 2 * P:4 * P]
                    if not first:
                        pe.wait_ge(s_copied, n - 1)
                    for half in range(2):
                        for k in range(KT):
                            c0 = (2 * h + half) * P
                            last = mm(q[:, half * P:(half + 1) * P], w_q[:, k, c0:c0 + P], x_cur[:, k, :], k, KT)
                    last.then_inc(q_done, 1)
                    pe.wait_ge(q_copied, n + 1)
                    for half in range(2):
                        last = mm(s[:, half * P:(half + 1) * P], peer_qT[:, h % 2, half, :], kT[:, 2 * h + half, :], 0, 1)
                    last.then_inc(s_done, 1)

                def block_rows():
                    for k in range(KT):
                        last = nc.tensor.transpose(psum[k // 4][:, (k % 4) * P:(k % 4 + 1) * P], x_cur[:, k, :], ident)
                    last.then_inc(xn_ready, 1)

                def add_up(n, h):
                    for k in range(TOPK):
                        pe.wait_ge(diag_set, n * TOPK + (k + 1))
                        pe.wait_ge(v_loaded[k % SLOTS], n * (16 * TOPK // SLOTS) + 16 * (k // SLOTS + 1))
                        for c in range(2):
                            last = nc.tensor.matmul(psum[2 + c][:, :], diag[:, k, :], v_rows[k % SLOTS][:, c * CW:(c + 1) * CW],
                                                    start=(h == 0 and k == 0), stop=(h == PH - 1 and k == TOPK - 1))
                        last.then_inc(v_used, 1)

                def token_block(it, more, beside={}):
                    for h in range(PH):
                        if h == PH - 2 and more:
                            pe.wait_ge(x_cur_set, it + 2)
                        if h < PH - 2 or more:
                            scores(it * PH + (h + 2), (h + 2) % PH)
                        if h == 0:
                            pe.wait_ge(x_added, it + 1)
                        if h == PH - 1 and more:
                            pe.wait_ge(u_used, it * (PH * TOPK) + (PH * TOPK + SLOTS))
                            block_rows()
                        add_up(it * PH + h, h)
                        if h in beside:
                            beside[h]()

                project(name, 0, w)
                if layer == 0:
                    pe.wait_ge(keys_in, 32)
                else:
                    use_chunk("keys_2", 0)
                keys(layer, raw_keys)
                if layer == 0:
                    gate_row("g2", 1, 11)
                project(name, 1, w, (0,))
                tile_rows(norm, 0)
                all_empty(pe, "nt", norm, 0, 1)
                pe.wait_ge(w_q_in, 16 * (2 * layer + 1))
                pe.wait_ge(x_cur_set, layer * TT + 1)
                scores(layer * TT * PH, 0, first=True)
                block_rows()
                scores(layer * TT * PH + 1, 1, first=True)
                project(name, 1, w, (1,))
                for t in (2, 3):
                    project(name, t, w)
                    tile_rows(norm, t - 1)
                tile_rows(norm, 3)
                all_empty(pe, "nt", norm, 3, 1)
                with pe.Fori(0, TT - 1) as b:
                    token_block(b + layer * TT, True)
                token_block(TT - 1 + layer * TT, False, beside)

            w = [use_chunk("w_out", CW * n) for n in range(2)]
            empty(pe, "yT", KT - 2)
            empty(pe, "yT", KT - 1)
            def mix_products(o, c0, tokens):
                for k in range(KT):
                    last = mm(o[:, tokens], w_in_2[:, k, c0:c0 + P], hT[:, k, tokens], k, KT)
                return last

            def mix_cols(name, j, c0):
                o = begin(name, j)
                mix_products(o, c0 + j * P, slice(0, L)).then_inc(bank_ready, 1)

            early, late = slice(0, L - P), slice(L - P, L)
            begun = [("cc", 0, 0), ("cv", 0, CW), ("cc", 1, P), ("cv", 1, CW + P)]

            def early_products(which):
                pe.wait_ge(w_q_in, 32)
                pe.wait_ge(s_copied, TT * PH)
                empty(pe, "nt", "gm", TT - 2, 0)
                empty(pe, "nt", "gm", TT - 2, 1)
                for name, j, c0 in which:
                    mix_products(psum[jobs.bank[jobs.number(name, j)]], c0, early)

            beside = {2 + t: (lambda t=t: tile_rows("gm", t)) for t in range(TT - 1)}
            beside[PH - 3] = lambda: early_products(begun[:2])
            beside[PH - 1] = lambda: early_products(begun[2:])
            peer(0, raw_keys.rearrange("p h s d -> p (h s) d"), "wo", w, "n1", beside)
            tile_rows("gm", TT - 1)
            all_empty(pe, "nt", "gm", TT - 1, 1)
            for name, j, c0 in begun:
                mix_products(begin(name, j), c0, late).then_inc(bank_ready, 1)
            pe.wait_ge(x_added, 1 + TT)
            for j in range(2, 4):
                mix_cols("cc", j, 0)
                mix_cols("cv", j, CW)
            pe.wait_ge(w_mix_in, 32)
            for g in range(4):
                mix_cols("pu", g, 2 * CW)
            for j in range(4):
                mix_cols("cb", j, 3 * CW)
            pe.wait_ge(pool_w_in, 16)
            for g in range(4):
                o = begin("py", g)
                pe.wait_ge(pooled, g + 1)
                mm(o[:, :], pool_w[:, g, :], mix[:, 4 + g, :], 0, 1).then_inc(bank_ready, 1)
            empty(pe, "cb", 3)
            empty(pe, "py", 3)
            w = [use_chunk("w_o_2", CW * n) for n in range(2)]

            def p_cols():
                pe.wait_ge(p_in, 16)
                for k in range(2):
                    o = begin("pT", k)
                    for t in range(TT):
                        last = nc.tensor.transpose(o[:, t * P:(t + 1) * P], p_rows[:, t, k * P:(k + 1) * P], ident)
                    last.then_inc(bank_ready, 1)

            def gates(t):
                for n in range(2):
                    o = begin("gate", t, n)
                    for k in range(KT):
                        last = mm(o[:, :], hT[:, k, t * P:(t + 1) * P], w_ple[:, k, n * CW:(n + 1) * CW], k, KT)
                    last.then_inc(bank_ready, 1)

            def products(t):
                for n in range(2):
                    o = begin("pp", t, n)
                    for k in range(2):
                        last = mm(o[:, :], pT[:, k, t * P:(t + 1) * P], w_proj[:, k, n * CW:(n + 1) * CW], k, 2)
                    last.then_inc(bank_ready, 1)

            def first_gates():
                pe.wait_ge(w_q_in, 64)
                empty(pe, "nt", "gp", 0, 0)
                empty(pe, "nt", "gp", 0, 1)
                gates(0)

            def second_gates():
                pe.wait_ge(s_copied, 2 * TT * PH)
                empty(pe, "nt", "gp", 1, 0)
                empty(pe, "nt", "gp", 1, 1)
                gates(1)
                p_cols()

            beside = {1 + t: (lambda t=t: tile_rows("gp", t)) for t in range(TT - 1)}
            beside.update({4: first_gates, 5: second_gates})
            peer(1, at(ring, (chunk_number("keys_2") % RING) * KT * CW, 2 * PH, P), "wo2", w, "gf", beside)

            empty(pe, "nt", "gp", TT - 2, 0)
            empty(pe, "nt", "gp", TT - 2, 1)
            gates(2)
            pe.wait_ge(w_proj_in, 16)
            empty(pe, "pT", 1)
            for t in range(TT - 1):
                products(t)
            tile_rows("gp", TT - 1)
            all_empty(pe, "nt", "gp", TT - 1, 1)
            gates(3)
            products(3)

        @block.scalar
        def _(act):
            def copy_out(dst, *name, scale=1.0):
                o = full(act, *name)
                n = int(np.prod(dst.shape[1:]))
                src = o[0:dst.shape[0], 0:n]
                if len(dst.shape) == 3:
                    src = src.rearrange("p (a b) -> p a b", b=dst.shape[2])
                return nc.scalar.activation(dst, src, ACT.Copy, scale=scale)

            def squares(tiles):
                for t, (rows, junk) in enumerate(tiles):
                    act.wait_ge(x_in if t < TT else ctx_in, 16)
                    nc.scalar.activation(junk, rows, ACT.Square, accum_out=stat[:, 0, t:t + 1]).then_inc(sumsq, 1)
                act.wait_ge(meansq, 1)
                nc.scalar.activation(stat[:, 2, :], stat[:, 1, :], ACT.Sqrt).then_inc(root, 1)

            def tile_square(name, t):
                nc.scalar.activation(hT[:, :, t * P:(t + 1) * P], X[:, t, :].rearrange("p (k d) -> p k d", d=P), ACT.Square,
                                     accum_out=tstat[:, 0, t:t + 1]).then_inc(t_sq, 1)

            def tile_root(name, t):
                act.wait_ge(t_mean, STATS.index((name, t)) + 1)
                nc.scalar.activation(tstat[:, 2, t:t + 1], tstat[:, 1, t:t + 1], ACT.Sqrt).then_inc(t_root, 1)

            def tile_out(name, t, gains, shifts):
                for half in range(2):
                    if jobs.who[jobs.number("nt", name, t, half)] == "A":
                        o = full(act, "nt", name, t, half)
                        for j in range(4):
                            k = 4 * half + j
                            ins = nc.scalar.activation(hT[:, k, t * P:(t + 1) * P], o[:, j * P:(j + 1) * P], ACT.Identity,
                                                       bias=shifts(k), scale=gains(k))
                        ins.then_inc(emptied["A"], 1)

            def added(name, t):
                empty(act, name, t, 1)

            empty(act, "cols")
            nc.scalar.activation(silu[:, :, :].rearrange("p k a -> p a k"),
                                 cols[:, 0:2 * KT].rearrange("p (a k) -> p a k", k=KT), ACT.Silu).then_inc(silu_done, 1)
            junk_c = at(scr, 23040, TC, D)
            squares([(X[:, t, :], xr[:, t, :]) for t in range(TT)]
                    + [(xc[:, t, :], junk_c[:, t, :]) for t in range(TC)])

            act.wait_ge(lg_in, 32)
            nc.scalar.activation(lg[:, 1, :], lg[:, 0, :], ACT.Abs).then_inc(lg_act, 1)
            act.wait_ge(lg_act, 1)
            nc.scalar.activation(lg[:, 1, :], lg[:, 1, :], ACT.Exp, scale=-1.0).then_inc(lg_act, 1)
            act.wait_ge(lg_act, 2)
            nc.scalar.activation(lg[:, 1, :], lg[:, 1, :], ACT.Ln, bias=1.0).then_inc(lg_act, 1)

            def decay_masks(h):
                if h >= 2:
                    empty(act, "rs", h - 2, TT + TC - 1)
                m, c = mask_m[h % 2], mask_c[h % 2]
                ahead, behind = const[:, C_AHEAD:C_AHEAD + 384 + L], const[:, C_BEHIND:C_BEHIND + 384 + L]
                since = const[:, C_AHEAD + 512:C_AHEAD + 512 + 640]
                nc.scalar.activation(m[:, 0, :], ahead, ACT.Exp, scale=lg[:, 3, h:h + 1]).then_inc(exps, 1)
                nc.scalar.activation(m[:, 1, :], behind, ACT.Exp, scale=lg[:, 3, 4 + h:5 + h]).then_inc(exps, 1)
                nc.scalar.activation(c[:, 0, :], since, ACT.Exp, scale=lg[:, 3, h:h + 1]).then_inc(exps, 1)
                nc.scalar.activation(c[:, 1, :], since, ACT.Exp, scale=lg[:, 1, 4 + h:5 + h], bias=lg[:, 2, 4 + h:5 + h]
                                     ).then_inc(exps, 1)

            act.wait_ge(lg_step, 4)
            act.wait_ge(const_in, 16)
            decay_masks(0)
            decay_masks(1)

            act.wait_ge(gains_done, 2)
            for k in range(0, KT, 2):
                o = full(act, "norm", 0, k)
                nc.scalar.activation(hT[:, k, :], o[:, :], ACT.Identity, bias=mod[:, k, 0:1], scale=gain[:, 0, k:k + 1]
                                     ).then_inc(emptied["A"], 1)
            for k in range(0, KT, 2):
                o = full(act, "normc", k)
                nc.scalar.activation(hTc[:, k, :], o[:, 0:LC], ACT.Identity, bias=mod[:, k, 1:2], scale=gain[:, 1, k:k + 1]
                                     ).then_inc(emptied["A"], 1)
            for h in range(HEADS):
                copy_out(rkT[:, h, :], "rk", h, scale=RET_DK ** -0.5).then_inc(emptied["A"], 1)
            for h in range(HEADS):
                copy_out(rqT[:, h, :], "rq", h).then_inc(emptied["A"], 1)
            for g in range(2):
                copy_out(rkTc[:, 2 * g:2 * g + 2, :], "rkc", g, scale=RET_DK ** -0.5).then_inc(emptied["A"], 1)
            for t in range(TT):
                copy_out(rv[:, t, :], "rv", t).then_inc(emptied["A"], 1)
            for t in range(TC):
                copy_out(rvc[:, t, :], "rvc", t).then_inc(emptied["A"], 1)
            for h in range(HEADS):
                copy_out(o_ret[:, :, h * DV:(h + 1) * DV], "ro", h).then_inc(emptied["A"], 1)
                if h + 2 < HEADS:
                    decay_masks(h + 2)

            act.wait_ge(ones_set, 1)
            for name, c0, n in (("lr", 0, L), ("lrc", L, LC)):
                o = full(act, name)
                nc.scalar.activation(lrT[0:RANK, c0:c0 + n], o[0:RANK, 0:n], ACT.Copy)
                nc.scalar.activation(lrT[32:32 + RANK, c0:c0 + n], o[32:32 + RANK, 0:n], ACT.Copy).then_inc(emptied["A"], 1)
            for p in range(PAIRS):
                copy_out(gqT[:, p, :], "gq", p, scale=GLA_DK ** -0.5).then_inc(emptied["A"], 1)
            for t in range(TT + TC):
                o = full(act, "la", t)
                nc.scalar.activation(la_tmp[:, t, :], o[:, :], ACT.Abs).then_inc(la_abs, 1)
            act.wait_ge(la_abs, TT + TC)
            nc.scalar.activation(la_tmp, la_tmp, ACT.Exp, scale=-1.0).then_inc(la_exp, 1)
            act.wait_ge(la_exp, 1)
            for part in (slice(0, TT), slice(TT, TT + TC)):
                nc.scalar.activation(la_tmp[:, part, :], la_tmp[:, part, :], ACT.Ln, bias=1.0).then_inc(la_ln, 1)
            for p in range(PAIRS):
                copy_out(gkT[:, p, :], "gk", p).then_inc(emptied["A"], 1)
            copy_out(gkTc, "gkc").then_inc(emptied["A"], 1)
            act.wait_ge(head_step, 2 * TT + 1)
            nc.scalar.activation(hstat[:, 2, 0:TT * HEADS], hstat[:, 1, 0:TT * HEADS], ACT.Sqrt).then_inc(head_root, 1)
            for t in range(0, TT, 2):
                copy_out(gv[:, t, :], "gv", t).then_inc(emptied["A"], 1)
            copy_out(gvc[:, 0, :], "gvc", 0).then_inc(emptied["A"], 1)
            for p in range(PAIRS):
                for d in (FWD, BWD):
                    i, last = 2 * p + d, P - 1 if d == FWD else 0
                    o = full(act, "cumc", p, d)
                    nc.scalar.activation(kc_exp, o[:, 0:LC], ACT.Exp).then_inc(emptied["A"], 1)
                    act.wait_ge(g_sub, 2 * (i + 1))
                    nc.scalar.activation(G_neg, G_mid, ACT.Exp, scale=-1.0).then_inc(g_exp, 1)
                    nc.scalar.activation(G_mid, G_mid, ACT.Exp).then_inc(g_exp, 1)
                    nc.scalar.activation(G_last, G_last, ACT.Exp, scale=-1.0).then_inc(g_exp, 1)
                    nc.scalar.activation(chunk_dec[:, i, :], G.rearrange("p (c t) -> p c t", t=P)[:, :, last], ACT.Exp
                                         ).then_inc(g_exp, 1)
                    act.wait_ge(g_exp, 5 * i + 4)
                    nc.scalar.activation(G, G, ACT.Exp).then_inc(g_exp, 1)
                    copy_out(ret_gate[:, i, :], "rg", i).then_inc(emptied["A"], 1)
                    copy_out(kcT, "kcT", p, d).then_inc(emptied["A"], 1)
                    copy_out(kdT[:, i, :, :], "kdT", p, d).then_inc(emptied["A"], 1)
            for h in range(HEADS):
                for d in (FWD, BWD):
                    copy_out(g_p[2 * h + d], "gs", h, d).then_inc(emptied["A"], 1)
            empty(act, "rg", TT - 1)
            nc.scalar.activation(ret_gate, ret_gate, ACT.Silu).then_inc(rg_silu, 1)
            for c in range(TT):
                for odd in range(2):
                    copy_out(o_gla[:, c, :].rearrange("p (a b v) -> p b a v", b=2, v=DV)[:, odd], "go", c, odd
                             ).then_inc(emptied["A"], 1)

            act.wait_ge(head_step, 4 * TT + 3)
            nc.scalar.activation(hstat[:, 2, TT * HEADS:], hstat[:, 1, TT * HEADS:], ACT.Sqrt).then_inc(head_root, 1)
            for t in range(TT):
                if t >= 2:
                    act.wait_ge(y_done, 1 + t - 1)
                o = full(act, "gg", t)
                nc.scalar.activation(gate_tmp[:, t % 2, :], o[:, :], ACT.Silu).then_inc(emptied["A"], 1)
            for k in range(0, KT, 2):
                copy_out(yT[:, k, :], "yT", k).then_inc(emptied["A"], 1)

            def peer(layer, gelu_func, name, norm, gains, shifts, beside):
                def rows_of(it, b):
                    nc.scalar.activation(x_cur, hT[:, :, bass.ds(b * P, P)], ACT.Copy).then_inc(x_cur_set, 1)

                def scores_out(n, h):
                    act.wait_ge(q_done, n + 1)
                    nc.scalar.activation(peer_qT[:, h % 2, :, :].rearrange("p a b -> p (a b)"), psum[4 + h % 2][:, 0:2 * P],
                                         ACT.Copy).then_inc(q_copied, 1)
                    hold(act, routed, n + 1)
                    act.wait_ge(s_done, n + 1)
                    nc.scalar.activation(score[:, h % 2, :, :].rearrange("p a b -> p (a b)"), psum[4 + h % 2][:, 2 * P:4 * P],
                                         ACT.Copy).then_inc(s_copied, 1)

                def softmax_exp(n):
                    act.wait_ge(topped, n + 1)
                    nc.scalar.activation(exp_s, top2, ACT.Exp, bias=neg_max, accum_out=exp_sum).then_inc(exp_done, 1)

                def head(n, h, more=True, beside=None):
                    if more:
                        scores_out(n + 1, (h + 1) % PH)
                        softmax_exp(n + 1)
                    activations_and_weights(n, h, beside)

                def activations_and_weights(n, h, beside=None):
                    act.wait_ge(u_used, n * TOPK + (TOPK + SLOTS))
                    nc.scalar.activation(gelu[:, h % 2, :], dots[:, h % 2, :], gelu_func).then_inc(gelu_done, 1)
                    if beside:
                        beside()
                    hold(act, weighted, n + 1)
                    for k in range(TOPK):
                        act.wait_ge(v_used, n * TOPK + (k + 1 - TOPK + V_CREDIT))
                        nc.scalar.activation(diag[:, k, :], ident, ACT.Copy, scale=weight[:, h % 2, k:k + 1]
                                             ).then_inc(diag_set, 1)

                def token_block(it, b, more, beside={}):
                    for h in range(1, PH):
                        if h == PH - 1 and more:
                            hold(act, q_done, it * PH + PH)
                            rows_of(it + 1, b + 1)
                        head(it * PH + h, h, h < PH - 1 or more, beside.get(h))
                    if more:
                        head(it * PH + PH, 0)

                added(name, 0)
                tile_square(norm, 0)
                tile_root(norm, 0)
                for g in range(4):
                    copy_out(kT[:, 4 * g:4 * g + 4, :], "kT", layer, g).then_inc(emptied["A"], 1)
                tile_out(norm, 0, gains, shifts)
                empty(act, "nt", norm, 0, 0)
                empty(act, "nt", norm, 0, 1)
                nc.scalar.activation(x_cur, hT[:, :, 0:P], ACT.Copy).then_inc(x_cur_set, 1)
                n0 = layer * TT * PH
                scores_out(n0, 0)
                scores_out(n0 + 1, 1)
                softmax_exp(n0)
                for t in (1, 2):
                    added(name, t)
                    tile_square(norm, t)
                    tile_root(norm, t)
                tile_out(norm, 1, gains, shifts)
                softmax_exp(n0 + 1)
                tile_out(norm, 2, gains, shifts)
                added(name, 3)
                tile_square(norm, 3)
                tile_root(norm, 3)
                tile_out(norm, 3, gains, shifts)
                all_empty(act, "nt", norm, 3, 1)
                activations_and_weights(n0, 0)
                with act.Fori(0, TT - 1) as b:
                    token_block(b + layer * TT, b, True)
                token_block(TT - 1 + layer * TT, TT - 1, False, beside)

            no_shift = lambda k: 0.0
            mix_gain = lambda k: col("g_mix_2", k)
            early = range(TT - 1)

            def first_squares():
                act.wait_ge(x_added, TT)
                act.wait_ge(x_cur_set, TT)
                for t in early:
                    tile_square("nf", t)
                for t in early:
                    tile_root("nf", t)

            def second_squares():
                act.wait_ge(x_new, TT - 1)
                for t in early:
                    tile_square("gm", t)
                for t in early:
                    tile_root("gm", t)

            beside = {1: first_squares, 2: second_squares}
            for t in early:
                beside[4 + t] = lambda t=t: tile_out("gm", t, mix_gain, no_shift)
            peer(0, ACT.Gelu, "wo", "n1", lambda k: gain[:, 2, k:k + 1], lambda k: mod[:, 3 * KT + k, 0:1], beside)
            act.wait_ge(x_added, 1 + TT)
            tile_square("nf", TT - 1)
            tile_root("nf", TT - 1)
            act.wait_ge(x_new, TT)
            tile_square("gm", TT - 1)
            tile_root("gm", TT - 1)
            tile_out("gm", TT - 1, mix_gain, no_shift)
            for j in range(4):
                if j >= 2:
                    empty(act, "cv", j - 2)
                copy_out(c_gate[:, j % 2, :], "cc", j).then_inc(emptied["A"], 1)
            act.wait_ge(pads_zeroed, 4)
            for g in range(4):
                if g >= 2:
                    act.wait_ge(pooled, g - 1)
                copy_out(u_pad[g % 2][:, PAD:PAD + L], "pu", g).then_inc(emptied["A"], 1)
            for g in range(4):
                copy_out(yT[:, 4 + g, :], "py", g, scale=col("pool_scale_2", g)).then_inc(emptied["A"], 1)

            def ple_squares():
                act.wait_ge(x_added, 2 * TT)
                act.wait_ge(x_cur_set, 2 * TT)
                for t in early:
                    tile_square("gp", t)
                for t in early:
                    tile_root("gp", t)

            ple_gain = lambda k: col("g_ple_2", k)

            def gates(t):
                for n in range(2):
                    o = full(act, "gate", t, n)
                    nc.scalar.activation(ple_gate[:, t, n, :], o[:, :], ACT.Sigmoid).then_inc(emptied["A"], 1)

            def second_gates():
                gates(1)
                for k in range(2):
                    copy_out(pT[:, k, :], "pT", k).then_inc(emptied["A"], 1)

            beside = {1: ple_squares, 6: lambda: gates(0), 7: second_gates}
            for t in early:
                beside[3 + t] = lambda t=t: tile_out("gp", t, ple_gain, no_shift)
            peer(1, ACT.Gelu_apprx_tanh, "wo2", "gf", lambda k: col("g_ffn_2", k), no_shift, beside)
            act.wait_ge(x_added, 1 + 2 * TT)
            tile_square("gp", TT - 1)
            tile_root("gp", TT - 1)
            gates(2)
            tile_out("gp", TT - 1, ple_gain, no_shift)
            for t in range(TT):
                if t == TT - 2:
                    gates(TT - 1)
                added("pp", t)
                tile_square("fin", t)
                tile_root("fin", t)

        @block.vector
        def _(dve):
            V = nc.vector
            dve.sem_inc(u_used, SLOTS)
            dve.sem_inc(routed, 2)
            dve.sem_inc(x_added, 1)

            def scale_rows(tiles):
                dve.wait_ge(sumsq, len(tiles))
                V.tensor_scalar(stat[:, 1, :], stat[:, 0, :], 1.0 / D, EPS, ALU.mult, ALU.add).then_inc(meansq, 1)
                dve.wait_ge(root, 1)
                V.reciprocal(stat[:, 3, :], stat[:, 2, :]).then_inc(rstd, 1)
                dve.wait_ge(rstd, 1)
                for t, (src, dst) in enumerate(tiles):
                    V.tensor_scalar(dst, src, stat[:, 3, t:t + 1], None, ALU.mult).then_inc(rows_scaled, 1)

            def tile_mean(name, t):
                dve.wait_ge(t_sq, STATS.index((name, t)) + 1)
                V.tensor_scalar(tstat[:, 1, t:t + 1], tstat[:, 0, t:t + 1], 1.0 / D, EPS, ALU.mult, ALU.add).then_inc(t_mean, 1)

            def tile_rstd(name, t):
                s = STATS.index((name, t))
                dve.wait_ge(t_root, s + 1)
                V.reciprocal(tstat[:, 3, t:t + 1], tstat[:, 2, t:t + 1]).then_inc(t_rstd, 1)
                dve.wait_ge(t_rstd, s + 1)
                if (name, t) in DIAGS:
                    i = DIAGS.index((name, t))
                    if i >= 3:
                        full(dve, "nt", *DIAGS[i - 3], 1)
                    V.tensor_scalar(tile_diag[:, i % 3, :], ident, tstat[:, 3, t:t + 1], None, ALU.mult).then_inc(t_diag, 1)

            def tile_stats(name, t):
                tile_mean(name, t)
                tile_rstd(name, t)

            def tile_out(name, t, gains, shifts):
                o = full(dve, "nt", name, t, 1)
                for k in range(4):
                    dst, src = hT[:, 4 + k, t * P:(t + 1) * P], o[:, k * P:(k + 1) * P]
                    if shifts is None:
                        ins = V.tensor_scalar(dst, src, gains(4 + k), None, ALU.mult)
                    else:
                        ins = V.tensor_scalar(dst, src, gains(4 + k), shifts(4 + k), ALU.mult, ALU.add)
                ins.then_inc(emptied["D"], 1)

            def tile_final(name, t, weights, done):
                tile_rstd(name, t)
                V.scalar_tensor_tensor(X[:, t, :], X[:, t, :], tstat[:, 3, t:t + 1], weights, ALU.mult, ALU.mult
                                       ).then_inc(done, 1)

            def modulation(c):
                o = full(dve, "mod", c)
                if c >= 2:
                    full(dve, "modT", c - 2)
                V.tensor_copy(mod_rows[:, c % 2, :], o[0:2, :]).then_inc(emptied["D"], 1)

            def modulation_cols(c):
                o = full(dve, "modT", c)
                V.tensor_tensor(mod[:, 4 * c:4 * c + 4, :], o[:, 0:8].rearrange("p (j v) -> p j v", v=2),
                                col("b_mod", 4 * c, 4).unsqueeze(2).to_broadcast([P, 4, 2]),
                                ALU.add).then_inc(emptied["D"], 1)

            def summed_cols(c):
                o = full(dve, "modT", c)
                V.tensor_tensor(mod[:, 4 * c:4 * c + 4, 0], o[:, 0:4], col("b_mod", 4 * c, 4), ALU.add).then_inc(emptied["D"], 1)

            def norm_gain(g, tile, v, name):
                V.scalar_tensor_tensor(gain[:, g, :], mod[:, tile:tile + KT, v], 1.0, col(name, 0, KT),
                                       ALU.add, ALU.mult).then_inc(gains_done, 1)

            o = full(dve, "cols")
            V.tensor_copy(cols[:, :], o[:, 0:N_VEC]).then_inc(emptied["D"], 1)
            empty(dve, "cols")
            modulation(0)
            modulation(1)
            modulation_cols(0)
            modulation(2)
            modulation_cols(1)
            scale_rows([(X[:, t, :], xr[:, t, :]) for t in range(TT)] + [(xc[:, t, :], xc[:, t, :]) for t in range(TC)])

            dve.wait_ge(lg_in, 32)
            V.tensor_scalar(lg[:, 2, :], lg[:, 0, :], 0.0, None, ALU.min).then_inc(lg_step, 1)
            dve.wait_ge(lg_act, 3)
            dve.wait_ge(lg_step, 1)
            V.tensor_tensor(lg[:, 3, :], lg[:, 2, :], lg[:, 1, :], ALU.subtract).then_inc(lg_step, 1)
            dve.wait_ge(lg_step, 2)
            V.tensor_scalar(lg[:, 1, :], lg[:, 3, :], -1.0, None, ALU.mult).then_inc(lg_step, 1)
            V.tensor_scalar(lg[:, 2, :], lg[:, 3, :], float(L + LC), None, ALU.mult).then_inc(lg_step, 1)

            modulation(3)
            modulation_cols(2)
            modulation_cols(3)
            empty(dve, "modT", 3)
            norm_gain(0, KT, 0, "norm1_w")
            norm_gain(1, KT, 1, "norm1_w")
            dve.wait_ge(gains_done, 2)
            for k in range(1, KT, 2):
                o = full(dve, "norm", 0, k)
                V.tensor_scalar(hT[:, k, :], o[:, :], gain[:, 0, k:k + 1], mod[:, k, 0:1], ALU.mult, ALU.add
                                ).then_inc(emptied["D"], 1)
            for k in range(1, KT, 2):
                o = full(dve, "normc", k)
                V.tensor_scalar(hTc[:, k, :], o[:, 0:LC], gain[:, 1, k:k + 1], mod[:, k, 1:2], ALU.mult, ALU.add
                                ).then_inc(emptied["D"], 1)

            def rope(name, first):
                for h in range(HEADS):
                    x = (rkT if name == "rk" else rqT)[:, h, :]
                    tmp = rot_tmp[:, h % 2, :]
                    o = full(dve, name + "rot", h)
                    V.tensor_tensor(tmp, o[:, :], sin_t, ALU.mult).then_inc(emptied["D"], 1)
                    V.tensor_tensor(x, x, cos_t, ALU.mult).then_inc(rotating, 1)
                    dve.wait_ge(rotating, first + h + 1)
                    empty(dve, name + "rot", h)
                    V.tensor_tensor(x, x, tmp, ALU.add).then_inc(roped, 1)

            def masks(h):
                m, c = mask_m[h % 2], mask_c[h % 2]
                dve.wait_ge(exps, 4 * h + 4)
                V.tensor_tensor(m[:, 0, :], m[:, 0, :], m[:, 1, :], ALU.mult).then_inc(mask_step, 1)
                V.tensor_tensor(c[:, 0, :], c[:, 0, :], c[:, 1, :], ALU.add).then_inc(mask_step, 1)
                dve.wait_ge(mask_step, 3 * h + 1)
                V.tensor_tensor(m[:, 0, 384:512], m[:, 0, 384:512], const[:, C_TWICE:C_TWICE + P], ALU.mult).then_inc(mask_step, 1)

            dve.wait_ge(const_in, 16)
            summed_cols(6)
            rope("rk", 0)
            rope("rq", HEADS)
            masks(0)
            summed_cols(7)
            summed_cols(8)
            for h in range(HEADS):
                if h >= 1:
                    full(dve, "ro", h - 1)
                dve.wait_ge(mask_step, 3 * h + 3)
                for j in range(TT + TC):
                    o = full(dve, "rs", h, j)
                    if j < TT:
                        m = mask_m[h % 2][:, 0, 384 - P * j:384 - P * j + L]
                    else:
                        m = mask_c[h % 2][:, 0, P * (TC - 1 - (j - TT)):P * (TC - 1 - (j - TT)) + L]
                    V.tensor_tensor(r_p[:, j, :], o[:, :], m, ALU.mult).then_inc(emptied["D"], 1)
                if h + 1 < HEADS:
                    masks(h + 1)

            summed_cols(9)
            empty(dve, "rs", HEADS - 1, TT + TC - 1)
            V.memset(lrT, 1.0).then_inc(ones_set, 1)

            def gate_row(name, n, row, bias_in):
                dve.wait_ge(bias_in, 16)
                o, r = full(dve, name, n), row[:, n * CW:(n + 1) * CW]
                V.tensor_tensor(r, o[:, :], r, ALU.add).then_inc(emptied["D"], 1)

            def head_squares(u):
                src, sq = ((o_ret, ret_sq) if u < TT else (o_gla, sq_tmp))
                V.tensor_tensor(sq[:, u % 2, :], src[:, u % TT, :], src[:, u % TT, :], ALU.mult).then_inc(head_step, 1)
                dve.wait_ge(head_step, 2 * u + 1 + (u >= TT) * 2)
                V.tensor_reduce(hstat[:, 0, 4 * u:4 * u + 4], sq[:, u % 2, :].rearrange("p (h v) -> p h v", v=DV),
                                AX_X, ALU.add).then_inc(head_step, 1)

            def head_means(i):
                s = slice(i * TT * HEADS, (i + 1) * TT * HEADS)
                dve.wait_ge(head_step, 2 * TT * (i + 1) + 2 * i)
                V.tensor_scalar(hstat[:, 1, s], hstat[:, 0, s], 1.0 / DV, EPS, ALU.mult, ALU.add).then_inc(head_step, 1)

            def head_roots(i):
                s = slice(i * TT * HEADS, (i + 1) * TT * HEADS)
                dve.wait_ge(head_root, i + 1)
                V.reciprocal(hstat[:, 3, s], hstat[:, 2, s]).then_inc(head_step, 1)
                dve.wait_ge(head_step, (2 * TT + 2) * (i + 1))

            def head_scale(u):
                src = (o_ret if u < TT else o_gla)[:, u % TT, :].rearrange("p (h v) -> p h v", v=DV)
                V.tensor_tensor(src, src, hstat[:, 3, 4 * u:4 * u + 4].unsqueeze(2).to_broadcast([P, HEADS, DV]), ALU.mult
                                ).then_inc(y_step, 1)

            for t in range(TT + TC):
                o = full(dve, "la", t)
                dve.wait_ge(la_abs, t + 1)
                V.tensor_scalar(la[:, t, :], o[:, :], 0.0, 1.0 / GATE_NORM, ALU.min, ALU.mult).then_inc(emptied["D"], 1)
            empty(dve, "la", TT + TC - 1)
            for i, part in enumerate((slice(0, TT), slice(TT, TT + TC))):
                dve.wait_ge(la_ln, i + 1)
                V.scalar_tensor_tensor(la[:, part, :], la_tmp[:, part, :], -1.0 / GATE_NORM, la[:, part, :], ALU.mult, ALU.add
                                       ).then_inc(la_done, 1)
            empty(dve, "ro", HEADS - 1)
            for u in range(TT):
                head_squares(u)
            head_means(0)
            for t in range(1, TT, 2):
                o = full(dve, "gv", t)
                V.tensor_copy(gv[:, t, :], o[:, :]).then_inc(emptied["D"], 1)
            head_roots(0)
            o = full(dve, "gvc", 1)
            V.tensor_copy(gvc[:, 1, :], o[:, :]).then_inc(emptied["D"], 1)
            for u in range(TT):
                head_scale(u)
            gate_row("g1", 0, row_a, row_a_in)
            for p in range(PAIRS):
                for d in (FWD, BWD):
                    i = 2 * p + d
                    mid, last = (P // 2 - 1, P - 1) if d == FWD else (P // 2, 0)
                    o = full(dve, "cum", p, d)
                    if i >= 1:
                        full(dve, "kdT", (i - 1) // 2, (i - 1) % 2)
                    V.tensor_copy(G, o[:, :]).then_inc(emptied["D"], 1)
                    empty(dve, "cum", p, d)
                    g3 = G.rearrange("p (c t) -> p c t", t=P)
                    for dst, at_t in ((G_mid, mid), (G_last, last)):
                        V.tensor_tensor(dst.rearrange("p (c t) -> p c t", t=P), g3,
                                        g3[:, :, at_t:at_t + 1].to_broadcast([P, TT, P]), ALU.subtract).then_inc(g_sub, 1)
                    empty(dve, "cumc", p, d)
                    V.tensor_tensor(kc_exp, kc_exp, gkTc[:, p, :], ALU.mult).then_inc(kc_mul, 1)
                    dve.wait_ge(g_exp, 5 * (i + 1))
                    V.tensor_tensor(G_last, G_last, gkT[:, p, :], ALU.mult).then_inc(g_mul, 1)
                    V.tensor_tensor(q_in[:, i, :], G_mid, gqT[:, p, :], ALU.mult).then_inc(g_mul, 1)
                    V.tensor_tensor(k_in[:, i, :], G_neg, gkT[:, p, :], ALU.mult).then_inc(g_mul, 1)
                    V.tensor_tensor(q_st[:, i, :], G, gqT[:, p, :], ALU.mult).then_inc(g_mul, 1)
                    c = 0 if d == FWD else TT - 1
                    o = full(dve, "s0", p, d)
                    V.tensor_copy(state[0:64, i, c, :], o[0:64, 0:DV]).then_inc(state_half, 1)
                    V.tensor_copy(state[64:128, i, c, :], o[64:128, DV:2 * DV]).then_inc(emptied["D"], 1)
                    for s in range(TT - 1):
                        to = c + 1 if d == FWD else c - 1
                        o = full(dve, "up", p, d, s)
                        dve.wait_ge(state_half, i * TT + s + 1)
                        if s == 0:
                            empty(dve, "s0", p, d)
                        else:
                            empty(dve, "up", p, d, s - 1)
                        for half, done in ((0, state_half), (1, emptied["D"])):
                            r = slice(64 * half, 64 * half + 64)
                            V.scalar_tensor_tensor(state[r, i, to, :], state[r, i, c, :], chunk_dec[r, i, c:c + 1],
                                                   o[r, half * DV:(half + 1) * DV], ALU.mult, ALU.add).then_inc(done, 1)
                        c = to

            gate_row("g1", 1, row_a, row_a_in)
            dve.wait_ge(rg_silu, 1)
            dve.wait_ge(y_step, TT)
            V.tensor_tensor(o_ret, o_ret, ret_gate, ALU.mult).then_inc(y_done, 1)
            empty(dve, "modT", 9)
            norm_gain(2, 4 * KT, 0, "norm2_w")
            for t in range(TT):
                empty(dve, "go", t, 1)
                head_squares(TT + t)
            gate_row("g2", 0, row_b, row_b_in)
            head_means(1)
            head_roots(1)
            for t in range(TT):
                head_scale(TT + t)
                dve.wait_ge(y_step, TT + t + 1)
                empty(dve, "gg", t)
                V.tensor_tensor(o_gla[:, t, :], o_gla[:, t, :], gate_tmp[:, t % 2, :], ALU.mult).then_inc(y_done, 1)
            for k in range(1, KT, 2):
                o = full(dve, "yT", k)
                V.tensor_copy(yT[:, k, :], o[:, :]).then_inc(emptied["D"], 1)
            empty(dve, "g1", 1)
            dve.wait_ge(gains_done, 3)

            def peer(layer, name, norm, gains, shifts, beside):
                def add_projection(t, halves=(0, 1)):
                    for n in halves:
                        o, x = full(dve, name, t, n), X[:, t, n * CW:(n + 1) * CW]
                        if layer == 0:
                            V.tensor_tensor(o[:, :], o[:, :], row_a[:, n * CW:(n + 1) * CW], ALU.mult).then_inc(wo_mul, 1)
                            dve.wait_ge(wo_mul, 2 * t + n + 1)
                        V.tensor_tensor(x, o[:, :], x, ALU.add).then_inc(emptied["D"], 1)

                def route(n, h):
                    step = [0]

                    def then(ins):
                        step[0] += 1
                        ins.then_inc(route_step, 1)

                    def after(k):
                        dve.wait_ge(route_step, k)

                    hold(dve, s_copied, n + 1)
                    hold(dve, v_used, n * TOPK + (V_CREDIT - (IDX_SLOTS - 1) * TOPK))
                    dve.sem_clear(route_step)
                    s = score[:, h % 2, :, :]
                    for half in range(2):
                        then(V.max(top1[:, half, 0:8], s[:, half, :]))
                    for half in range(2):
                        after(1 + half)
                        then(V.match_replace(score_rest[:, half, :], top1[:, half, 0:8], s[:, half, :], LOWEST))
                    for half in range(2):
                        then(V.max_index(key_i[:, half, 0:8], top1[:, half, 0:8], s[:, half, :]))
                    for half in range(2):
                        after(3 + half)
                        then(V.max(top1[:, half, 8:16], score_rest[:, half, :]))
                    after(8)
                    then(V.tensor_tensor(cand, top1[:, 0, :].unsqueeze(2).to_broadcast([P, TOPK, TOPK]),
                                         top1[:, 1, :].unsqueeze(1).to_broadcast([P, TOPK, TOPK]), ALU.add))
                    for half in range(2):
                        then(V.max_index(key_i[:, half, 8:16], top1[:, half, 8:16], score_rest[:, half, :]))
                    after(9)
                    flat = cand.rearrange("p a b -> p (a b)")
                    then(V.max(top2[:, 0:8], flat))
                    after(11)
                    then(V.tensor_copy(key_f.rearrange("p a b -> p (a b)"), key_i[:, :, :].rearrange("p a b -> p (a b)")))
                    after(12)
                    then(V.match_replace(cand_rest, top2[:, 0:8], flat, LOWEST))
                    then(V.max_index(pos_i[:, 0:8], top2[:, 0:8], flat))
                    after(14)
                    then(V.max(top2[:, 8:16], cand_rest))
                    then(V.tensor_scalar(neg_max, top2[:, 0:1], -1.0, None, ALU.mult))
                    after(17)
                    V.max_index(pos_i[:, 8:16], top2[:, 8:16], cand_rest).then_inc(topped, 1)
                    dve.wait_ge(topped, n + 1)
                    then(V.tensor_scalar(pos_ab[:, 0, :], pos_i[:, :], 4, None, ALU.logical_shift_right))
                    then(V.tensor_scalar(pos_ab[:, 1, :], pos_i[:, :], TOPK - 1, None, ALU.bitwise_and))
                    after(19)
                    hot = onehot.rearrange("p h k a -> p (h k) a")
                    then(V.tensor_tensor(hot, pos_ab[:, :, :].rearrange("p h k -> p (h k)").unsqueeze(2).to_broadcast([P, 2 * TOPK, TOPK]),
                                         const[:, C_IOTA:C_IOTA + TOPK].unsqueeze(1).to_broadcast([P, 2 * TOPK, TOPK]), ALU.is_equal))
                    after(20)
                    then(V.tensor_tensor(onehot, onehot, key_f.unsqueeze(2).to_broadcast([P, 2, TOPK, TOPK]), ALU.mult))
                    after(21)
                    then(V.tensor_reduce(picked.rearrange("p h k -> p (h k)"), hot, AX_X, ALU.add))
                    after(22)
                    then(V.scalar_tensor_tensor(idx_f, picked[:, 0, :], float(NKEYS), picked[:, 1, :], ALU.mult, ALU.add))
                    after(23)
                    V.tensor_copy(idx[:, h % IDX_SLOTS, :], idx_f).then_inc(routed, 1)

                def softmax(n, h):
                    hold(dve, exp_done, n + 1)
                    V.reciprocal(exp_inv, exp_sum).then_inc(route_step, 1)
                    dve.wait_ge(route_step, 24)
                    V.tensor_scalar(gate[:, h % 2, :], exp_s, exp_inv, None, ALU.mult).then_inc(route_step, 1)
                    dve.wait_ge(route_step, 25)

                def dot_products(n, h, ranks=range(TOPK)):
                    for k in ranks:
                        dve.wait_ge(u_loaded[k % SLOTS], n * (16 * TOPK // SLOTS) + 16 * (k // SLOTS + 1))
                        V.tensor_tensor_reduce(u_rows[:, k % SLOTS, :], u_rows[:, k % SLOTS, :], xn, 1.0, 0.0, ALU.mult,
                                               ALU.add, dots[:, h % 2, k:k + 1]).then_inc(u_used, 1)

                def weights(n, h):
                    dve.wait_ge(gelu_done, n + 1)
                    V.tensor_tensor(weight[:, h % 2, :], gelu[:, h % 2, :], gate[:, h % 2, :], ALU.mult).then_inc(weighted, 1)

                def add_output(it, b):
                    dve.wait_ge(v_used, it * (PH * TOPK) + (PH * TOPK + V_CREDIT))
                    if layer == 0:
                        V.tensor_tensor(peer_sum, peer_sum, row_b[:, :], ALU.mult).then_inc(sum_scaled, 1)
                        dve.wait_ge(sum_scaled, it + 1)
                    x = X[:, bass.ds(b, 1), :].rearrange("p a d -> p (a d)")
                    V.tensor_tensor(x, peer_sum, x, ALU.add).then_inc(x_added, 1)

                def head(n, h, more=True, blocks=None, beside=None):
                    if more:
                        route(n + 1, (h + 1) % PH)
                    if h == 0:
                        hold(dve, xn_ready, blocks)
                    dot_products(n, h)
                    if more:
                        softmax(n + 1, (h + 1) % PH)
                    weights(n, h)
                    if beside:
                        beside()

                def token_block(it, b, more, beside={}):
                    for h in range(1, PH):
                        head(it * PH + h, h, h < PH - 1 or more, beside=beside.get(h))
                    if more:
                        head(it * PH + PH, 0, blocks=it + 2)
                    add_output(it, b)

                n0 = layer * TT * PH
                add_projection(0)
                tile_stats(norm, 0)
                if layer == 0:
                    gate_row("g2", 1, row_b, row_b_in)
                add_projection(1, (0,))
                tile_out(norm, 0, gains, shifts)
                route(n0, 0)
                softmax(n0, 0)
                add_projection(1, (1,))
                tile_stats(norm, 1)
                dve.wait_ge(xn_ready, layer * TT + 1)
                dot_products(n0, 0, range(SLOTS // 2))
                add_projection(2)
                tile_stats(norm, 2)
                tile_out(norm, 1, gains, shifts)
                dot_products(n0, 0, range(SLOTS // 2, SLOTS))
                route(n0 + 1, 1)
                add_projection(3)
                tile_stats(norm, 3)
                dot_products(n0, 0, range(SLOTS, TOPK))
                softmax(n0 + 1, 1)
                weights(n0, 0)
                with dve.Fori(0, TT - 1) as b:
                    token_block(b + layer * TT, b, True)
                token_block(TT - 1 + layer * TT, TT - 1, False, beside)

            early = range(TT - 1)
            mix_gain = lambda k: col("g_mix_2", k)

            def early_final():
                for t in early:
                    tile_mean("nf", t)
                dve.wait_ge(row_a_in, 32)
                for t in early:
                    tile_final("nf", t, row_a[:, :], x_new)

            def early_diagonals():
                for t in early:
                    tile_mean("gm", t)
                for t in early:
                    tile_rstd("gm", t)

            beside = {1: early_final, 2: early_diagonals}
            for t in early:
                beside[4 + t] = lambda t=t: tile_out("gm", t, mix_gain, None)
            peer(0, "wo", "n1", lambda k: gain[:, 2, k:k + 1], lambda k: mod[:, 3 * KT + k, 0:1], beside)
            tile_mean("nf", TT - 1)
            tile_final("nf", TT - 1, row_a[:, :], x_new)
            tile_stats("gm", TT - 1)
            tile_out("gm", TT - 1, mix_gain, None)

            dve.wait_ge(pads_zeroed, 4)
            for j in range(4):
                z, y = z_pad[j % 2], mix[:, j, :]
                empty(dve, "cc", j)
                o = full(dve, "cv", j)
                V.tensor_tensor(z[:, 1:1 + L], o[:, :], c_gate[:, j % 2, :], ALU.mult).then_inc(emptied["D"], 1)
                empty(dve, "cv", j)
                V.tensor_scalar(y, z[:, 0:L], col("conv_w_2", j), None, ALU.mult).then_inc(conv_step, 1)
                for tap in (1, 2):
                    dve.wait_ge(conv_step, 3 * j + tap)
                    V.scalar_tensor_tensor(y, z[:, tap:tap + L], col("conv_w_2", 4 * tap + j), y, ALU.mult, ALU.add
                                           ).then_inc(conv_step, 1)
            dve.wait_ge(inv_in, 16)
            steps = 0
            for g, w in enumerate(WINDOWS):
                empty(dve, "pu", g)
                src, n, span, dst = u_pad[g % 2], L + 2 * PAD, 1, 0
                while span < w:
                    n -= span
                    V.tensor_tensor(win[dst][:, 0:n], src[:, 0:n], src[:, span:span + n], ALU.add).then_inc(pool_step, 1)
                    steps += 1
                    dve.wait_ge(pool_step, steps)
                    src, dst, span = win[dst], 1 - dst, 2 * span
                y = mix[:, 4 + g, :]
                V.tensor_tensor(y, src[:, PAD - w // 2:PAD - w // 2 + L], inv_cnt[:, g, :], ALU.mult).then_inc(pool_step, 1)
                steps += 1
                dve.wait_ge(pool_step, steps)
                V.tensor_tensor(y, y, u_pad[g % 2][:, PAD:PAD + L], ALU.subtract).then_inc(pooled, 1)
            full(dve, "cb", 3)
            dve.wait_ge(conv_step, 12)
            for j in range(4):
                o = full(dve, "cb", j)
                V.tensor_tensor(yT[:, j, :], o[:, :], mix[:, j, :], ALU.mult).then_inc(emptied["D"], 1)

            ple_gain = lambda k: col("g_ple_2", k)

            def ple_diagonals():
                for t in early:
                    tile_mean("gp", t)
                for t in early:
                    tile_rstd("gp", t)

            def add_gated(t):
                for n in range(2):
                    empty(dve, "gate", t, n)
                    o, x = full(dve, "pp", t, n), X[:, t, n * CW:(n + 1) * CW]
                    V.tensor_tensor(o[:, :], o[:, :], ple_gate[:, t, n, :], ALU.mult).then_inc(ple_mul, 1)
                    dve.wait_ge(ple_mul, 2 * t + n + 1)
                    V.tensor_tensor(x, o[:, :], x, ALU.add).then_inc(emptied["D"], 1)

            def final(t):
                tile_mean("fin", t)
                tile_final("fin", t, row_b[:, :], out_ready)

            beside = {1: ple_diagonals}
            for t in early:
                beside[3 + t] = lambda t=t: tile_out("gp", t, ple_gain, None)
            peer(1, "wo2", "gf", lambda k: col("g_ffn_2", k), None, beside)
            tile_stats("gp", TT - 1)
            for t in range(TT - 1):
                add_gated(t)
            tile_out("gp", TT - 1, ple_gain, None)
            dve.wait_ge(row_b_in, 32)
            for t in range(TT - 1):
                final(t)
            add_gated(TT - 1)
            final(TT - 1)


_INPUTS = ["x", "c", "ctx", "c_ctx", "w_mod", "b_mod", "norm1_w", "norm2_w", "w_in", "ret_decay_f", "ret_decay_b",
           "gla_gk_up_f", "gla_gk_bias_f", "gla_gk_up_b", "gla_gk_bias_b", "w_out", "peer_w_q", "peer_k1", "peer_k2",
           "peer_down", "peer_up", "norm_f_w", "p_2", "g_mix_2", "w_in_2", "conv_w_2", "pool_w_2", "pool_scale_2", "w_o_2",
           "g_ffn_2", "w_q_2", "sub_keys_2", "expert_u_2", "expert_v_2", "g_ple_2", "w_ple_gate_2", "w_ple_proj_2",
           "g_final_2"]


def kernel(**inputs):
    import concourse.bacc as bacc
    from concourse.bass_utils import run_bass_kernel_spmd

    nc = bacc.Bacc("TRN2", target_bir_lowering=False, num_devices=1)
    arrays = {f"in_{n}": np.ascontiguousarray(inputs[n]) for n in _INPUTS}
    arrays["shape_tables"], arrays["inverse_counts"] = shape_constants()
    aps = {n: nc.dram_tensor(n, v.shape, F32, kind="ExternalInput").ap() for n, v in arrays.items()}
    out = nc.dram_tensor("out", (1, L, D), F32, kind="ExternalOutput").ap()
    build(nc, {n: aps[f"in_{n}"] for n in _INPUTS}, aps["shape_tables"], aps["inverse_counts"], out)
    r = run_bass_kernel_spmd(nc, [arrays], core_ids=[0])
    return r.results[0]["out"]
```
